# Optimizing a Trainium2 kernel written in Bass

```python
import jax, jax.numpy as jnp
from jax import lax
import numpy as np
import math

D_MODEL = 1024
BATCH = 1
SEQ = 512
DEPTH = 2

HEAD_DIM = 64
GROUP_HEADS = 4
GROUP_WIDTH = GROUP_HEADS * HEAD_DIM
N_GROUPS = 4
MIX_WIDTH = N_GROUPS * GROUP_WIDTH
BLOCK = 128
NEG_INF = -1e30

FOX_H = GROUP_HEADS
FOX_BIAS_INIT = 3.0
MLA_H = GROUP_HEADS
MLA_Q_RANK = D_MODEL // 4
MLA_KV_RANK = D_MODEL // 8
MLA_NOPE = HEAD_DIM
MLA_ROPE = HEAD_DIM // 2
MLA_V = HEAD_DIM
ROPE_THETA = 10000.0
SB_H = GROUP_HEADS
SWA_H = GROUP_HEADS
SWA_KV_H = 2
WINDOW = 128
D_FF = ((8 * D_MODEL + 767) // 768) * 256
ALPHA = (2.0 * DEPTH) ** 0.25
BETA = (8.0 * DEPTH) ** -0.25

SPLIT_SIZES = (
    FOX_H * HEAD_DIM, FOX_H * HEAD_DIM, FOX_H * HEAD_DIM, FOX_H,
    MLA_Q_RANK, MLA_KV_RANK, MLA_ROPE,
    SB_H * HEAD_DIM, SB_H * HEAD_DIM, SB_H * HEAD_DIM,
    SWA_H * HEAD_DIM, SWA_KV_H * HEAD_DIM, SWA_KV_H * HEAD_DIM,
)
IN_WIDTH = sum(SPLIT_SIZES)


def _layernorm(x, g, b, eps=1e-5):
    xf = x.astype(jnp.float32)
    mu = jnp.mean(xf, axis=-1, keepdims=True)
    var = jnp.mean(jnp.square(xf - mu), axis=-1, keepdims=True)
    return ((xf - mu) * lax.rsqrt(var + eps) * g + b).astype(x.dtype)

def _rmsnorm(x, g, eps=1e-6):
    xf = x.astype(jnp.float32)
    return (xf * lax.rsqrt(jnp.mean(jnp.square(xf), axis=-1, keepdims=True) + eps) * g).astype(x.dtype)

def _group_rmsnorm(mix, g, eps=1e-6):
    B, S, _ = mix.shape
    xf = mix.astype(jnp.float32).reshape(B, S, N_GROUPS, GROUP_WIDTH)
    xf = xf * lax.rsqrt(jnp.mean(jnp.square(xf), axis=-1, keepdims=True) + eps)
    return (xf.reshape(B, S, MIX_WIDTH) * g).astype(mix.dtype)

def _heads(t, n):
    B, S, _ = t.shape
    return t.reshape(B, S, n, -1)

def _rope_tables(S):
    pos = jnp.arange(S, dtype=jnp.float32)
    inv = ROPE_THETA ** (-jnp.arange(0, MLA_ROPE, 2, dtype=jnp.float32) / MLA_ROPE)
    ang = pos[:, None] * inv[None, :]
    return jnp.cos(ang), jnp.sin(ang)

def _rope(x, cos, sin):
    x1, x2 = jnp.split(x.astype(jnp.float32), 2, axis=-1)
    c = cos[None, :, None, :]
    s = sin[None, :, None, :]
    return jnp.concatenate([x1 * c - x2 * s, x1 * s + x2 * c], axis=-1).astype(x.dtype)

def _alibi_slopes(n):
    return jnp.exp2(-8.0 * jnp.arange(1, n + 1, dtype=jnp.float32) / n)

def _causal_softmax_blocks(q, k, v, scale, cum_log_f=None):
    B, S, H, _ = q.shape
    nb = S // BLOCK
    qb = q.reshape(B, nb, BLOCK, H, -1).swapaxes(0, 1)
    kpos = jnp.arange(S)

    def one_block(args):
        i, qi = args
        s = jnp.einsum('bqhd,bkhd->bhqk', qi, k).astype(jnp.float32) * scale
        qpos = i * BLOCK + jnp.arange(BLOCK)
        if cum_log_f is not None:
            cq = lax.dynamic_slice_in_dim(cum_log_f, i * BLOCK, BLOCK, axis=2)
            s = s + cq[..., :, None] - cum_log_f[..., None, :]
        s = jnp.where(kpos[None, :] <= qpos[:, None], s, NEG_INF)
        p = jax.nn.softmax(s, axis=-1).astype(v.dtype)
        return jnp.einsum('bhqk,bkhd->bqhd', p, v)

    out = lax.map(one_block, (jnp.arange(nb), qb))
    return out.swapaxes(0, 1).reshape(B, S, H, -1)

def _stick_breaking_blocks(q, k, v):
    B, S, H, D = q.shape
    nb = S // BLOCK
    scale = D ** -0.5
    qb = q.reshape(B, nb, BLOCK, H, D).swapaxes(0, 1)
    kpos = jnp.arange(S)

    def one_block(args):
        i, qi = args
        z = jnp.einsum('bqhd,bkhd->bhqk', qi, k).astype(jnp.float32) * scale
        qpos = i * BLOCK + jnp.arange(BLOCK)
        strict = kpos[None, :] < qpos[:, None]
        log_1mb = jnp.where(strict, jax.nn.log_sigmoid(-z), 0.0)
        between = lax.cumsum(log_1mb, axis=3, reverse=True) - log_1mb
        a = jnp.where(strict, jnp.exp(jax.nn.log_sigmoid(z) + between), 0.0)
        return jnp.einsum('bhqk,bkhd->bqhd', a.astype(v.dtype), v)

    out = lax.map(one_block, (jnp.arange(nb), qb))
    return out.swapaxes(0, 1).reshape(B, S, H, D)

def _mla(cq, ckv, kr, g_q, g_kv, w_uq, w_ukv, cos, sin):
    B, S, _ = cq.shape
    q = (_rmsnorm(cq, g_q) @ w_uq).reshape(B, S, MLA_H, MLA_NOPE + MLA_ROPE)
    kv = (_rmsnorm(ckv, g_kv) @ w_ukv).reshape(B, S, MLA_H, MLA_NOPE + MLA_V)
    k_nope, v = kv[..., :MLA_NOPE], kv[..., MLA_NOPE:]
    q = jnp.concatenate([q[..., :MLA_NOPE], _rope(q[..., MLA_NOPE:], cos, sin)], axis=-1)
    k_rope = jnp.broadcast_to(_rope(kr[:, :, None, :], cos, sin), (B, S, MLA_H, MLA_ROPE))
    k = jnp.concatenate([k_nope, k_rope.astype(k_nope.dtype)], axis=-1)
    return _causal_softmax_blocks(q.astype(k.dtype), k, v, (MLA_NOPE + MLA_ROPE) ** -0.5)

def _swa_sink_alibi(q, k, v, sinks, slopes):
    B, S, Hq, D = q.shape
    Hkv = k.shape[2]
    G = Hq // Hkv
    nb = S // BLOCK
    qb = q.reshape(B, nb, BLOCK, Hkv, G, D)
    pad = jnp.zeros((B, BLOCK, Hkv, D), k.dtype)
    kp = jnp.concatenate([pad, k], axis=1).reshape(B, nb + 1, BLOCK, Hkv, D)
    vp = jnp.concatenate([pad.astype(v.dtype), v], axis=1).reshape(B, nb + 1, BLOCK, Hkv, D)
    kb = jnp.concatenate([kp[:, :-1], kp[:, 1:]], axis=2)
    vb = jnp.concatenate([vp[:, :-1], vp[:, 1:]], axis=2)
    s = jnp.einsum('bnqhgd,bnkhd->bnhgqk', qb, kb).astype(jnp.float32) * (D ** -0.5)
    dist = jnp.arange(BLOCK)[:, None] + BLOCK - jnp.arange(2 * BLOCK)[None, :]
    band = (dist >= 0) & (dist < WINDOW)
    kpos = (jnp.arange(nb)[:, None] - 1) * BLOCK + jnp.arange(2 * BLOCK)[None, :]
    valid = band[None, :, :] & (kpos >= 0)[:, None, :]
    s = s - slopes.reshape(Hkv, G)[:, :, None, None] * dist.astype(jnp.float32)
    s = jnp.where(valid[None, :, None, None], s, NEG_INF)
    sink = jnp.broadcast_to(sinks.astype(jnp.float32).reshape(Hkv, G)[None, None, :, :, None, None],
                            s.shape[:-1] + (1,))
    p = jax.nn.softmax(jnp.concatenate([s, sink], axis=-1), axis=-1)[..., :-1]
    out = jnp.einsum('bnhgqk,bnkhd->bnqhgd', p.astype(v.dtype), vb)
    return out.reshape(B, S, Hq, D)

def first_inputs(seed: int = 0) -> dict:
    key = jax.random.key(seed)
    ks = jax.random.split(key, 17)
    L = DEPTH

    def nrm(k, shape, scale):
        return jax.random.normal(k, shape, jnp.float32) * scale

    def gain(k, shape):
        return 1.0 + 0.02 * jax.random.normal(k, shape, jnp.float32)

    return {
        'x': nrm(ks[0], (BATCH, SEQ, D_MODEL), 1.0),
        'w_in': nrm(ks[1], (L, D_MODEL, IN_WIDTH), D_MODEL ** -0.5),
        'fox_b_f': FOX_BIAS_INIT + nrm(ks[2], (L, FOX_H), 0.1),
        'mla_g_q': gain(ks[3], (L, MLA_Q_RANK)),
        'mla_g_kv': gain(ks[4], (L, MLA_KV_RANK)),
        'mla_w_uq': nrm(ks[5], (L, MLA_Q_RANK, MLA_H * (MLA_NOPE + MLA_ROPE)), MLA_Q_RANK ** -0.5),
        'mla_w_ukv': nrm(ks[6], (L, MLA_KV_RANK, MLA_H * (MLA_NOPE + MLA_V)), MLA_KV_RANK ** -0.5),
        'swa_sinks': nrm(ks[7], (L, SWA_H), 0.5),
        'mix_g': gain(ks[8], (L, MIX_WIDTH)),
        'w_o': nrm(ks[9], (L, MIX_WIDTH, D_MODEL), BETA * MIX_WIDTH ** -0.5),
        'ln1_g': gain(ks[10], (L, D_MODEL)),
        'ln1_b': nrm(ks[11], (L, D_MODEL), 0.02),
        'w_gate': nrm(ks[12], (L, D_MODEL, D_FF), D_MODEL ** -0.5),
        'w_up': nrm(ks[13], (L, D_MODEL, D_FF), D_MODEL ** -0.5),
        'w_down': nrm(ks[14], (L, D_FF, D_MODEL), BETA * D_FF ** -0.5),
        'ln2_g': gain(ks[15], (L, D_MODEL)),
        'ln2_b': nrm(ks[16], (L, D_MODEL), 0.02),
    }

def first_block(x, w_in, fox_b_f, mla_g_q, mla_g_kv, mla_w_uq, mla_w_ukv, swa_sinks, mix_g, w_o,
              ln1_g, ln1_b, w_gate, w_up, w_down, ln2_g, ln2_b):
    B, S, _ = x.shape
    cos, sin = _rope_tables(S)
    slopes = _alibi_slopes(SWA_H)
    points = [int(p) for p in np.cumsum(SPLIT_SIZES)[:-1]]
    for l in range(DEPTH):
        h = x @ w_in[l]
        (fq, fk, fv, fgate, cq, ckv, kr, sq, sk, sv, wq, wk, wv) = jnp.split(h, points, axis=-1)
        log_f = jax.nn.log_sigmoid(fgate.astype(jnp.float32) + fox_b_f[l].astype(jnp.float32))
        cum = jnp.cumsum(log_f, axis=1).transpose(0, 2, 1)
        out_a = _causal_softmax_blocks(_heads(fq, FOX_H), _heads(fk, FOX_H), _heads(fv, FOX_H),
                                       HEAD_DIM ** -0.5, cum)
        out_b = _mla(cq, ckv, kr, mla_g_q[l], mla_g_kv[l], mla_w_uq[l], mla_w_ukv[l], cos, sin)
        out_c = _stick_breaking_blocks(_heads(sq, SB_H), _heads(sk, SB_H), _heads(sv, SB_H))
        out_d = _swa_sink_alibi(_heads(wq, SWA_H), _heads(wk, SWA_KV_H), _heads(wv, SWA_KV_H),
                                swa_sinks[l], slopes)
        mix = jnp.concatenate([out_a.reshape(B, S, GROUP_WIDTH), out_b.reshape(B, S, GROUP_WIDTH),
                               out_c.reshape(B, S, GROUP_WIDTH), out_d.reshape(B, S, GROUP_WIDTH)],
                              axis=-1).astype(x.dtype)
        y = _group_rmsnorm(mix, mix_g[l]) @ w_o[l]
        x = _layernorm(ALPHA * x + y, ln1_g[l], ln1_b[l])
        f = (jax.nn.silu(x @ w_gate[l]) * (x @ w_up[l])) @ w_down[l]
        x = _layernorm(ALPHA * x + f, ln2_g[l], ln2_b[l])
    return x


ATT_HEADS = 8
ATT_KV_HEADS = 2
IDX_HEADS = 8
IDX_DIM = 64
TOPK_MAX = 256
Q_BLOCK = 128
RWKV_HEADS = 4
RWKV_HEAD = 64
RWKV_DECAY_LORA = 32
RWKV_A_LORA = 32
RWKV_MV_LORA = 32
RWKV_GATE_LORA = 64
RWKV_GN_EPS = 64e-5
GDN_HEADS = 4
GDN_HEAD = 64
GDN_CONV = 4
GDN_CHUNK = 64
D_FF_2 = 2816
NORM_EPS = 1e-6

ATT_W = ATT_HEADS * HEAD_DIM
KV_W = ATT_KV_HEADS * HEAD_DIM
RWKV_W = RWKV_HEADS * RWKV_HEAD
GDN_W = GDN_HEADS * GDN_HEAD
MIX_W = ATT_W + RWKV_W + GDN_W
ATT_SPLITS = (ATT_W, KV_W, KV_W, IDX_HEADS * IDX_DIM, IDX_DIM, IDX_HEADS)
RWKV_SPLITS = (RWKV_W, RWKV_W, RWKV_W, RWKV_DECAY_LORA, RWKV_A_LORA, RWKV_GATE_LORA)
GDN_SPLITS = (GDN_W, GDN_W, GDN_W, GDN_W, GDN_HEADS, GDN_HEADS)
RWKV_IN = sum(RWKV_SPLITS)
GROUP_SPLITS = (sum(ATT_SPLITS), RWKV_IN, sum(GDN_SPLITS))
IN_W = sum(GROUP_SPLITS)


def split_cols(p, sizes):
    offs = [int(o) for o in np.cumsum(sizes)[:-1]]
    return jnp.split(p, offs, axis=-1)

def rms_norm(x, g, eps=NORM_EPS):
    xf = x.astype(jnp.float32)
    y = xf * lax.rsqrt(jnp.mean(xf * xf, axis=-1, keepdims=True) + eps)
    return (y * g.astype(jnp.float32)).astype(x.dtype)

def l2_normalize(x, eps):
    xf = x.astype(jnp.float32)
    return xf * lax.rsqrt(jnp.sum(xf * xf, axis=-1, keepdims=True) + eps)

def rope(x, pos):
    half = x.shape[-1] // 2
    inv = ROPE_THETA ** (-jnp.arange(half, dtype=jnp.float32) / half)
    ang = pos.astype(jnp.float32)[:, None] * inv[None, :]
    cos, sin = jnp.cos(ang)[:, None, :], jnp.sin(ang)[:, None, :]
    xf = x.astype(jnp.float32)
    x1, x2 = xf[..., :half], xf[..., half:]
    return jnp.concatenate([x1 * cos - x2 * sin, x2 * cos + x1 * sin], axis=-1).astype(x.dtype)

def swiglu(h, w_gate, w_up, w_down):
    return (jax.nn.silu(h @ w_gate) * (h @ w_up)) @ w_down

def dsa_attention(pa, q_norm, k_norm):
    B, L, _ = pa.shape
    q, k, v, qi, ki, wi = split_cols(pa, ATT_SPLITS)
    pos = jnp.arange(L)
    q = rope(rms_norm(q.reshape(B, L, ATT_HEADS, HEAD_DIM), q_norm), pos)
    k = rope(rms_norm(k.reshape(B, L, ATT_KV_HEADS, HEAD_DIM), k_norm), pos)
    v = v.reshape(B, L, ATT_KV_HEADS, HEAD_DIM)
    qi = rope(qi.reshape(B, L, IDX_HEADS, IDX_DIM), pos).astype(jnp.float32)
    ki = rope(ki[:, :, None, :], pos)[:, :, 0].astype(jnp.float32)
    wi = wi.astype(jnp.float32) * (IDX_HEADS ** -0.5 * IDX_DIM ** -0.5)
    n_sel = min(TOPK_MAX, L // 4)
    n_blk = L // Q_BLOCK
    rep = ATT_HEADS // ATT_KV_HEADS
    scale = HEAD_DIM ** -0.5

    def to_blocks(a):
        return a.reshape(B, n_blk, Q_BLOCK, *a.shape[2:]).swapaxes(0, 1)

    def block(args):
        qb, qib, wib, tb = args
        logits = jnp.einsum('bqhd,bsd->bqhs', qib, ki)
        score = jnp.einsum('bqhs,bqh->bqs', jax.nn.relu(logits), wib)
        score = jnp.where(pos[None, None, :] <= tb[None, :, None], score, -jnp.inf)
        _, idx = lax.top_k(score, n_sel)
        valid = idx <= tb[None, :, None]
        ks = jax.vmap(lambda kb, ib: kb[ib])(k, idx).astype(jnp.float32)
        vs = jax.vmap(lambda vb, ib: vb[ib])(v, idx)
        qg = qb.reshape(B, Q_BLOCK, ATT_KV_HEADS, rep, HEAD_DIM).astype(jnp.float32)
        s = jnp.einsum('bqgrd,bqkgd->bqgrk', qg, ks) * scale
        s = jnp.where(valid[:, :, None, None, :], s, -jnp.inf)
        p = jax.nn.softmax(s, axis=-1).astype(vs.dtype)
        o = jnp.einsum('bqgrk,bqkgd->bqgrd', p, vs)
        return o.reshape(B, Q_BLOCK, ATT_W)

    out = lax.map(block, (to_blocks(q), to_blocks(qi), to_blocks(wi), pos.reshape(n_blk, Q_BLOCK)))
    return out.swapaxes(0, 1).reshape(B, L, ATT_W).astype(pa.dtype)

def rwkv7_scan(r, w, k, v, a, b):
    B, L, H, N = r.shape

    def step(S, inp):
        rt, wt, kt, vt, at, bt = inp
        sa = jnp.einsum('bhij,bhj->bhi', S, at)
        S = S * wt[:, :, None, :] + sa[..., None] * bt[:, :, None, :] + vt[..., None] * kt[:, :, None, :]
        return S, jnp.einsum('bhij,bhj->bhi', S, rt)

    xs = tuple(jnp.moveaxis(t, 1, 0) for t in (r, w, k, v, a, b))
    _, y = lax.scan(step, jnp.zeros((B, H, N, N), jnp.float32), xs)
    return jnp.moveaxis(y, 0, 1)

def rwkv7_time_mix(pb, mu, w0, w_up, a0, a_up, g_up, k_k, k_a, r_k, gn_w, gn_b, v_first, v0, v_down, v_up):
    dt = pb.dtype
    B, L, _ = pb.shape
    hb = pb.astype(jnp.float32)
    prev = jnp.pad(hb, ((0, 0), (1, 0), (0, 0)))[:, :-1]
    hb = hb + (prev - hb) * mu
    r, k, v, wd, ad, gd = split_cols(hb, RWKV_SPLITS)
    heads = lambda t: t.reshape(B, L, RWKV_HEADS, RWKV_HEAD)
    w_log = -jax.nn.softplus(-(w0 + jnp.tanh(wd) @ w_up)) - 0.5
    decay = jnp.exp(-jnp.exp(w_log))
    a = jax.nn.sigmoid(a0 + ad @ a_up)
    g = jax.nn.sigmoid(gd) @ g_up
    kk = l2_normalize(heads(k * k_k), 1e-12)
    k = k * (1.0 + (a - 1.0) * k_a)
    if v_first is None:
        v_first = v
    else:
        v = v + (v_first - v) * jax.nn.sigmoid(v0 + (v @ v_down) @ v_up)
    rh, kh, vh = heads(r), heads(k), heads(v)
    y = rwkv7_scan(rh, heads(decay), kh, vh, -kk, kk * heads(a))
    mean = jnp.mean(y, axis=-1, keepdims=True)
    var = jnp.mean(jnp.square(y - mean), axis=-1, keepdims=True)
    y = ((y - mean) * lax.rsqrt(var + RWKV_GN_EPS)).reshape(B, L, RWKV_W) * gn_w + gn_b
    bonus = jnp.sum(rh * kh * r_k, axis=-1, keepdims=True) * vh
    y = (y + bonus.reshape(B, L, RWKV_W)) * g
    return y.astype(dt), v_first

def causal_dwconv(x, w):
    C = x.shape[-1]
    return lax.conv_general_dilated(x, w[:, None, :], window_strides=(1,), padding=[(w.shape[0] - 1, 0)],
                                    dimension_numbers=('NWC', 'WIO', 'NWC'), feature_group_count=C)

def chunk_gated_delta_rule(q, k, v, g, beta):
    B, L, H, Dk = q.shape
    Dv = v.shape[-1]
    C = GDN_CHUNK
    n = L // C
    chunks = lambda t: t.reshape(B, n, C, H, t.shape[-1]).transpose(0, 3, 1, 2, 4)
    q, k, v = chunks(q), chunks(k), chunks(v)
    beta = beta.reshape(B, n, C, H).transpose(0, 3, 1, 2)
    g = jnp.cumsum(g.reshape(B, n, C, H).transpose(0, 3, 1, 2), axis=-1)
    incl = jnp.tril(jnp.ones((C, C), bool))
    strict = jnp.tril(jnp.ones((C, C), bool), -1)
    decay = jnp.exp(jnp.where(incl, g[..., :, None] - g[..., None, :], -jnp.inf))
    kb = k * beta[..., None]
    lower = jnp.where(strict, jnp.einsum('bhncd,bhnsd->bhncs', kb, k) * decay, 0.0)
    rhs = jnp.concatenate([v * beta[..., None], kb * jnp.exp(g)[..., None]], axis=-1)
    sol = lax.linalg.triangular_solve(jnp.eye(C, dtype=jnp.float32) + lower, rhs,
                                      left_side=True, lower=True, unit_diagonal=True)
    u, wk = sol[..., :Dv], sol[..., Dv:]
    intra = jnp.where(incl, jnp.einsum('bhncd,bhnsd->bhncs', q, k) * decay, 0.0)

    def step(S, inp):
        qc, kc, uc, wc, gc, ac = inp
        v_new = uc - jnp.einsum('bhck,bhkv->bhcv', wc, S)
        o = jnp.einsum('bhck,bhkv->bhcv', qc * jnp.exp(gc)[..., None], S) + jnp.einsum('bhcs,bhsv->bhcv', ac, v_new)
        g_last = gc[..., -1]
        S = S * jnp.exp(g_last)[..., None, None] + jnp.einsum(
            'bhck,bhcv->bhkv', kc * jnp.exp(g_last[..., None] - gc)[..., None], v_new)
        return S, o

    xs = tuple(jnp.moveaxis(t, 2, 0) for t in (q, k, u, wk, g, intra))
    _, o = lax.scan(step, jnp.zeros((B, H, Dk, Dv), jnp.float32), xs)
    return o.transpose(1, 0, 3, 2, 4).reshape(B, L, H, Dv)

def gated_deltanet(pc, conv_w, a_log, dt_bias, o_norm):
    dt = pc.dtype
    B, L, _ = pc.shape
    q, k, v, z, b_in, a_in = split_cols(pc.astype(jnp.float32), GDN_SPLITS)
    qkv = jax.nn.silu(causal_dwconv(jnp.concatenate([q, k, v], axis=-1), conv_w.astype(jnp.float32)))
    q, k, v = jnp.split(qkv, 3, axis=-1)
    heads = lambda t: t.reshape(B, L, GDN_HEADS, GDN_HEAD)
    q = l2_normalize(heads(q), 1e-6) * (GDN_HEAD ** -0.5)
    k = l2_normalize(heads(k), 1e-6)
    beta = jax.nn.sigmoid(b_in)
    g = -jnp.exp(a_log.astype(jnp.float32)) * jax.nn.softplus(a_in + dt_bias)
    o = chunk_gated_delta_rule(q, k, heads(v), g, beta)
    o = rms_norm(o, o_norm) * jax.nn.silu(heads(z))
    return o.reshape(B, L, GDN_W).astype(dt)

def second_inputs(seed: int = 0) -> dict:
    key = jax.random.key(seed)
    ks = iter(jax.random.split(key, 40))
    nrm = lambda shape, s: jax.random.normal(next(ks), shape, jnp.float32) * s
    uni = lambda shape, lo, hi: jax.random.uniform(next(ks), shape, jnp.float32, lo, hi)
    D, F = D_MODEL, D_FF_2
    dt0 = jnp.exp(uni((DEPTH, GDN_HEADS), math.log(1e-3), math.log(1e-1)))
    return {
        'x': nrm((BATCH, SEQ, D), 1.0),
        'ffn_norm': 1.0 + nrm((DEPTH, 2, D), 0.02),
        'ffn_w_gate': nrm((DEPTH, 2, D, F), D ** -0.5),
        'ffn_w_up': nrm((DEPTH, 2, D, F), D ** -0.5),
        'ffn_w_down': nrm((DEPTH, 2, F, D), F ** -0.5),
        'mix_norm': 1.0 + nrm((DEPTH, D), 0.02),
        'w_in': nrm((DEPTH, D, IN_W), D ** -0.5),
        'w_out': nrm((DEPTH, MIX_W, D), MIX_W ** -0.5),
        'att_q_norm': 1.0 + nrm((DEPTH, HEAD_DIM), 0.02),
        'att_k_norm': 1.0 + nrm((DEPTH, HEAD_DIM), 0.02),
        'rwkv_mu': uni((DEPTH, RWKV_IN), 0.0, 1.0),
        'rwkv_w0': uni((DEPTH, RWKV_W), -6.5, -1.5),
        'rwkv_w_up': nrm((DEPTH, RWKV_DECAY_LORA, RWKV_W), RWKV_DECAY_LORA ** -0.5),
        'rwkv_a0': nrm((DEPTH, RWKV_W), 0.1),
        'rwkv_a_up': nrm((DEPTH, RWKV_A_LORA, RWKV_W), RWKV_A_LORA ** -0.5),
        'rwkv_g_up': nrm((DEPTH, RWKV_GATE_LORA, RWKV_W), RWKV_GATE_LORA ** -0.5),
        'rwkv_k_k': 0.85 + nrm((DEPTH, RWKV_W), 0.05),
        'rwkv_k_a': 1.0 + nrm((DEPTH, RWKV_W), 0.05),
        'rwkv_r_k': nrm((DEPTH, RWKV_HEADS, RWKV_HEAD), 0.1),
        'rwkv_gn_w': 1.0 + nrm((DEPTH, RWKV_W), 0.02),
        'rwkv_gn_b': nrm((DEPTH, RWKV_W), 0.02),
        'rwkv_v0': 1.0 + nrm((DEPTH - 1, RWKV_W), 0.05),
        'rwkv_v_down': nrm((DEPTH - 1, RWKV_W, RWKV_MV_LORA), RWKV_W ** -0.5),
        'rwkv_v_up': nrm((DEPTH - 1, RWKV_MV_LORA, RWKV_W), 0.1 * RWKV_MV_LORA ** -0.5),
        'gdn_conv': nrm((DEPTH, GDN_CONV, 3 * GDN_W), GDN_CONV ** -0.5),
        'gdn_a_log': jnp.log(uni((DEPTH, GDN_HEADS), 1.0, 16.0)),
        'gdn_dt_bias': dt0 + jnp.log(-jnp.expm1(-dt0)),
        'gdn_o_norm': 1.0 + nrm((DEPTH, GDN_HEAD), 0.02),
    }

def second_block(x, ffn_norm, ffn_w_gate, ffn_w_up, ffn_w_down, mix_norm, w_in, w_out, att_q_norm, att_k_norm,
              rwkv_mu, rwkv_w0, rwkv_w_up, rwkv_a0, rwkv_a_up, rwkv_g_up, rwkv_k_k, rwkv_k_a, rwkv_r_k,
              rwkv_gn_w, rwkv_gn_b, rwkv_v0, rwkv_v_down, rwkv_v_up, gdn_conv, gdn_a_log, gdn_dt_bias, gdn_o_norm):
    v_first = None
    for l in range(DEPTH):
        x = x + 0.5 * swiglu(rms_norm(x, ffn_norm[l, 0]), ffn_w_gate[l, 0], ffn_w_up[l, 0], ffn_w_down[l, 0])
        p = rms_norm(x, mix_norm[l]) @ w_in[l]
        pa, pb, pc = split_cols(p, GROUP_SPLITS)
        ya = dsa_attention(pa, att_q_norm[l], att_k_norm[l])
        if l == 0:
            vres = (None, None, None)
        else:
            vres = (rwkv_v0[l - 1], rwkv_v_down[l - 1], rwkv_v_up[l - 1])
        yb, v_first = rwkv7_time_mix(pb, rwkv_mu[l], rwkv_w0[l], rwkv_w_up[l], rwkv_a0[l], rwkv_a_up[l],
                                     rwkv_g_up[l], rwkv_k_k[l], rwkv_k_a[l], rwkv_r_k[l], rwkv_gn_w[l],
                                     rwkv_gn_b[l], v_first, *vres)
        yc = gated_deltanet(pc, gdn_conv[l], gdn_a_log[l], gdn_dt_bias[l], gdn_o_norm[l])
        x = x + jnp.concatenate([ya, yb, yc], axis=-1) @ w_out[l]
        x = x + 0.5 * swiglu(rms_norm(x, ffn_norm[l, 1]), ffn_w_gate[l, 1], ffn_w_up[l, 1], ffn_w_down[l, 1])
    return x


def setup_inputs(seed=0):
    out = dict(first_inputs(seed))
    for name, value in second_inputs(seed + 1).items():
        if name != "x":
            out[name + "_2"] = value
    return out


def reference(
    x, w_in, fox_b_f, mla_g_q, mla_g_kv, mla_w_uq, mla_w_ukv, swa_sinks, mix_g, w_o, ln1_g,
    ln1_b, w_gate, w_up, w_down, ln2_g, ln2_b, ffn_norm_2, ffn_w_gate_2, ffn_w_up_2,
    ffn_w_down_2, mix_norm_2, w_in_2, w_out_2, att_q_norm_2, att_k_norm_2, rwkv_mu_2, rwkv_w0_2,
    rwkv_w_up_2, rwkv_a0_2, rwkv_a_up_2, rwkv_g_up_2, rwkv_k_k_2, rwkv_k_a_2, rwkv_r_k_2,
    rwkv_gn_w_2, rwkv_gn_b_2, rwkv_v0_2, rwkv_v_down_2, rwkv_v_up_2, gdn_conv_2, gdn_a_log_2,
    gdn_dt_bias_2, gdn_o_norm_2,
):
    x = first_block(
        x, w_in, fox_b_f, mla_g_q, mla_g_kv, mla_w_uq, mla_w_ukv, swa_sinks, mix_g, w_o, ln1_g,
        ln1_b, w_gate, w_up, w_down, ln2_g, ln2_b,
    )
    return second_block(
        x, ffn_norm_2, ffn_w_gate_2, ffn_w_up_2, ffn_w_down_2, mix_norm_2, w_in_2, w_out_2,
        att_q_norm_2, att_k_norm_2, rwkv_mu_2, rwkv_w0_2, rwkv_w_up_2, rwkv_a0_2, rwkv_a_up_2,
        rwkv_g_up_2, rwkv_k_k_2, rwkv_k_a_2, rwkv_r_k_2, rwkv_gn_w_2, rwkv_gn_b_2, rwkv_v0_2,
        rwkv_v_down_2, rwkv_v_up_2, gdn_conv_2, gdn_a_log_2, gdn_dt_bias_2, gdn_o_norm_2,
    )


_drawn_inputs = setup_inputs


def setup_inputs(seed=0):
    import zlib

    import numpy as np

    out = dict(_drawn_inputs(seed))
    spreads = {}
    factors = {'mla_g_q': 5.295,
     'mla_g_kv': 3.622,
     'swa_sinks': 3.17,
     'mix_g': 2.682,
     'att_q_norm_2': 8.0,
     'att_k_norm_2': 8.0,
     'rwkv_a0_2': 3.95,
     'rwkv_gn_w_2': 6.208,
     'rwkv_gn_b_2': 6.321,
     'rwkv_v0_2': 200.0,
     'rwkv_v_down_2': 64.0,
     'rwkv_v_up_2': 64.0,
     'gdn_o_norm_2': 5.386}
    for name, (base, spread) in spreads.items():
        noise = np.random.default_rng([zlib.crc32(name.encode()), seed]).standard_normal(out[name].shape)
        drawn = base * np.exp(spread * noise) if base else spread * noise
        out[name] = __import__('jax').numpy.asarray(drawn.astype(out[name].dtype))
    for name, factor in factors.items():
        out[name] = (out[name] * factor).astype(out[name].dtype)
    return out
```

```python
from contextlib import ExitStack

import numpy as np

import concourse.bass as bass
from concourse import mybir

F32 = mybir.dt.float32
ALU = mybir.AluOpType
ACT = mybir.ActivationFunctionType
AX_X = mybir.AxisListType.X

P = 128
T = 512
NT = 4
D = 1024
DFF = 2816
NF = DFF // P
ALPHA = 4.0 ** 0.25
NEG = -1e30
SENT = -3e38
WSLOT = 2176
NW = 6

C_ID, C_U, C_ONE, C_CM = 0, 128, 256, 384
C_LT, C_PM, C_SM = 512, 640, 768
C_EXTRA = 896
C_AB = C_EXTRA
C_SWA = C_AB + 2
C_RP1 = C_SWA + 1024
N1 = C_RP1 + 128
C_RP2 = C_EXTRA
C_BI = C_RP2 + 256
C_BS = C_BI + 128
C_BR = C_BS + 128
C_IND = C_BR + 128
C_LV = C_IND + 2
N2 = C_LV + 12 * 128


def make_consts():
    i = np.arange(P)
    r, c = i[:, None], i[None, :]
    f = np.float32
    common = [(r == c).astype(f), (r <= c).astype(f), np.ones((P, P), f),
              np.where(c > r, f(NEG), f(0)), (r >= c).astype(f),
              np.where(r >= c, f(1e30), f(0)), (r < c).astype(f)]
    ab = np.zeros((P, 2), f)
    ab[[0, 64], 1] = 1
    ab[[1, 65], 0] = 1
    swa = []
    for h in range(4):
        dist = r + P - np.arange(2 * P)[None, :]
        slope = f(2.0 ** (-2.0 * (h + 1)))
        swa.append(np.where((dist >= 0) & (dist < P), -slope * dist.astype(f), f(NEG)).astype(f))

    def rope_tab(half):
        pos = np.arange(T, dtype=f)
        inv = (f(10000.0) ** (-np.arange(half, dtype=f) / f(half))).astype(f)
        ang = (pos[:, None] * inv[None, :]).astype(f)
        cs = np.stack([np.cos(ang), np.sin(ang)], 0).astype(f)
        return cs.reshape(2, NT, P, half).transpose(2, 0, 1, 3).reshape(P, -1)

    c1 = np.concatenate(common + [ab] + swa + [rope_tab(16)], 1)
    same = (r // 64) == (c // 64)
    lv = []
    for k in range(6):
        w = 1 << k
        m = ((r // (2 * w)) == (c // (2 * w))) & ((r // w) % 2 == 0) & ((c // w) % 2 == 1)
        lv.append(m.astype(f))
    for k in range(6):
        lv.append(lv[k].T.copy())
    ind = np.stack([(i < 64), (i >= 64)], 1).astype(f)
    c2 = np.concatenate(common + [rope_tab(32), (same & (r <= c)).astype(f), (same & (r < c)).astype(f),
                                  (same & (r > c)).astype(f), ind] + lv, 1)
    assert c1.shape[1] == N1 and c2.shape[1] == N2
    return np.ascontiguousarray(c1.astype(f)), np.ascontiguousarray(c2.astype(f))


def flat(x):
    if x is None:
        return []
    if isinstance(x, tuple) and len(x) == 2 and isinstance(x[1], int) and isinstance(x[0], str):
        return [x]
    out = []
    for y in x:
        out += flat(y)
    return out


class Queue:

    def __init__(self, name, chain):
        self.name, self.chain = name, chain
        self.ops, self.n, self.pend = [], 0, []

    def after(self, *toks):
        self.pend += flat(toks)

    def __call__(self, fn, *toks, inc=True):
        w = flat(toks) + self.pend
        self.pend = []
        if self.chain and self.n:
            w.append((self.name, self.n))
        if inc:
            self.n += 1
        self.ops.append((fn, w, (self.name, 1) if inc else None))
        return (self.name, self.n)

    def dma(self, sem, count, fn, *toks):
        self.ops.append((fn, flat(toks) + self.pend, (sem, 16)))
        self.pend = []
        count[sem] = count.get(sem, 0) + 16
        return (sem, count[sem])

    def mark(self):
        return (self.name, self.n)


class Slots:

    def __init__(self, bufs):
        self.bufs, self.free, self.held, self.at = bufs, [[] for _ in bufs], [False] * len(bufs), 0

    def take(self):
        i = self.at % len(self.bufs)
        self.at += 1
        assert not self.held[i], "slot held"
        self.held[i] = True
        return i, self.bufs[i], self.free[i]

    def release(self, i, *toks):
        self.held[i] = False
        self.free[i] = flat(toks)


def build_program(nc, A, out, dbg):
    ctx = ExitStack()
    with ctx:
        sems = {}

        def sem(name):
            if name not in sems:
                sems[name] = ctx.enter_context(nc.semaphore(name))
            return sems[name]

        def sb(name, n):
            return ctx.enter_context(nc.sbuf_tensor(name, [P, n], F32))

        dcount = {}
        PE, V, S, G, SP = (Queue(n, c) for n, c in
                           (("pe", False), ("dve", True), ("act", True), ("pool", True), ("sp", False)))
        ENG = (PE, V, S, G)
        x_tm = sb("x_tm", 4096)
        x_T = sb("x_T", 4096)
        mix = sb("mix", 4096)
        con = sb("con", max(N1, N2))
        cols = sb("cols", 256)
        small = sb("small", 64 * 16)
        wr = [sb(f"wr{i}", WSLOT) for i in range(NW)]
        scr = [sb(f"scr{i}", 512) for i in range(10)]
        AR = 14900
        arena = sb("arena", AR)
        psum = [ctx.enter_context(nc.psum_tensor(f"ps{i}", [P, 512], F32)) for i in range(8)]
        W = Slots(wr)
        B = Slots(psum)
        R = Slots(scr)
        sm_at = [0]

        xtm = x_tm[:, :].rearrange("p (t d) -> p t d", t=NT)
        xT = x_T[:, :].rearrange("p (k t) -> p k t", k=8)
        mx = mix[:, :].rearrange("p (t d) -> p t d", t=NT)
        ident = con[:, C_ID:C_ID + P]
        uu = con[:, C_U:C_U + P]
        ones = con[:, C_ONE:C_ONE + P]
        cmask = con[:, C_CM:C_CM + P]
        ltm = con[:, C_LT:C_LT + P]
        pmask = con[:, C_PM:C_PM + P]
        smask = con[:, C_SM:C_SM + P]

        def sml():
            sm_at[0] += 1
            o = (sm_at[0] % 64) * 16
            return small[:, o:o + 16]

        def marks():
            return [q.mark() for q in ENG if q.n]

        def barrier():
            m = marks()
            for q in ENG:
                q.after(m)
            return m

        ar_at = [0]

        def take(n, view=None, **kw):
            o = ar_at[0]
            ar_at[0] += n
            assert ar_at[0] <= AR, ar_at[0]
            v = arena[:, o:o + n]
            return v.rearrange(view, **kw) if view else v

        def wget(shape_n, *parts):
            i, buf, free = W.take()
            s = f"w{i}"
            tok = None
            for dst, src in parts:
                tok = SP.dma(s, dcount, lambda e, d=dst(buf), x=src: e.dma_start(d, x), free)
            return i, buf, tok

        def wmat(M, r0, nk, c0, n):
            src = M[r0:r0 + nk * P, c0:c0 + n].rearrange("(k p) n -> p k n", p=P)
            i, buf, tok = wget(nk * n, (lambda b: b[:, 0:nk * n].rearrange("p (k n) -> p k n", k=nk), src))
            return i, buf[:, 0:nk * n].rearrange("p (k n) -> p k n", k=nk), tok

        def mms(lst, *toks):
            t = None
            for n, (o, l, r, st, sp) in enumerate(lst):
                t = PE(lambda e, o=o, l=l, r=r, st=st, sp=sp: e.matmul(o, l, r, start=st, stop=sp,
                                                                      skip_group_check=True),
                       *(toks if n == 0 else ()), inc=(n == len(lst) - 1))
            return t

        def trs(lst, *toks):
            t = None
            for n, (o, x) in enumerate(lst):
                k = x.shape[0]
                b = x.base_partition() if callable(x.base_partition) else x.base_partition
                t = PE(lambda e, o=o, x=x, k=k: e.transpose(o, x, ident[0:k, 0:k]),
                       *(toks if n == 0 else ()), inc=(n == len(lst) - 1))
            return t

        alt = [0]

        def copy(dst, src, *toks, scale=None, eng=None):
            if eng is None:
                alt[0] += 1
                eng = "S" if alt[0] % 2 else "V"
            if eng == "S":
                if scale is None:
                    return S(lambda e: e.activation(dst, src, ACT.Copy), *toks)
                return S(lambda e: e.activation(dst, src, ACT.Copy, scale=scale), *toks)
            if scale is None:
                return V(lambda e: e.tensor_copy(dst, src), *toks)
            return V(lambda e: e.tensor_scalar(dst, src, scale, None, ALU.mult), *toks)

        def tt(dst, a, b, op, *toks):
            return V(lambda e: e.tensor_tensor(dst, a, b, op), *toks)

        def ts(dst, a, s1, s2, o1, o2, *toks):
            if s2 is None:
                return V(lambda e: e.tensor_scalar(dst, a, s1, None, o1), *toks)
            return V(lambda e: e.tensor_scalar(dst, a, s1, s2, o1, o2), *toks)

        def stt(dst, a, s, b, o1, o2, *toks):
            return V(lambda e: e.scalar_tensor_tensor(out=dst, in0=a, scalar=s, in1=b, op0=o1, op1=o2), *toks)

        def act(dst, src, f, *toks, **kw):
            return S(lambda e: e.activation(dst, src, f, **kw), *toks)

        def red(dst, src, op, *toks, **kw):
            return V(lambda e: e.tensor_reduce(dst, src, AX_X, op, **kw), *toks)

        def rec(dst, src, *toks):
            return V(lambda e: e.reciprocal(dst, src), *toks)

        def vcopy(dst, src, *toks):
            return V(lambda e: e.tensor_copy(dst, src), *toks)

        def memset(dst, v, *toks):
            return V(lambda e: e.memset(dst, v), *toks)

        def rstd(dst, ssq, scale, eps, *toks):
            t = ts(dst, ssq, scale, eps, ALU.mult, ALU.add, *toks)
            t = act(dst, dst, ACT.Sqrt, t)
            return rec(dst, dst, t)

        def bc(ap, shape):
            return ap.broadcast_to(shape)

        def dma_small(batch, dst, src, *toks):
            return S.dma(batch, dcount, lambda e: e.dma_start(dst, src, allow_slow_non_contiguous=True), *toks)

        colat = {}
        coln = [0]
        tcol = None

        def load_cols(name, src, k):
            nonlocal tcol
            o = coln[0]
            coln[0] += k
            assert coln[0] <= 256
            colat[name] = cols[:, o:o + k]
            tcol = dma_small("cols", cols[:, o:o + k], src.rearrange("(k p) -> p k", p=P))

        tcon = S.dma("con", dcount, lambda e: e.dma_start(con[:, 0:N1], A["c_one"]))
        tx = None
        for i in range(NT):
            tx = SP.dma("xin", dcount, lambda e, i=i: e.dma_start(xtm[:, i, :], A["x"][0, i * P:(i + 1) * P, :]))
        for l in range(2):
            load_cols(("gq", l), A["mla_g_q"][l], 2)
            load_cols(("gkv", l), A["mla_g_kv"][l], 1)
            load_cols(("mixg", l), A["mix_g"][l], 8)
            load_cols(("mixn", l), A["mix_norm_2"][l], 8)
            for j in range(2):
                load_cols(("ffn", l, j), A["ffn_norm_2"][l, j], 8)
            load_cols(("mu", l), A["rwkv_mu_2"][l], 7)
            for w in range(4):
                load_cols(("conv", l, w), A["gdn_conv_2"][l, w], 6)

        pbuf = sb("pbuf", 2432)
        pb_at = [0]

        def load_row(batch, src, n, *toks):
            o = pb_at[0]
            pb_at[0] += n
            dst = pbuf[:, o:o + n]
            t = dma_small(batch, dst, src.unsqueeze(0).broadcast_to([P, n]), *toks)
            return dst, t

        def to_T(src, dst, scale_col, *toks):
            last = []
            for k in range(8):
                i, b, fr = B.take()
                t = trs([(b[:, j * P:(j + 1) * P], src[:, j, k * P:(k + 1) * P]) for j in range(NT)], fr, *toks)
                sc = None if scale_col is None else scale_col[:, k:k + 1]
                t = copy(dst[:, k, :], b[:, :], t, scale=sc)
                B.release(i, t)
                last.append(t)
            return last

        def proj_F(w, tw, c0, m, rd, K=8, src=None):
            src = xT if src is None else src
            i, b, fr = B.take()
            t = mms([(b[0:m, :], w[:, k, c0:c0 + m], src[:, k, :], k == 0, k == K - 1) for k in range(K)],
                    fr, tw, rd)
            return i, b, t

        def proj_T(w, tw, c0, n, tile, rd, K=8, src=None):
            src = xT if src is None else src
            i, b, fr = B.take()
            t = mms([(b[:, 0:n], src[:, k, tile * P:(tile + 1) * P], w[:, k, c0:c0 + n], k == 0, k == K - 1)
                     for k in range(K)], fr, tw, rd)
            return i, b, t

        def rms_norm_T(gcol, *toks):
            ss = sml()
            for i in range(NT):
                t = act(mx[:, i, :], xtm[:, i, :], ACT.Square, *toks, accum_out=ss[:, i:i + 1])
            rr = sml()
            t = rstd(rr[:, 0:NT], ss[:, 0:NT], 1.0 / D, 1e-6, t)
            for i in range(NT):
                t = ts(mx[:, i, :], xtm[:, i, :], rr[:, i:i + 1], None, ALU.mult, None, t)
            return to_T(mx, xT, gcol, t, tcol)

        def layer_norm(gsrc, bsrc, *toks):
            wi, wb, tw = wget(2048, (lambda b: b[:, 0:1024], gsrc.unsqueeze(0).broadcast_to([P, D])),
                              (lambda b: b[:, 1024:2048], bsrc.unsqueeze(0).broadcast_to([P, D])))
            st, mv = [], sml()
            for i in range(NT):
                s = sml()
                for j in range(2):
                    V(lambda e, s=s, i=i, j=j: e.bn_stats(s[:, 6 * j:6 * j + 6], xtm[:, i, j * 512:(j + 1) * 512]),
                      *toks)
                t = V(lambda e, s=s, i=i: e.bn_aggr(mv[:, 2 * i:2 * i + 2], s[:, 0:12]))
            rr = sml()
            t = rstd(rr[:, 0:NT], mv[:, 1:2 * NT:2], 1.0, 1e-5, t)
            for i in range(NT):
                t = ts(xtm[:, i, :], xtm[:, i, :], mv[:, 2 * i:2 * i + 1], rr[:, i:i + 1], ALU.subtract, ALU.mult, t)
                t = tt(xtm[:, i, :], xtm[:, i, :], wb[:, 0:1024], ALU.mult, tw)
                t = tt(xtm[:, i, :], xtm[:, i, :], wb[:, 1024:2048], ALU.add)
            W.release(wi, t)
            return t

        def ffn(Wg, Wu, Wd, rd, finish):
            ar_at[0] = 0
            hT = take(NF * T, "p (f t) -> p f t", f=NF)
            th = None
            for c in range(NF // 2):
                gi, wg, tg = wmat(Wg, 0, 8, c * 256, 256)
                ui, wu, tu = wmat(Wu, 0, 8, c * 256, 256)
                for s in range(2):
                    f = 2 * c + s
                    bi, bg, t1 = proj_F(wg, tg, s * P, P, rd)
                    bj, bu, t2 = proj_F(wu, tu, s * P, P, rd)
                    ri, sg, rf = R.take()
                    t = act(sg[:, :], bg[:, :], ACT.Sigmoid, t1, rf)
                    t = tt(sg[:, :], sg[:, :], bg[:, :], ALU.mult, t)
                    B.release(bi, t)
                    th = tt(hT[:, f, :], sg[:, :], bu[:, :], ALU.mult, t2)
                    R.release(ri, th)
                    B.release(bj, th)
                W.release(gi, t1)
                W.release(ui, t2)
            last = []
            for half in range(2):
                bks = [B.take() for _ in range(NT)]
                for f0 in range(0, NF, 4):
                    nf = min(4, NF - f0)
                    di, wd, td = wmat(Wd, f0 * P, nf, half * 512, 512)
                    t = mms([(bks[i][1][:, :], hT[:, f0 + f, i * P:(i + 1) * P], wd[:, f, :],
                              f0 + f == 0, f0 + f == NF - 1) for f in range(nf) for i in range(NT)],
                            td, th, [b[2] for b in bks] if f0 == 0 else None)
                    W.release(di, t)
                for i in range(NT):
                    tf = finish(i, half, bks[i][1], t)
                    B.release(bks[i][0], tf)
                    last.append(tf)
            return last

        def run(gens, depth):
            live = []
            gens = list(gens)
            while gens or live:
                if gens:
                    live.append(gens.pop(0))
                for g in list(live):
                    try:
                        next(g)
                    except StopIteration:
                        live.remove(g)

        def softmax_unit(tile, nk, qk, vs, dst, *toks, mask=None, sink=None):
            bi, b, fr = B.take()
            t = mms([(b[:, c0:c1], l, r, n == 0, n == len(qk) - 1) for n, (c0, c1, l, r) in enumerate(qk)], fr, *toks)
            yield
            m = sml()
            pi, pbf, pf = R.take()
            if mask is not None:
                t = tt(pbf[:, 0:nk], b[:, 0:nk], mask, ALU.add, t, pf)
                B.release(bi, t)
                t = red(m[:, 0:1], pbf[:, 0:nk], ALU.max, t, negate=True)
                src = pbf
            else:
                src = b
                if sink is not None:
                    t = red(m[:, 2:3], b[:, 0:nk], ALU.max, t)
                    t = ts(m[:, 0:1], m[:, 2:3], sink, -1.0, ALU.max, ALU.mult, t)
                else:
                    t = red(m[:, 0:1], b[:, 0:nk], ALU.max, t, negate=True)
            te = act(pbf[:, 0:nk], src[:, 0:nk], ACT.Exp, t, pf, bias=m[:, 0:1], accum_out=m[:, 1:2])
            if mask is None:
                B.release(bi, te)
            if sink is not None:
                t = act(m[:, 3:4], sink, ACT.Exp, te, bias=m[:, 0:1])
                t = tt(m[:, 1:2], m[:, 1:2], m[:, 3:4], ALU.add, t)
            else:
                t = te
            tr = rec(m[:, 4:5], m[:, 1:2], t)
            yield
            nb = nk // P
            ti, tb, tf = B.take()
            t = trs([(tb[:, j * P:(j + 1) * P], pbf[:, j * P:(j + 1) * P]) for j in range(nb)], tf, te)
            R.release(pi, t)
            qi, qb, qf = R.take()
            t = copy(qb[:, 0:nk], tb[:, 0:nk], t, qf)
            B.release(ti, t)
            yield
            oi, ob, of = B.take()
            t = mms([(ob[:, 0:64], qb[:, j * P:(j + 1) * P], vs[j], j == 0, j == nb - 1) for j in range(nb)], of, t)
            R.release(qi, t)
            t = ts(dst, ob[:, 0:64], m[:, 4:5], None, ALU.mult, None, t, tr)
            B.release(oi, t)

        def hb(h):
            return slice((h % 2) * 64, (h % 2) * 64 + 64)

        def debug(name, ap, *toks):
            if name in dbg:
                d = dbg[name]
                S.dma("dbg", dcount, lambda e: e.dma_start(d, ap), marks())
                for q in ENG:
                    q.after(("dbg", dcount["dbg"]))

        tx_in = [tx]
        t = to_T(xtm, xT, None, tx, tcon)
        for l in range(2):
            barrier()
            ar_at[0] = 0
            pb_at[0] = 0
            win = A["w_in"][l]
            bn = f"pb1{l}"
            fb, tp = load_row(bn, A["fox_b_f"][l], 4, marks())
            snk, tp = load_row(bn, A["swa_sinks"][l], 4)
            fq = take(2 * T, "p (k t) -> p k t", k=2)
            fk = take(2 * T, "p (k t) -> p k t", k=2)
            fv = take(4 * 260, "p (t n) -> p t n", t=4)

            def load_F(c0, n, dst, scale=None):
                wi, w, tw = wmat(win, 0, 8, c0, n)
                for s in range(n // P):
                    i, b, t = proj_F(w, tw, s * P, P, None)
                    t2 = copy(dst[:, s, :], b[:, :], t, scale=scale)
                    B.release(i, t2)
                W.release(wi, t)

            def load_T(c0, n, dst, off=0, o2=0):
                wi, w, tw = wmat(win, 0, 8, c0, n)
                for j in range(NT):
                    i, b, t = proj_T(w, tw, 0, n, j, None)
                    t2 = copy(dst[:, j, o2:o2 + n], b[:, 0:n], t)
                    B.release(i, t2)
                W.release(wi, t)

            load_F(0, 256, fq, 0.125)
            load_F(256, 256, fk)
            load_T(512, 260, fv)
            g1 = sml()
            g2 = sml()
            g3 = sml()

            def v44(x):
                return x.rearrange("p (t h) -> p t h", t=4)

            t = tt(v44(g1), fv[:, :, 256:260], bc(fb.unsqueeze(1), [P, 4, 4]), ALU.add, marks(), tp)
            t = ts(g2, g1, -1.0, None, ALU.mult, None)
            t = tt(g2, g2, g1, ALU.max)
            t = act(g2, g2, ACT.Exp, t, scale=-1.0)
            t = act(g2, g2, ACT.Ln, t, bias=1.0)
            t = ts(g1, g1, 0.0, None, ALU.min, None, t)
            t = tt(g3, g1, g2, ALU.subtract)
            LQ = take(4 * 2 * 128, "p (t a c) -> p t a c", t=4, a=2)
            LK = take(4 * 2 * 128, "p (t a c) -> p t a c", t=4, a=2)
            AQ = take(2 * T, "p (a t) -> p a t", a=2)
            AK = take(2 * T, "p (a t) -> p a t", a=2)
            memset(LQ, 0.0)
            memset(LK, 0.0)
            for a in range(2):
                for q in range(2):
                    src = v44(g3)[:, :, 2 * a + q:2 * a + q + 1]
                    vcopy(LQ[:, :, a, 64 * q:64 * q + 1], src)
                    t = ts(LK[:, :, a, 64 * q + 1:64 * q + 2], src, -1.0, None, ALU.mult, None)
            for L_, O_, cc in ((LQ, AQ, 0), (LK, AK, 1)):
                for a in range(2):
                    i, b, fr = B.take()
                    t2 = mms([(b[:, tb * P:(tb + 1) * P], L_[:, jt, a, :], uu if jt == tb else ones,
                               jt == 0, jt == tb) for tb in range(4) for jt in range(tb + 1)], fr, t)
                    t3 = act(O_[:, a, :], b[:, :], ACT.Identity, t2, bias=con[:, C_AB + cc:C_AB + cc + 1])
                    B.release(i, t3)
            t = marks()

            def fox_unit(h, i):
                a, nk = h // 2, (i + 1) * P
                qk = [(0, nk, fq[hb(h), a, i * P:nk], fk[hb(h), a, 0:nk]),
                      (0, nk, AQ[hb(h), a, i * P:nk], AK[hb(h), a, 0:nk]),
                      (i * P, nk, ident, cmask)]
                return softmax_unit(i, nk, qk, [fv[:, j, h * 64:h * 64 + 64] for j in range(i + 1)],
                                    mx[:, i, h * 64:h * 64 + 64], t)
            run([fox_unit(h, i) for h in range(4) for i in range(4)], 4)

            barrier()
            ar_at[0] = 0
            cqg = take(2 * T, "p (k t) -> p k t", k=2)
            ckg = take(T, "p (k t) -> p k t", k=1)
            sq2 = take(3 * T, "p (k t) -> p k t", k=3)
            kr = take(4 * 32, "p (t n) -> p t n", t=4)
            qtm = take(4 * 384, "p (t n) -> p t n", t=4)
            ktm = take(4 * 384, "p (t n) -> p t n", t=4)
            vtm = take(4 * 256, "p (t n) -> p t n", t=4)
            qTh = take(4 * T, "p (h t) -> p h t", h=4)
            kTh = take(4 * T, "p (h t) -> p h t", h=4)
            rt = take(4 * 256, "p (a n) -> p a n", a=4)
            gq, gkv = colat[("gq", l)], colat[("gkv", l)]
            wi, w, tw = wmat(win, 0, 8, 772, 256)
            for s in range(2):
                i, b, t = proj_F(w, tw, s * P, P, None)
                t2 = act(sq2[:, s, :], b[:, :], ACT.Square, t)
                t3 = ts(cqg[:, s, :], b[:, :], gq[:, s:s + 1], None, ALU.mult, None, t2, tcol)
                B.release(i, t3)
            W.release(wi, t)
            wi, w, tw = wmat(win, 0, 8, 1028, 160)
            i, b, t = proj_F(w, tw, 0, P, None)
            t2 = act(sq2[:, 2, :], b[:, :], ACT.Square, t)
            t3 = ts(ckg[:, 0, :], b[:, :], gkv[:, 0:1], None, ALU.mult, None, t2)
            B.release(i, t3)
            for j in range(NT):
                i, b, t = proj_T(w, tw, 128, 32, j, None)
                t4 = copy(kr[:, j, :], b[:, 0:32], t)
                B.release(i, t4)
            W.release(wi, t)
            i, b, fr = B.take()
            t = mms([(b[:, 8 * k + j:8 * k + j + 1], sq2[:, s, j * P:(j + 1) * P], ones[:, 0:1], s in (0, 2), s in (1, 2))
                     for j in range(NT) for k, s in ((0, 0), (0, 1), (1, 2))], fr, marks())
            rq, rk = sml(), sml()
            t = ts(rq[:, 0:4], b[:, 0:4], 1.0 / 256, 1e-6, ALU.mult, ALU.add, t)
            t = ts(rk[:, 0:4], b[:, 8:12], 1.0 / 128, 1e-6, ALU.mult, ALU.add)
            B.release(i, t)
            act(rq[:, 0:4], rq[:, 0:4], ACT.Sqrt, t)
            t = act(rk[:, 0:4], rk[:, 0:4], ACT.Sqrt)
            rec(rq[:, 0:4], rq[:, 0:4], t)
            rec(rk[:, 0:4], rk[:, 0:4])
            t = ts(rq[:, 0:4], rq[:, 0:4], 96.0 ** -0.5, None, ALU.mult, None)
            wi, wb, tw = wget(0, (lambda b: b[:, 0:768].rearrange("p (k n) -> p k n", k=2),
                                  A["mla_w_uq"][l].rearrange("(k p) n -> p k n", p=P)),
                              (lambda b: b[:, 768:1280], A["mla_w_ukv"][l]))
            wuq = wb[:, 0:768].rearrange("p (k n) -> p k n", k=2)
            wukv = wb[:, 768:1280].rearrange("p (k n) -> p k n", k=1)
            for j in range(NT):
                i, b, t1 = proj_T(wuq, tw, 0, 384, j, t, K=2, src=cqg)
                t2 = ts(qtm[:, j, :], b[:, 0:384], rq[:, j:j + 1], None, ALU.mult, None, t1)
                B.release(i, t2)
                i, b, t1 = proj_T(wukv, tw, 0, 512, j, t, K=1, src=ckg)
                bv = b[:, :].rearrange("p (h a d) -> p h a d", h=4, a=2)
                kv_ = ktm[:, j, :].rearrange("p (h d) -> p h d", h=4)
                t2 = ts(kv_[:, :, 0:64], bv[:, :, 0, :], rk[:, j:j + 1], None, ALU.mult, None, t1)
                t2 = ts(vtm[:, j, :].rearrange("p (h d) -> p h d", h=4), bv[:, :, 1, :], rk[:, j:j + 1],
                        None, ALU.mult, None)
                B.release(i, t2)
            W.release(wi, t1)
            cosb = con[:, C_RP1:C_RP1 + 64].rearrange("p (t n) -> p t n", t=4)
            sinb = con[:, C_RP1 + 64:C_RP1 + 128].rearrange("p (t n) -> p t n", t=4)

            def rope(x1, x2, cs, sn, tmp, shape):
                a, b_, c_, d_ = tmp
                tt(a, x1, cs, ALU.mult, marks())
                tt(b_, x2, sn, ALU.mult)
                tt(c_, x1, sn, ALU.mult)
                tt(d_, x2, cs, ALU.mult)
                tt(x1, a, b_, ALU.subtract)
                return tt(x2, c_, d_, ALU.add)

            for j in range(NT):
                q4 = qtm[:, j, :].rearrange("p (h d) -> p h d", h=4)
                tm = [rt[:, a, 0:64].rearrange("p (h d) -> p h d", h=4) for a in range(4)]
                rope(q4[:, :, 64:80], q4[:, :, 80:96], bc(cosb[:, j, :].unsqueeze(1), [P, 4, 16]),
                     bc(sinb[:, j, :].unsqueeze(1), [P, 4, 16]), tm, None)
            tm = [rt[:, a, 0:64].rearrange("p (h d) -> p h d", h=4) for a in range(4)]
            rope(kr[:, :, 0:16], kr[:, :, 16:32], cosb, sinb, tm, None)
            for j in range(NT):
                t = vcopy(ktm[:, j, :].rearrange("p (h d) -> p h d", h=4)[:, :, 64:96],
                          bc(kr[:, j, :].unsqueeze(1), [P, 4, 32]))
            for h in range(4):
                for src, dst in ((qtm, qTh), (ktm, kTh)):
                    i, b, fr = B.take()
                    t1 = trs([(b[0:96, j * P:(j + 1) * P], src[:, j, h * 96:h * 96 + 96]) for j in range(NT)], fr, t)
                    t2 = copy(dst[0:96, h, :], b[0:96, :], t1)
                    B.release(i, t2)
            t = marks()

            def mla_unit(h, i):
                nk = (i + 1) * P
                qk = [(0, nk, qTh[0:96, h, i * P:nk], kTh[0:96, h, 0:nk]), (i * P, nk, ident, cmask)]
                return softmax_unit(i, nk, qk, [vtm[:, j, h * 64:h * 64 + 64] for j in range(i + 1)],
                                    mx[:, i, 256 + h * 64:256 + h * 64 + 64], t)
            run([mla_unit(h, i) for h in range(4) for i in range(4)], 4)

            barrier()
            ar_at[0] = 0
            sq = take(2 * T, "p (k t) -> p k t", k=2)
            sk = take(2 * T, "p (k t) -> p k t", k=2)
            sv = take(4 * 256, "p (t n) -> p t n", t=4)
            zbuf = [take(1280) for _ in range(3)]
            spbuf = [take(1280) for _ in range(3)]
            ZS, SS = Slots(zbuf), Slots(spbuf)
            load_F(1188, 256, sq, 0.125)
            load_F(1444, 256, sk)
            load_T(1700, 256, sv)
            t = marks()

            def blk(s, c):
                if s == c:
                    return s * P
                return {0: 512, 2: 896, 1: 1024}[s] + (c - s - 1) * P

            def stick_unit(h):
                a = h // 2
                zi, z, zf = ZS.take()
                si, sp, sf = SS.take()
                tz = []
                parts = [(0, [(s, s, s + 1) for s in range(4)]), (512, [(0, 1, 4), (2, 3, 4)]), (1024, [(1, 2, 4)])]
                for base, ents in parts:
                    bi, b, fr = B.take()
                    wdt = sum((c1 - c0) * P for _, c0, c1 in ents)
                    t1 = mms([(b[:, blk(s, c0) - base:blk(s, c0) - base + (c1 - c0) * P], sk[hb(h), a, s * P:(s + 1) * P],
                               sq[hb(h), a, c0 * P:c1 * P], True, True) for s, c0, c1 in ents], fr, t)
                    t2 = copy(z[:, base:base + wdt], b[:, 0:wdt], t1, zf)
                    B.release(bi, t2)
                    tz.append(t2)
                yield
                t1 = act(sp[:, :], z[:, :], ACT.Abs, tz, sf)
                t1 = act(sp[:, :], sp[:, :], ACT.Exp, scale=-1.0)
                t1 = act(sp[:, :], sp[:, :], ACT.Ln, bias=1.0)
                t1 = stt(sp[:, :], z[:, :], 0.0, sp[:, :], ALU.max, ALU.add, t1)
                sd = sp[:, 0:512].rearrange("p (s c) -> p s c", s=4)
                tsp = tt(sd, sd, bc(smask.unsqueeze(1), [P, 4, P]), ALU.mult)
                yield
                te = []
                for base, ents in parts:
                    bi, b, fr = B.take()
                    lst = []
                    for s, c0, c1 in ents:
                        for c in range(c0, c1):
                            o = b[:, blk(s, c) - base:blk(s, c) - base + P]
                            if s == c:
                                lst.append((o, ident, pmask, True, False))
                            for j in range(s, c + 1):
                                lst.append((o, ltm if j == s else ones, sp[:, blk(j, c):blk(j, c) + P],
                                            s != c and j == s, j == c))
                    wdt = sum((c1 - c0) * P for _, c0, c1 in ents)
                    t1 = mms(lst, fr, tsp)
                    t2 = tt(z[:, base:base + wdt], z[:, base:base + wdt], b[:, 0:wdt], ALU.subtract, t1)
                    B.release(bi, t2)
                SS.release(si, t1)
                te = act(z[:, :], z[:, :], ACT.Exp, t2)
                yield
                bi, b, fr = B.take()
                t1 = mms([(b[:, c * 64:c * 64 + 64], z[:, blk(s, c):blk(s, c) + P], sv[:, s, h * 64:h * 64 + 64],
                           s == 0, s == c) for c in range(4) for s in range(c + 1)], fr, te)
                ZS.release(zi, t1)
                t2 = copy(mx[:, :, 512 + h * 64:512 + h * 64 + 64], b[:, 0:256].rearrange("p (c d) -> p c d", c=4), t1)
                B.release(bi, t2)
            run([stick_unit(h) for h in range(4)], 4)

            barrier()
            ar_at[0] = 0
            wq = take(2 * T, "p (k t) -> p k t", k=2)
            wk = take(2 * T, "p (k t) -> p k t", k=2)
            wv = take(4 * 128, "p (t n) -> p t n", t=4)
            load_F(1956, 256, wq, 0.125)
            wi, w, tw = wmat(win, 0, 8, 2212, 256)
            i, b, t = proj_F(w, tw, 0, P, None)
            for g in range(2):
                for q in range(2):
                    t2 = copy(wk[64 * q:64 * q + 64, g, :], b[64 * g:64 * g + 64, :], t, eng="S")
            B.release(i, t2)
            for j in range(NT):
                i, b, t = proj_T(w, tw, 128, 128, j, None)
                t2 = copy(wv[:, j, :], b[:, 0:128], t)
                B.release(i, t2)
            W.release(wi, t)
            t = marks()

            def swa_unit(h, i):
                a, g = h // 2, h // 2
                j0 = max(i - 1, 0)
                nk = (i + 1 - j0) * P
                so = C_SWA + 256 * h
                qk = [(0, nk, wq[hb(h), a, i * P:(i + 1) * P], wk[hb(h), g, j0 * P:(i + 1) * P]),
                      (0, nk, ident, con[:, so + 256 - nk:so + 256])]
                return softmax_unit(i, nk, qk, [wv[:, j, g * 64:g * 64 + 64] for j in range(j0, i + 1)],
                                    mx[:, i, 768 + h * 64:768 + h * 64 + 64], t, tp, sink=snk[:, h:h + 1])
            run([swa_unit(h, i) for h in range(4) for i in range(4)], 4)

            barrier()
            debug(f"mix{l}", mix[:, :])
            ss = sml()
            ri, rb, rf = R.take()
            for i in range(NT):
                for g in range(4):
                    t = act(rb[:, 0:256], mx[:, i, g * 256:(g + 1) * 256], ACT.Square, rf,
                            accum_out=ss[:, 4 * i + g:4 * i + g + 1])
            R.release(ri, t)
            rr = sml()
            t = rstd(rr, ss, 1.0 / 256, 1e-6, t)
            for i in range(NT):
                m4 = mx[:, i, :].rearrange("p (g d) -> p g d", g=4)
                t = tt(m4, m4, bc(rr[:, 4 * i:4 * i + 4].unsqueeze(2), [P, 4, 256]), ALU.mult, t)
            t = to_T(mx, xT, colat[("mixg", l)], t, tcol)
            for c in range(4):
                wi, w, tw = wmat(A["w_o"][l], 0, 8, c * 256, 256)
                for j in range(NT):
                    i, b, t1 = proj_T(w, tw, 0, 256, j, t)
                    xs = xtm[:, j, c * 256:(c + 1) * 256]
                    t2 = stt(xs, xs, ALPHA, b[:, 0:256], ALU.mult, ALU.add, t1)
                    B.release(i, t2)
                W.release(wi, t1)
            t = layer_norm(A["ln1_g"][l], A["ln1_b"][l], t2)
            debug(f"x1{l}", x_tm[:, :])
            t = to_T(xtm, xT, None, t)

            def fin1(i, half, b, t):
                xs = xtm[:, i, half * 512:(half + 1) * 512]
                return stt(xs, xs, ALPHA, b[:, :], ALU.mult, ALU.add, t)
            barrier()
            t = ffn(A["w_gate"][l], A["w_up"][l], A["w_down"][l], t, fin1)
            t = layer_norm(A["ln2_g"][l], A["ln2_b"][l], t)
            debug(f"x2{l}", x_tm[:, :])
            if l == 0:
                t = to_T(xtm, xT, None, t)

        def fin2(i, half, b, t):
            xs = xtm[:, i, half * 512:(half + 1) * 512]
            return stt(xs, b[:, :], 0.5, xs, ALU.mult, ALU.add, t)

        m = barrier()
        t = S.dma("con2", dcount, lambda e: e.dma_start(con[:, 0:N2], A["c_two"]), m)
        for q in ENG:
            q.after(t)
        rope_c = con[:, C_RP2:C_RP2 + 128].rearrange("p (t n) -> p t n", t=4)
        rope_s = con[:, C_RP2 + 128:C_RP2 + 256].rearrange("p (t n) -> p t n", t=4)
        m_bi = con[:, C_BI:C_BI + P]
        m_bs = con[:, C_BS:C_BS + P]
        m_br = con[:, C_BR:C_BR + P]
        m_bibs = con[:, C_BI:C_BI + 256]
        ind = con[:, C_IND:C_IND + 2]
        vfirst = sb("vfirst", 1024)
        vf3 = vfirst[:, :].rearrange("p (t n) -> p t n", t=4)

        def h64(ap, n):
            return ap.rearrange("p (h d) -> p h d", h=n)

        for l in range(2):
            barrier()
            pb_at[0] = 0
            bn = f"pb2{l}"
            mk = marks()
            rows = {}
            for nm, src, n in ([(k, A[f"rwkv_{k}_2"][l], 256) for k in ("w0", "a0", "k_k", "k_a")] +
                               [("r_k", A["rwkv_r_k_2"][l].rearrange("h d -> (h d)"), 256),
                                ("gn_w", A["rwkv_gn_w_2"][l], 256), ("gn_b", A["rwkv_gn_b_2"][l], 256)] +
                               ([("v0", A["rwkv_v0_2"][0], 256)] if l else []) +
                               [("qn", A["att_q_norm_2"][l], 64), ("kn", A["att_k_norm_2"][l], 64),
                                ("on", A["gdn_o_norm_2"][l], 64), ("al", A["gdn_a_log_2"][l], 4),
                                ("dt", A["gdn_dt_bias_2"][l], 4)]):
                rows[nm], tp = load_row(bn, src, n, mk)
            t = rms_norm_T(colat[("ffn", l, 0)], marks())
            barrier()
            t = ffn(A["ffn_w_gate_2"][l, 0], A["ffn_w_up_2"][l, 0], A["ffn_w_down_2"][l, 0], t, fin2)
            debug(f"xa{l}", x_tm[:, :])
            t = rms_norm_T(colat[("mixn", l)], marks())
            win = A["w_in_2"][l]

            barrier()
            ar_at[0] = 0
            pa = take(4 * 1352, "p (t n) -> p t n", t=4)
            qT = take(4 * T, "p (a t) -> p a t", a=4)
            qiT = take(4 * T, "p (a t) -> p a t", a=4)
            kd = take(2 * T, "p (a t) -> p a t", a=2)
            kid = take(T)
            rt = take(4 * 320, "p (a n) -> p a n", a=4)
            msk = take(3 * 512, "p (a n) -> p a n", a=3)

            def load_F2(c0, n, dst, s0):
                wi, w, tw = wmat(win, 0, 8, c0, n)
                for s in range(n // P):
                    i, b, t = proj_F(w, tw, s * P, P, None)
                    t2 = copy(dst[:, s0 + s, :], b[:, :], t)
                    B.release(i, t2)
                W.release(wi, t)

            def load_T2(c0, n, dst, o2):
                wi, w, tw = wmat(win, 0, 8, c0, n)
                for j in range(NT):
                    i, b, t = proj_T(w, tw, 0, n, j, None)
                    t2 = copy(dst[:, j, o2:o2 + n], b[:, 0:n], t)
                    B.release(i, t2)
                W.release(wi, t)

            for c0, n in ((0, 256), (256, 256), (512, 256), (768, 256), (1024, 256), (1280, 72)):
                load_T2(c0, n, pa, c0)
            rr2 = take(4 * 16, "p (t n) -> p t n", t=4)
            t = marks()
            for j in range(NT):
                ri, rb, rf = R.take()
                rj, rc_, rf2 = R.take()
                t = act(rb[:, :], pa[:, j, 0:512], ACT.Square, t, rf)
                t = act(rc_[:, 0:128], pa[:, j, 512:640], ACT.Square, rf2)
                t = red(rr2[:, j, 0:8], h64(rb[:, :], 8), ALU.add, t)
                t = red(rr2[:, j, 8:10], h64(rc_[:, 0:128], 2), ALU.add, t)
                R.release(ri, t)
                R.release(rj, t)
            t = rstd(rr2[:, :, 0:10], rr2[:, :, 0:10], 1.0 / 64, 1e-6, t)
            ts(rr2[:, :, 0:8], rr2[:, :, 0:8], 0.125, None, ALU.mult, None, t)
            for j in range(NT):
                x10 = h64(pa[:, j, 0:640], 10)
                tt(x10, x10, bc(rr2[:, j, 0:10].unsqueeze(2), [P, 10, 64]), ALU.mult)
                tt(x10[:, 0:8, :], x10[:, 0:8, :], bc(rows["qn"].unsqueeze(1), [P, 8, 64]), ALU.mult, tp)
                tt(x10[:, 8:10, :], x10[:, 8:10, :], bc(rows["kn"].unsqueeze(1), [P, 2, 64]), ALU.mult)
                for c0, nh in ((0, 10), (768, 9)):
                    xx = h64(pa[:, j, c0:c0 + nh * 64], nh)
                    tm = [h64(rt[:, a, 0:nh * 32], nh) for a in range(4)]
                    t = rope(xx[:, :, 0:32], xx[:, :, 32:64], bc(rope_c[:, j, :].unsqueeze(1), [P, nh, 32]),
                             bc(rope_s[:, j, :].unsqueeze(1), [P, nh, 32]), tm, None)
                t = ts(pa[:, j, 1344:1352], pa[:, j, 1344:1352], 8 ** -0.5 * 64 ** -0.5, None, ALU.mult, None)
            for a in range(4):
                for dst, c0 in ((qT, 0), (qiT, 768)):
                    i, b, fr = B.take()
                    t1 = trs([(b[:, j * P:(j + 1) * P], pa[:, j, c0 + a * P:c0 + (a + 1) * P]) for j in range(NT)], fr, t)
                    t2 = copy(dst[:, a, :], b[:, :], t1)
                    B.release(i, t2)
            i, b, fr = B.take()
            t1 = trs([(b[:, j * P:(j + 1) * P], pa[:, j, 512:640]) for j in range(NT)], fr, t)
            for g in range(2):
                for q in range(2):
                    t2 = copy(kd[64 * q:64 * q + 64, g, :], b[64 * g:64 * g + 64, :], t1, eng="S")
            B.release(i, t2)
            i, b, fr = B.take()
            t1 = trs([(b[0:64, j * P:(j + 1) * P], pa[:, j, 1280:1344]) for j in range(NT)], fr, t)
            for q in range(2):
                t2 = copy(kid[64 * q:64 * q + 64, :], b[0:64, :], t1, eng="S")
            B.release(i, t2)
            t = marks()
            for i in range(1, NT):
                nk = (i + 1) * P
                acc = msk[:, i - 1, 0:nk]
                for h in range(8):
                    bi, b, fr = B.take()
                    t1 = mms([(b[:, 0:nk], qiT[hb(h), h // 2, i * P:nk], kid[hb(h), 0:nk], True, True)], fr, t)
                    ri, rb, rf = R.take()
                    t1 = act(rb[:, 0:nk], b[:, 0:nk], ACT.Relu, t1, rf)
                    B.release(bi, t1)
                    wi_ = pa[:, i, 1344 + h:1345 + h]
                    if h == 0:
                        t1 = ts(acc, rb[:, 0:nk], wi_, None, ALU.mult, None, t1)
                    else:
                        t1 = stt(acc, rb[:, 0:nk], wi_, acc, ALU.mult, ALU.add, t1)
                    R.release(ri, t1)
                tt(msk[:, i - 1, i * P:nk], msk[:, i - 1, i * P:nk], cmask, ALU.add)
                m8 = sml()

                def top8(acc, m8):
                    V(lambda e: e.max(m8[:, 0:8], acc))
                    V(lambda e: e.match_replace(acc, m8[:, 0:8], acc, SENT))
                for _ in range(16):
                    top8(acc, m8)
                ts(acc, acc, SENT, 1.0, ALU.is_equal, ALU.subtract)
                t1 = ts(acc, acc, 1e30, None, ALU.mult, None)
            t = marks()

            def dsa_unit(h, i):
                nk = (i + 1) * P
                qk = [(0, nk, qT[hb(h), h // 2, i * P:nk], kd[hb(h), h // 4, 0:nk])]
                mask = None
                if i == 0:
                    qk.append((0, P, ident, cmask))
                else:
                    mask = msk[:, i - 1, 0:nk]
                g = h // 4
                return softmax_unit(i, nk, qk, [pa[:, j, 640 + g * 64:704 + g * 64] for j in range(i + 1)],
                                    mx[:, i, h * 64:h * 64 + 64], t, mask=mask)
            run([dsa_unit(h, i) for i in range(4) for h in range(8)], 4)

            barrier()
            ar_at[0] = 0
            hbT = take(7 * T, "p (a t) -> p a t", a=7)
            gT = take(6 * T, "p (a t) -> p a t", a=6)
            gz = take(4 * 264, "p (t n) -> p t n", t=4)
            lora = take(256)
            vdn = take(64, "p (k n) -> p k n", k=2)
            vup = take(256)
            gate = take(64, "p (a t h) -> p a t h", a=4, t=4)
            vz = take(512)
            UNs = [take(512) for _ in range(2)]
            Ms = [take(256) for _ in range(4)]
            extra = [take(512) for _ in range((AR - ar_at[0]) // 512)]
            mk = marks()
            ln_ = f"lora{l}"
            dma_small(ln_, lora[0:32, :], A["rwkv_w_up_2"][l], mk)
            dma_small(ln_, lora[32:64, :], A["rwkv_a_up_2"][l])
            tl = dma_small(ln_, lora[64:128, :], A["rwkv_g_up_2"][l])
            if l:
                dma_small(ln_, vdn, A["rwkv_v_down_2"][0].rearrange("(k p) n -> p k n", p=P))
                tl = dma_small(ln_, vup[0:32, :], A["rwkv_v_up_2"][0])
            for c0, n, s0 in ((1352, 256, 0), (1608, 256, 2), (1864, 256, 4), (2120, 128, 6)):
                load_F2(c0, n, hbT, s0)
            for c0, s0 in ((2248, 0), (2504, 2), (2760, 4)):
                load_F2(c0, 256, gT, s0)
            load_T2(3016, 264, gz, 0)
            barrier()
            mu = colat[("mu", l)]
            for s in range(7):
                ri, rb, rf = R.take()
                t = tt(rb[:, 1:512], hbT[:, s, 0:511], hbT[:, s, 1:512], ALU.subtract, rf, tcol)
                t = ts(rb[:, 0:1], hbT[:, s, 0:1], -1.0, None, ALU.mult, None)
                t = stt(hbT[:, s, :], rb[:, :], mu[:, s:s + 1], hbT[:, s, :], ALU.mult, ALU.add)
                R.release(ri, t)
            t = act(hbT[0:32, 6, :], hbT[0:32, 6, :], ACT.Tanh, t)
            t = act(hbT[64:128, 6, :], hbT[64:128, 6, :], ACT.Sigmoid, t)
            cv = [colat[("conv", l, w)] for w in range(4)]
            for s in range(6):
                ri, rb, rf = R.take()
                rj, rc_, rf2 = R.take()
                t = ts(rb[:, :], gT[:, s, :], cv[3][:, s:s + 1], None, ALU.mult, None, rf, rf2)
                for w in range(1, 4):
                    t = stt(rb[:, w:512], gT[:, s, 0:512 - w], cv[3 - w][:, s:s + 1], rb[:, w:512], ALU.mult, ALU.add)
                t = act(rc_[:, :], rb[:, :], ACT.Sigmoid, t)
                t = tt(gT[:, s, :], rb[:, :], rc_[:, :], ALU.mult, t)
                R.release(ri, t)
                R.release(rj, t)
            ga, gb_, gg, gt = (gate[:, a] for a in range(4))
            t = act(gb_, gz[:, :, 256:260], ACT.Sigmoid, t)
            t = tt(ga, gz[:, :, 260:264], bc(rows["dt"].unsqueeze(1), [P, 4, 4]), ALU.add, tp)
            ts(gt, ga, -1.0, None, ALU.mult, None)
            t = tt(gt, gt, ga, ALU.max)
            t = act(gt, gt, ACT.Exp, t, scale=-1.0)
            t = act(gt, gt, ACT.Ln, t, bias=1.0)
            t = stt(gt, ga, 0.0, gt, ALU.max, ALU.add, t)
            al = sml()
            t = act(al[:, 0:4], rows["al"], ACT.Exp, t)
            t = tt(gg, gt, bc(al[:, 0:4].unsqueeze(1), [P, 4, 4]), ALU.mult, t)
            t = ts(gg, gg, -1.0, None, ALU.mult, None)
            if l:
                i, b, fr = B.take()
                t1 = mms([(b[0:32, :], vdn[:, k, :], hbT[:, 4 + k, :], k == 0, k == 1) for k in range(2)],
                         fr, tl, marks())
                t2 = copy(vz[0:32, :], b[0:32, :], t1)
                B.release(i, t2)
            barrier()
            for u_ in UNs:
                memset(u_, 0.0)
            memset(Ms[0], 0.0)

            stock = [(x, []) for x in [x_T[:, i * 512:(i + 1) * 512] for i in range(8)] + extra]
            for _ in range(10):
                stock.append((R.bufs[_][:, :], []))

            def get():
                buf, fr = stock.pop(0)
                for q in ENG:
                    q.after(fr)
                return buf

            def put(*bufs):
                m = marks()
                for b_ in bufs:
                    stock.append((b_, m))

            mcur = [0]

            def rec_tile(j):
                js = slice(j * P, (j + 1) * P)
                RK, VV, QK = get(), get(), get()
                for dst, srcs in ((RK, [hbT[:, a, js] for a in range(4)]),
                                  (VV, [hbT[:, 4, js], hbT[:, 5, js], gT[:, 4, js], gT[:, 5, js]]),
                                  (QK, [gT[:, a, js] for a in range(4)])):
                    i, b, fr = B.take()
                    t1 = trs([(b[:, n * P:(n + 1) * P], s) for n, s in enumerate(srcs)], fr)
                    t2 = copy(dst, b[:, :], t1)
                    B.release(i, t2)
                LW, UA = get(), get()
                i1, b1, f1 = B.take()
                i2, b2, f2 = B.take()
                i3, b3, f3 = B.take()
                t1 = mms([(b1[:, 0:256], hbT[0:32, 6, js], lora[0:32, :], True, True)] +
                         ([(b1[:, 256:512], vz[0:32, js], vup[0:32, :], True, True)] if l else []), f1, tl)
                t2 = mms([(b2[:, 0:256], hbT[32:64, 6, js], lora[32:64, :], True, True)], f2)
                t3 = mms([(b3[:, 0:256], hbT[64:128, 6, js], lora[64:128, :], True, True)], f3)
                tt(LW[:, 0:256], b1[:, 0:256], rows["w0"], ALU.add, t1)
                if l:
                    tt(UA[:, 256:512], b1[:, 256:512], rows["v0"], ALU.add)
                t = tt(UA[:, 0:256], b2[:, 0:256], rows["a0"], ALU.add, t2)
                B.release(i1, t)
                B.release(i2, t)
                GG = get()
                t = copy(GG[:, 0:256], b3[:, 0:256], t3, t)
                B.release(i3, t)
                t = act(LW[:, 0:256], LW[:, 0:256], ACT.Sigmoid, marks())
                w_ = 512 if l else 256
                t = act(UA[:, 0:w_], UA[:, 0:w_], ACT.Sigmoid)
                t = ts(LW[:, 0:256], LW[:, 0:256], -float(np.exp(-0.5)), None, ALU.mult, None, t)
                t = vcopy(h64(LW[:, 256:512], 4), bc(gg[:, j, :].unsqueeze(2), [P, 4, 64]))
                r_, k_, v_ = RK[:, 0:256], RK[:, 256:512], VV[:, 0:256]
                a_ = UA[:, 0:256]
                KB, BK = get(), get()
                kk = KB[:, 0:256]
                tmp = get()
                tt(kk, k_, rows["k_k"], ALU.mult, tp)
                tt(tmp[:, 0:256], kk, kk, ALU.mult)
                nn = sml()
                t = red(nn[:, 0:4], h64(tmp[:, 0:256], 4), ALU.add)
                t = act(tmp, QK, ACT.Square, t)
                t = red(nn[:, 4:12], h64(tmp, 8), ALU.add, t)
                ts(nn[:, 0:4], nn[:, 0:4], 1e-12, None, ALU.add, None)
                t = ts(nn[:, 4:12], nn[:, 4:12], 1e-6, None, ALU.add, None)
                t = rec(nn[:, 0:12], nn[:, 0:12])
                t = act(nn[:, 0:12], nn[:, 0:12], ACT.Sqrt, t)
                t = ts(nn[:, 4:8], nn[:, 4:8], 0.125, None, ALU.mult, None, t)
                tt(h64(kk, 4), h64(kk, 4), bc(nn[:, 0:4].unsqueeze(2), [P, 4, 64]), ALU.mult)
                tt(h64(QK, 8), h64(QK, 8), bc(nn[:, 4:12].unsqueeze(2), [P, 8, 64]), ALU.mult)
                tt(BK[:, 0:256], kk, a_, ALU.mult)
                vcopy(BK[:, 256:512], QK[:, 256:512])
                bcb = bc(gb_[:, j, :].unsqueeze(2), [P, 4, 64])
                tt(h64(KB[:, 256:512], 4), h64(QK[:, 256:512], 4), bcb, ALU.mult)
                stt(tmp[:, 0:256], a_, 1.0, rows["k_a"], ALU.subtract, ALU.mult)
                stt(k_, tmp[:, 0:256], 1.0, k_, ALU.add, ALU.mult)
                if l:
                    tt(tmp[:, 0:256], vf3[:, j, :], v_, ALU.subtract)
                    tt(tmp[:, 0:256], tmp[:, 0:256], UA[:, 256:512], ALU.mult)
                    tt(v_, v_, tmp[:, 0:256], ALU.add)
                else:
                    vcopy(vf3[:, j, :], v_)
                bon = sml()
                tt(tmp[:, 0:256], r_, k_, ALU.mult)
                tt(tmp[:, 0:256], tmp[:, 0:256], rows["r_k"], ALU.mult)
                t = red(bon[:, 0:4], h64(tmp[:, 0:256], 4), ALU.add)
                put(tmp, UA)
                yield
                i1, b1, f1 = B.take()
                i2, b2, f2 = B.take()
                i3, b3, f3 = B.take()
                t1 = mms([(b1[:, :], m_bi, LW, True, True)], f1, marks())
                t2 = mms([(b2[:, :], m_br, LW, True, True)], f2)
                t3 = mms([(b3[:, 0:256], m_bs, LW[:, 0:256], True, True)] +
                         [(b3[:, 256 + 2 * p:258 + 2 * p], LW[:, p * P:(p + 1) * P], ind, True, True)
                          for p in range(4)], f3)
                E1, E3, E4, EX = get(), get(), get(), get()
                DC, gcs = sml(), sml()
                act(E1, b1[:, :], ACT.Exp, t1)
                act(E3[:, 0:256], b1[:, 0:256], ACT.Exp, scale=-1.0)
                t = act(E4, b2[:, :], ACT.Exp, t2)
                B.release(i2, t)
                act(EX[:, 0:256], b3[:, 0:256], ACT.Exp, t3)
                t = act(DC[:, 0:8], b3[:, 256:264], ACT.Exp)
                B.release(i3, t)
                t = vcopy(gcs[:, 0:4], b1[:, 256:512:64], t)
                B.release(i1, t)
                vcopy(EX[:, 256:512], E1[:, 256:512])
                Qh, K2, K3, BT = get(), get(), get(), get()
                tt(Qh[:, 0:256], r_, E1[:, 0:256], ALU.mult)
                tt(Qh[:, 256:512], QK[:, 0:256], E1[:, 256:512], ALU.mult)
                tt(K2, BK, E4, ALU.mult)
                tt(K3[:, 0:256], k_, E4[:, 0:256], ALU.mult)
                tt(BT[:, 0:256], BK[:, 0:256], E3[:, 0:256], ALU.mult)
                tt(BT[:, 256:512], k_, E3[:, 0:256], ALU.mult)
                F4 = get()
                f4v = F4.rearrange("p (a c n) -> p a c n", a=2, c=2)
                F3 = get()
                i, b, fr = B.take()
                t = trs([(b[:, (2 * a + 0) * P:(2 * a + 1) * P], QK[:, a * P:(a + 1) * P]) for a in range(2)] +
                        [(b[:, (2 * a + 1) * P:(2 * a + 2) * P], KB[:, 256 + a * P:384 + a * P]) for a in range(2)],
                        fr, marks())
                t2 = copy(F4, b[:, :], t)
                B.release(i, t2)
                t = tt(KB, KB, EX, ALU.mult, t)
                put(E1, E3, E4, EX, BK)
                i, b, fr = B.take()
                t = trs([(b[:, a * P:(a + 1) * P], QK[:, 256 + a * P:384 + a * P]) for a in range(2)] +
                        [(b[:, (2 + a) * P:(3 + a) * P], Qh[:, 256 + a * P:384 + a * P]) for a in range(2)],
                        fr, t)
                t2 = copy(F3, b[:, :], t)
                B.release(i, t2)
                F1, F2 = get(), get()
                f1v = F1.rearrange("p (a c n) -> p a c n", a=2, c=2)
                i, b, fr = B.take()
                t = trs([(b[:, (2 * a) * P:(2 * a + 1) * P], Qh[:, a * P:(a + 1) * P]) for a in range(2)] +
                        [(b[:, (2 * a + 1) * P:(2 * a + 2) * P], KB[:, a * P:(a + 1) * P]) for a in range(2)],
                        fr, marks())
                t2 = copy(F1, b[:, :], t)
                B.release(i, t2)
                i, b, fr = B.take()
                t = trs([(b[:, a * P:(a + 1) * P], BT[:, a * P:(a + 1) * P]) for a in range(4)], fr)
                t2 = copy(F2, b[:, :], t)
                B.release(i, t2)
                put(QK, BT, Qh)
                yield
                i, b, fr = B.take()
                t = mms([(b[:, h * P:(h + 1) * P], bc(gg[:, j, h:h + 1], [P, P]), m_bi, True, True)
                         for h in range(4)], fr, marks())
                DT, DN = get(), get()
                for h in range(4):
                    hs = slice(h * P, (h + 1) * P)
                    t1 = ts(DT[:, hs], b[:, hs], gcs[:, h:h + 1], 0.0, ALU.subtract, ALU.min, t)
                    t2 = ts(DN[:, hs], b[:, hs], gcs[:, h:h + 1], 0.0, ALU.subtract, ALU.max)
                B.release(i, t2)
                act(DT, DT, ACT.Exp, t2)
                t = act(DN, DN, ACT.Exp, scale=-1.0)
                RW = [get() for _ in range(4)]
                tn = marks()
                for h in range(4):
                    i, b, fr = B.take()
                    fa = F1.rearrange("p (a n) -> p a n", a=2)[hb(h), h // 2, :]
                    p_ = h // 2
                    t1 = mms([(b[:, 0:256], F2[hb(h), p_ * P:(p_ + 1) * P], fa, True, True),
                              (b[:, 256:512], F2[hb(h), 256 + p_ * P:384 + p_ * P], fa, True, True)], fr, tn)
                    t2 = tt(RW[h].rearrange("p (a n) -> p a n", a=2), b[:, :].rearrange("p (a n) -> p a n", a=2),
                            bc(m_bibs.unsqueeze(1), [P, 2, 256]), ALU.mult, t1)
                    B.release(i, t2)
                NR, NG = get(), get()
                for par in range(2):
                    i, b, fr = B.take()
                    t1 = mms([(b[:, q * P:(q + 1) * P], f1v[64 * par:64 * par + 64, q, 1, :],
                               F2[64 * par:64 * par + 64, q * P:(q + 1) * P], True, True) for q in range(2)] +
                             [(b[:, (2 + q) * P:(3 + q) * P], f4v[64 * par:64 * par + 64, q, 1, :],
                               F3[64 * par:64 * par + 64, q * P:(q + 1) * P], True, True) for q in range(2)], fr)
                    nv = NR.rearrange("p (q r n) -> p q r n", q=2, r=2)[:, :, par, :]
                    gv = NG.rearrange("p (q r n) -> p q r n", q=2, r=2)[:, :, par, :]
                    mb = bc(m_br.unsqueeze(1), [P, 2, P])
                    tt(nv, b[:, 0:256].rearrange("p (q n) -> p q n", q=2), mb, ALU.mult, t1)
                    t2 = tt(gv, b[:, 256:512].rearrange("p (q n) -> p q n", q=2), mb, ALU.mult)
                    B.release(i, t2)
                tt(NG, NG, DN, ALU.mult, t)
                PN = [get(), get()]
                for par in range(2):
                    i, b, fr = B.take()
                    t1 = mms([(b[:, q * 256:(q + 1) * 256], F3[64 * par:64 * par + 64, q * P:(q + 1) * P],
                               F4.rearrange("p (a n) -> p a n", a=2)[64 * par:64 * par + 64, q, :], True, True)
                              for q in range(2)], fr)
                    pv = PN[par].rearrange("p (q c n) -> p q c n", q=2, c=2)
                    t2 = tt(PN[par].rearrange("p (q n) -> p q n", q=2), b[:, :].rearrange("p (q n) -> p q n", q=2),
                            bc(m_bibs.unsqueeze(1), [P, 2, 256]), ALU.mult, t1)
                    B.release(i, t2)
                    dv = DT.rearrange("p (q r n) -> p q r n", q=2, r=2)[:, :, par, :]
                    for c in range(2):
                        tt(pv[:, :, c, :], pv[:, :, c, :], dv, ALU.mult)
                put(DT, DN, F4, F2)
                yield

                def lv(k, tr):
                    o = C_LV + (k + 6 * tr) * P
                    return bc(con[:, o:o + P].unsqueeze(1), [P, 4, P])

                def v4(ap):
                    return ap.rearrange("p (h n) -> p h n", h=4)
                DR, DRt, DG, DGt = get(), get(), get(), get()
                idb = bc(ident.unsqueeze(1), [P, 4, P])
                for h in range(4):
                    hs = slice(h * P, (h + 1) * P)
                    tt(DR[:, hs], RW[h][:, 128:256], con[:, C_LV:C_LV + P], ALU.mult)
                    tt(DG[:, hs], PN[h % 2][:, (h // 2) * 256 + 128:(h // 2) * 256 + 256],
                       con[:, C_LV:C_LV + P], ALU.mult)
                tt(v4(DRt), v4(NR), lv(0, 1), ALU.mult)
                tt(v4(DGt), v4(NG), lv(0, 1), ALU.mult)
                for x in (DR, DG, DRt, DGt):
                    t = tt(v4(x), idb, v4(x), ALU.subtract)
                tD = {0: t, 1: t}
                for k in range(1, 6):
                    ym = {}
                    for g, (N_, D_, Dt_) in enumerate(((NR, DR, DRt), (NG, DG, DGt))):
                        i, b, fr = B.take()
                        t1 = mms([(b[:, h * P:(h + 1) * P], N_[:, h * P:(h + 1) * P], D_[:, h * P:(h + 1) * P],
                                   True, True) for h in range(4)], fr, tD[g])
                        y_ = get()
                        t2 = tt(v4(y_), v4(b[:, :]), lv(k, 0), ALU.mult, t1)
                        B.release(i, t2)
                        ym[g] = (y_, t2)
                    for g, (N_, D_, Dt_) in enumerate(((NR, DR, DRt), (NG, DG, DGt))):
                        y_, t2 = ym[g]
                        i, b, fr = B.take()
                        t1 = mms([(b[:, h * P:(h + 1) * P], Dt_[:, h * P:(h + 1) * P], y_[:, h * P:(h + 1) * P],
                                   True, True) for h in range(4)], fr, t2)
                        if k < 5:
                            i_, b_, fr_ = B.take()
                            t1_ = mms([(b_[:, h * P:(h + 1) * P], y_[:, h * P:(h + 1) * P],
                                        Dt_[:, h * P:(h + 1) * P], True, True) for h in range(4)], fr_)
                            t1 = t1_
                        t3 = tt(D_, D_, b[:, :], ALU.subtract, t1)
                        B.release(i, t3)
                        if k < 5:
                            t3 = tt(Dt_, Dt_, b_[:, :], ALU.subtract)
                            B.release(i_, t3)
                        tD[g] = t3
                        put(y_)
                    yield
                put(DRt, DGt, NR, NG)
                X, WT = get(), get()
                i, b, fr = B.take()
                t1 = mms([(b[:, h * 64:(h + 1) * 64], RW[h][:, 384:512], VV[:, h * 64:(h + 1) * 64], True, True)
                          for h in range(4)], fr, marks())
                t2 = copy(X[:, 0:256], b[:, 0:256], t1)
                B.release(i, t2)
                t2 = stt(h64(X[:, 256:512], 4), h64(VV[:, 256:512], 4), -1.0, bcb, ALU.mult, ALU.mult)
                i, b, fr = B.take()
                t1 = mms([(b[hb(h), (h // 2) * P:(h // 2 + 1) * P], KB[:, h * 64:(h + 1) * 64],
                           (DR if h < 4 else DG)[:, (h % 4) * P:(h % 4 + 1) * P], True, True) for h in range(8)], fr)
                t2 = copy(WT, b[:, :], t1, eng="S")
                B.release(i, t2)
                put(KB)
                UN = UNs[j % 2]
                tm_ = marks()
                m0s = []
                for e_ in range(2):
                    rs = slice(64 * e_, 64 * e_ + 64)
                    M = Ms[mcur[0] % 4]
                    Mn = Ms[(mcur[0] + 1) % 4]
                    mcur[0] += 1
                    m0s.append(M)
                    bks = []
                    for par in range(2):
                        i, b, fr = B.take()
                        lst = []
                        for q in range(4):
                            h = 2 * q + par
                            TT_ = (DR if h < 4 else DG)[:, (h % 4) * P + 64 * e_:(h % 4) * P + 64 * e_ + 64]
                            o = b[rs, q * 64:(q + 1) * 64]
                            lst.append((o, TT_, X[:, h * 64:(h + 1) * 64], True, False))
                            lst.append((o, WT[hb(h), q * P + 64 * e_:q * P + 64 * e_ + 64],
                                        M[hb(h), q * 64:(q + 1) * 64], False, True))
                        t1 = mms(lst, fr, tm_)
                        t2 = copy(UN[rs, par * 256:(par + 1) * 256], b[rs, 0:256], t1, scale=-1.0,
                                  eng="SV"[par])
                        B.release(i, t2)
                        bks.append(t2)
                    tt(h64(Mn, 4), h64(M, 4), bc(DC[:, e_:8:2].unsqueeze(2), [P, 4, 64]), ALU.mult)
                    i, b, fr = B.take()
                    lst = []
                    for h in range(8):
                        o = b[hb(h), (h // 2) * 64:(h // 2) * 64 + 64]
                        un = UN[rs, (h % 2) * 256 + (h // 2) * 64:(h % 2) * 256 + (h // 2) * 64 + 64]
                        lst.append((o, K2[rs, h * 64:(h + 1) * 64], un, True, h >= 4))
                        if h < 4:
                            lst.append((o, K3[rs, h * 64:(h + 1) * 64], VV[rs, h * 64:(h + 1) * 64], False, True))
                    t1 = mms(lst, fr, bks)
                    tm_ = tt(Mn, Mn, b[:, 0:256], ALU.add, t1)
                    B.release(i, tm_)
                yield
                Y = get()
                for par in range(2):
                    i, b, fr = B.take()
                    lst = []
                    for q in range(4):
                        h = 2 * q + par
                        o = b[:, q * 64:(q + 1) * 64]
                        un = UN[:, par * 256 + q * 64:par * 256 + q * 64 + 64]
                        if h < 4:
                            lst.append((o, RW[h][:, 0:128], un, True, False))
                            lst.append((o, RW[h][:, 256:384], VV[:, h * 64:(h + 1) * 64], False, False))
                        else:
                            lst.append((o, PN[par][:, (q - 2) * 256:(q - 2) * 256 + 128], un, True, False))
                        for e_ in range(2):
                            if h < 4:
                                qs = f1v[hb(h), q, 0, 64 * e_:64 * e_ + 64]
                            else:
                                qs = F3[hb(h), 256 + (q - 2) * P + 64 * e_:256 + (q - 2) * P + 64 * e_ + 64]
                            lst.append((b[64 * e_:64 * e_ + 64, q * 64:(q + 1) * 64], qs,
                                        m0s[e_][hb(h), q * 64:(q + 1) * 64], False, e_ == 1))
                    t1 = mms(lst, fr)
                    yv = Y.rearrange("p (q r n) -> p q r n", q=4, r=2)[:, :, par, :]
                    t2 = copy(yv, b[:, 0:256].rearrange("p (q n) -> p q n", q=4), t1, eng="V")
                    B.release(i, t2)
                put(*RW, *PN, DR, DG, X, WT, K2, K3, F1, F3)
                tmp, tmp2 = get(), get()
                yr, yg = Y[:, 0:256], Y[:, 256:512]
                s1 = sml()
                s2 = sml()
                t = red(s1[:, 0:4], h64(yr, 4), ALU.add, t2)
                ts(s1[:, 0:4], s1[:, 0:4], 1.0 / 64, None, ALU.mult, None)
                tt(h64(yr, 4), h64(yr, 4), bc(s1[:, 0:4].unsqueeze(2), [P, 4, 64]), ALU.subtract)
                t = tt(tmp, Y, Y, ALU.mult)
                red(s2[:, 0:8], h64(tmp, 8), ALU.add)
                ts(s2[:, 0:4], s2[:, 0:4], 1.0 / 64, 64e-5, ALU.mult, ALU.add)
                t = ts(s2[:, 4:8], s2[:, 4:8], 1.0 / 64, 1e-6, ALU.mult, ALU.add)
                t = act(s2[:, 0:8], s2[:, 0:8], ACT.Sqrt, t)
                t = rec(s2[:, 0:8], s2[:, 0:8], t)
                t = act(tmp[:, 0:256], gz[:, j, 0:256], ACT.Sigmoid, t)
                tt(h64(Y, 8), h64(Y, 8), bc(s2[:, 0:8].unsqueeze(2), [P, 8, 64]), ALU.mult, t)
                tt(yr, yr, rows["gn_w"], ALU.mult)
                tt(yr, yr, rows["gn_b"], ALU.add)
                tt(h64(tmp2[:, 0:256], 4), h64(v_, 4), bc(bon[:, 0:4].unsqueeze(2), [P, 4, 64]), ALU.mult)
                tt(yr, yr, tmp2[:, 0:256], ALU.add)
                tt(mx[:, j, 512:768], yr, GG[:, 0:256], ALU.mult)
                tt(h64(yg, 4), h64(yg, 4), bc(rows["on"].unsqueeze(1), [P, 4, 64]), ALU.mult)
                tt(tmp[:, 0:256], tmp[:, 0:256], gz[:, j, 0:256], ALU.mult)
                tt(mx[:, j, 768:1024], yg, tmp[:, 0:256], ALU.mult)
                put(Y, tmp, tmp2, RK, VV, LW, GG)

            for j in range(4):
                for _ in rec_tile(j):
                    pass
            assert len(stock) == 18 + len(extra)

            barrier()
            debug(f"my{l}", mix[:, :])
            t = to_T(mx, xT, None)
            for c in range(4):
                wi, w, tw = wmat(A["w_out_2"][l], 0, 8, c * 256, 256)
                for j in range(NT):
                    i, b, t1 = proj_T(w, tw, 0, 256, j, t)
                    xs = xtm[:, j, c * 256:(c + 1) * 256]
                    t2 = tt(xs, xs, b[:, 0:256], ALU.add, t1)
                    B.release(i, t2)
                W.release(wi, t1)
            debug(f"xb{l}", x_tm[:, :])
            barrier()
            t = rms_norm_T(colat[("ffn", l, 1)], marks())
            barrier()
            t = ffn(A["ffn_w_gate_2"][l, 1], A["ffn_w_up_2"][l, 1], A["ffn_w_down_2"][l, 1], t, fin2)

        for i in range(NT):
            t = SP.dma("out", dcount, lambda e, i=i: e.dma_start(out[0, i * P:(i + 1) * P, :], xtm[:, i, :]), marks())
        SP.ops.append((None, [t], None))
        if "dbg" in dcount:
            SP.ops.append((None, [("dbg", dcount["dbg"])], None))

        for q in ENG + (SP,):
            for fn, w, inc in q.ops:
                for s, v in w:
                    sem(s)
                if inc:
                    sem(inc[0])
        block = ctx.enter_context(nc.Block())

        def play(q):
            def body(e):
                seen = {}
                for fn, w, inc in q.ops:
                    need = {}
                    for s, v in w:
                        if v > seen.get(s, 0):
                            need[s] = max(need.get(s, 0), v)
                    for s, v in need.items():
                        e.wait_ge(sems[s], v)
                        seen[s] = v
                    if fn is not None:
                        ins = fn(e)
                        if inc:
                            ins.then_inc(sems[inc[0]], inc[1])
            return body

        block.tensor(play(PE))
        block.vector(play(V))
        block.scalar(play(S))
        block.gpsimd(play(G))
        block.sync(play(SP))


_INS = ['x', 'w_in', 'fox_b_f', 'mla_g_q', 'mla_g_kv', 'mla_w_uq', 'mla_w_ukv', 'swa_sinks', 'mix_g', 'w_o',
        'ln1_g', 'ln1_b', 'w_gate', 'w_up', 'w_down', 'ln2_g', 'ln2_b', 'ffn_norm_2', 'ffn_w_gate_2',
        'ffn_w_up_2', 'ffn_w_down_2', 'mix_norm_2', 'w_in_2', 'w_out_2', 'att_q_norm_2', 'att_k_norm_2',
        'rwkv_mu_2', 'rwkv_w0_2', 'rwkv_w_up_2', 'rwkv_a0_2', 'rwkv_a_up_2', 'rwkv_g_up_2', 'rwkv_k_k_2',
        'rwkv_k_a_2', 'rwkv_r_k_2', 'rwkv_gn_w_2', 'rwkv_gn_b_2', 'rwkv_v0_2', 'rwkv_v_down_2',
        'rwkv_v_up_2', 'gdn_conv_2', 'gdn_a_log_2', 'gdn_dt_bias_2', 'gdn_o_norm_2']
_DBG = []


def kernel(**inputs):
    import numpy as _np
    import concourse.bacc as _bacc
    from concourse import mybir as _mybir
    from concourse.bass_utils import run_bass_kernel_spmd as _run

    nc = _bacc.Bacc("TRN2", target_bir_lowering=False, num_devices=1)
    c1, c2 = make_consts()
    arrays, aps = {}, {}
    for name in _INS + ["c_one", "c_two"]:
        a = c1 if name == "c_one" else c2 if name == "c_two" else _np.ascontiguousarray(inputs[name])
        arrays[f"in_{name}_dram"] = a
        aps[name] = nc.dram_tensor(f"in_{name}_dram", a.shape, _mybir.dt.from_np(a.dtype), kind="ExternalInput").ap()
    out = nc.dram_tensor("out_0_dram", (1, T, D), F32, kind="ExternalOutput").ap()
    dbg = {n: nc.dram_tensor(f"dbg_{n}", (P, w), F32, kind="ExternalOutput").ap() for n, w in _DBG}
    build_program(nc, aps, out, dbg)
    r = _run(nc, [arrays], core_ids=[0])
    got = r.results[0]["out_0_dram"]
    if _DBG:
        return (got,) + tuple(r.results[0][f"dbg_{n}"] for n, _ in _DBG)
    return got
```

```python
from contextlib import ExitStack

import numpy as np

import concourse.bass as bass
from concourse import mybir

F32 = mybir.dt.float32
FR = mybir.dt.float32r
ALU = mybir.AluOpType
ACT = mybir.ActivationFunctionType
AX_X = mybir.AxisListType.X

P = 128
T = 512
NT = 4
D = 1024
DFF = 2816
NF = DFF // P
ALPHA = 4.0 ** 0.25
NEG = -1e30
SENT = -3e38
WCH = 1024
NRAW = 3
NHL = 3
AHEAD = NHL - 1

C_ID, C_U, C_ONE, C_CM = 0, 128, 256, 384
C_LT, C_PM, C_SM = 512, 640, 768
C_EXTRA = 896
C_AB = C_EXTRA
C_SWA = C_AB + 2
C_RP1 = C_SWA + 1024
N1 = C_RP1 + 128
C_RP2 = C_EXTRA
C_BI = C_RP2 + 256
C_BS = C_BI + 128
C_BR = C_BS + 128
C_IND = C_BR + 128
C_LV = C_IND + 2
N2 = C_LV + 12 * 128


def make_consts():
    i = np.arange(P)
    r, c = i[:, None], i[None, :]
    f = np.float32
    common = [(r == c).astype(f), (r <= c).astype(f), np.ones((P, P), f),
              np.where(c > r, f(NEG), f(0)), (r >= c).astype(f),
              np.where(r >= c, f(1e30), f(0)), (r < c).astype(f)]
    ab = np.zeros((P, 2), f)
    ab[[0, 64], 1] = 1
    ab[[1, 65], 0] = 1
    swa = []
    for h in range(4):
        dist = r + P - np.arange(2 * P)[None, :]
        slope = f(2.0 ** (-2.0 * (h + 1)))
        swa.append(np.where((dist >= 0) & (dist < P), -slope * dist.astype(f), f(NEG)).astype(f))

    def rope_tab(half):
        pos = np.arange(T, dtype=f)
        inv = (f(10000.0) ** (-np.arange(half, dtype=f) / f(half))).astype(f)
        ang = (pos[:, None] * inv[None, :]).astype(f)
        cs = np.stack([np.cos(ang), np.sin(ang)], 0).astype(f)
        return cs.reshape(2, NT, P, half).transpose(2, 0, 1, 3).reshape(P, -1)

    c1 = np.concatenate(common + [ab] + swa + [rope_tab(16)], 1)
    same = (r // 64) == (c // 64)
    lv = []
    for k in range(6):
        w = 1 << k
        m = ((r // (2 * w)) == (c // (2 * w))) & ((r // w) % 2 == 0) & ((c // w) % 2 == 1)
        lv.append(m.astype(f))
    for k in range(6):
        lv.append(lv[k].T.copy())
    ind = np.stack([(i < 64), (i >= 64)], 1).astype(f)
    c2 = np.concatenate(common + [rope_tab(32), (same & (r <= c)).astype(f), (same & (r < c)).astype(f),
                                  (same & (r > c)).astype(f), ind] + lv, 1)
    assert c1.shape[1] == N1 and c2.shape[1] == N2
    return np.ascontiguousarray(c1.astype(f)), np.ascontiguousarray(c2.astype(f))


def flat(x):
    if x is None:
        return []
    if isinstance(x, tuple) and len(x) == 2 and isinstance(x[1], int) and isinstance(x[0], str):
        return [x]
    out = []
    for y in x:
        out += flat(y)
    return out


class Queue:

    def __init__(self, name, chain):
        self.name, self.chain = name, chain
        self.ops, self.n, self.pend = [], 0, []

    def after(self, *toks):
        self.pend += flat(toks)

    def __call__(self, fn, *toks, inc=True):
        w = flat(toks) + self.pend
        self.pend = []
        if self.chain and self.n:
            w.append((self.name, self.n))
        if inc:
            self.n += 1
        self.ops.append((fn, w, (self.name, 1) if inc else None))
        return (self.name, self.n)

    def dma(self, sem, count, fn, *toks):
        self.ops.append((fn, flat(toks) + self.pend, (sem, 16)))
        self.pend = []
        count[sem] = count.get(sem, 0) + 16
        return (sem, count[sem])

    def mark(self):
        return (self.name, self.n)


class Slots:

    def __init__(self, bufs):
        self.bufs, self.free, self.held, self.at = bufs, [[] for _ in bufs], [False] * len(bufs), 0

    def take(self):
        i = self.at % len(self.bufs)
        self.at += 1
        assert not self.held[i], "slot held"
        self.held[i] = True
        return i, self.bufs[i], self.free[i]

    def release(self, i, *toks):
        self.held[i] = False
        self.free[i] = flat(toks)


def weight_order(A):
    out = []

    def one(name, l, r0, nk, c0, n):
        M = A[name]
        M = M[l // 2, l % 2] if len(M.shape) == 4 else M[l]
        out.append(((name, l, r0, nk, c0, n), M))

    def f(name, l, c0, n):
        for s in range(n // P):
            one(name, l, 0, 8, c0 + s * P, P)

    def t(name, l, r0, K, c0, n):
        kk = max(1, WCH // n)
        for k0 in range(0, K, kk):
            one(name, l, r0 + k0 * P, min(kk, K - k0), c0, n)

    def ffn(g, u, d, l):
        for grp in range(2):
            for i in range(11):
                f(g, l, (11 * grp + i) * P, P)
                f(u, l, (11 * grp + i) * P, P)
            for half in range(2):
                t(d, l, 11 * grp * P, 11, half * 512, 512)

    for l in range(2):
        w = "w_in"
        f(w, l, 0, 512)
        t(w, l, 0, 8, 512, 260)
        f(w, l, 772, 384)
        t(w, l, 0, 8, 1156, 32)
        f(w, l, 1188, 512)
        t(w, l, 0, 8, 1700, 256)
        f(w, l, 1956, 384)
        t(w, l, 0, 8, 2340, 128)
        for half in range(2):
            t("w_o", l, 0, 8, half * 512, 512)
        ffn("w_gate", "w_up", "w_down", l)
    for l in range(2):
        ffn("ffn_w_gate_2", "ffn_w_up_2", "ffn_w_down_2", 2 * l)
        w = "w_in_2"
        for c0, n in ((0, 512), (512, 256), (768, 512), (1280, 72)):
            t(w, l, 0, 8, c0, n)
        f(w, l, 1352, 896)
        f(w, l, 2248, 768)
        t(w, l, 0, 8, 3016, 264)
        for half in range(2):
            t("w_out_2", l, 0, 8, half * 512, 512)
        ffn("ffn_w_gate_2", "ffn_w_up_2", "ffn_w_down_2", 2 * l + 1)
    return out


def build_program(nc, A, out, dbg):
    ctx = ExitStack()
    with ctx:
        sems = {}

        def sem(name):
            if name not in sems:
                sems[name] = ctx.enter_context(nc.semaphore(name))
            return sems[name]

        def sb(name, n, dt=F32):
            return ctx.enter_context(nc.sbuf_tensor(name, [P, n], dt))

        def sb2(*pair):
            with nc.sbuf_tensor(pair[0][0], [P, pair[0][1]], pair[0][2]) as a:
                pass
            b = ctx.enter_context(nc.sbuf_tensor(pair[1][0], [P, pair[1][1]], pair[1][2]))
            assert pair[1][1] >= pair[0][1]
            return a, b

        dcount = {}
        PE, V, S, G, SP = (Queue(n, c) for n, c in
                           (("pe", False), ("dve", True), ("act", True), ("pool", True), ("sp", False)))
        ENG = (PE, V, S, G)
        x_tm = sb("x_tm", 4096)
        mix = sb("mix", 4096)
        con = sb("con", max(N1, N2))
        cols = sb("cols", 256)
        small = sb("small", 64 * 16)
        wraw = [sb(f"wraw{i}", WCH) for i in range(NRAW)]
        whl = [(sb(f"wh{i}", WCH, FR), sb(f"wl{i}", WCH, FR)) for i in range(NHL)]
        vfirst = sb("vfirst", 1024)
        pbuf = sb("pbuf", 2304)
        scr = [sb(f"scr{i}", 512) for i in range(8)]
        prm = [sb(f"prm{i}", D) for i in range(2)]
        x_T, spare = sb2(("x_T", 8192, FR), ("spare", 8192, F32))
        AR = 13700
        h_T, arena = sb2(("h_T", 11 * 2 * T, FR), ("arena", AR, F32))
        psum = [ctx.enter_context(nc.psum_tensor(f"ps{i}", [P, 512], F32)) for i in range(8)]
        RAW = Slots(wraw)
        HL = Slots(whl)
        PR = Slots(prm)
        B = Slots(psum)
        R = Slots(scr)
        sm_at = [0]

        xtm = x_tm[:, :].rearrange("p (t d) -> p t d", t=NT)
        xTs = x_T[:, :].rearrange("p (c k t) -> p c k t", c=2, k=8)
        xTh, xTl = xTs[:, 0], xTs[:, 1]
        hTs = h_T[:, :].rearrange("p (c f t) -> p c f t", c=2, f=11)
        hTh, hTl = hTs[:, 0], hTs[:, 1]
        mx = mix[:, :].rearrange("p (t d) -> p t d", t=NT)
        ident = con[:, C_ID:C_ID + P]
        uu = con[:, C_U:C_U + P]
        ones = con[:, C_ONE:C_ONE + P]
        cmask = con[:, C_CM:C_CM + P]
        ltm = con[:, C_LT:C_LT + P]
        pmask = con[:, C_PM:C_PM + P]
        smask = con[:, C_SM:C_SM + P]

        def sml():
            sm_at[0] += 1
            o = (sm_at[0] % 64) * 16
            return small[:, o:o + 16]

        def marks():
            return [q.mark() for q in ENG if q.n]

        def barrier():
            m = marks()
            for q in ENG:
                q.after(m)
            return m

        ar_at = [0]

        def take(n, view=None, **kw):
            o = ar_at[0]
            ar_at[0] += n
            assert ar_at[0] <= AR, ar_at[0]
            v = arena[:, o:o + n]
            return v.rearrange(view, **kw) if view else v

        def rget(n, src, view=None):
            i, buf, free = PR.take()
            dst = buf[:, 0:n]
            if view:
                dst = dst.rearrange("p (k n) -> p k n", k=view)
            return i, dst, SP.dma(f"p{i}", dcount, lambda e: e.dma_start(dst, src), free)

        weights = weight_order(A)
        staged = []

        def stage(M, r0, nk, c0, n):
            src = M[r0:r0 + nk * P, c0:c0 + n].rearrange("(k p) n -> p k n", p=P)
            ri, raw, rfree = RAW.take()
            raw = raw[:, 0:nk * n].rearrange("p (k n) -> p k n", k=nk)
            tr = SP.dma(f"w{ri}", dcount, lambda e: e.dma_start(raw, src), rfree)
            i, (wh, wl), free = HL.take()
            wh = wh[:, 0:nk * n].rearrange("p (k n) -> p k n", k=nk)
            wl = wl[:, 0:nk * n].rearrange("p (k n) -> p k n", k=nk)
            t = S(lambda e: e.activation(wh, raw, ACT.Copy), tr, free)
            t = G(lambda e: e.tensor_tensor(wl, raw, wh.bitcast(F32), ALU.subtract), t)
            RAW.release(ri, t)
            staged.append((i, (wh, wl), t))

        wat = [0]

        def wmat(name, l, r0, nk, c0, n):
            assert weights[wat[0]][0] == (name, l, r0, nk, c0, n), (weights[wat[0]][0], (name, l, r0, nk, c0, n))
            wat[0] += 1
            while len(staged) < min(wat[0] + AHEAD, len(weights)):
                nm, M = weights[len(staged)]
                stage(M, *nm[2:])
            return staged[wat[0] - 1]

        def mms(lst, *toks):
            t = None
            for n, (o, l, r, st, sp) in enumerate(lst):
                t = PE(lambda e, o=o, l=l, r=r, st=st, sp=sp: e.matmul(o, l, r, start=st, stop=sp,
                                                                      skip_group_check=True),
                       *(toks if n == 0 else ()), inc=(n == len(lst) - 1))
            return t

        def trs(lst, *toks):
            t = None
            for n, (o, x) in enumerate(lst):
                k = x.shape[0]
                b = x.base_partition() if callable(x.base_partition) else x.base_partition
                t = PE(lambda e, o=o, x=x, k=k: e.transpose(o, x, ident[0:k, 0:k]),
                       *(toks if n == 0 else ()), inc=(n == len(lst) - 1))
            return t

        alt = [0]

        def copy(dst, src, *toks, scale=None, eng=None):
            if eng is None:
                alt[0] += 1
                eng = "S" if alt[0] % 2 else "V"
            if eng == "S":
                if scale is None:
                    return S(lambda e: e.activation(dst, src, ACT.Copy), *toks)
                return S(lambda e: e.activation(dst, src, ACT.Copy, scale=scale), *toks)
            if scale is None:
                return V(lambda e: e.tensor_copy(dst, src), *toks)
            return V(lambda e: e.tensor_scalar(dst, src, scale, None, ALU.mult), *toks)

        def tt(dst, a, b, op, *toks):
            return V(lambda e: e.tensor_tensor(dst, a, b, op), *toks)

        def ts(dst, a, s1, s2, o1, o2, *toks):
            if s2 is None:
                return V(lambda e: e.tensor_scalar(dst, a, s1, None, o1), *toks)
            return V(lambda e: e.tensor_scalar(dst, a, s1, s2, o1, o2), *toks)

        def stt(dst, a, s, b, o1, o2, *toks):
            return V(lambda e: e.scalar_tensor_tensor(out=dst, in0=a, scalar=s, in1=b, op0=o1, op1=o2), *toks)

        def act(dst, src, f, *toks, **kw):
            return S(lambda e: e.activation(dst, src, f, **kw), *toks)

        def red(dst, src, op, *toks, **kw):
            return V(lambda e: e.tensor_reduce(dst, src, AX_X, op, **kw), *toks)

        def rec(dst, src, *toks):
            return V(lambda e: e.reciprocal(dst, src), *toks)

        def vcopy(dst, src, *toks):
            return V(lambda e: e.tensor_copy(dst, src), *toks)

        def memset(dst, v, *toks):
            return V(lambda e: e.memset(dst, v), *toks)

        def rstd(dst, ssq, scale, eps, *toks):
            t = ts(dst, ssq, scale, eps, ALU.mult, ALU.add, *toks)
            t = act(dst, dst, ACT.Sqrt, t)
            return rec(dst, dst, t)

        def bc(ap, shape):
            return ap.broadcast_to(shape)

        def dma_small(batch, dst, src, *toks):
            return S.dma(batch, dcount, lambda e: e.dma_start(dst, src, allow_slow_non_contiguous=True), *toks)

        colat = {}
        coln = [0]
        tcol = None

        def load_cols(name, src, k):
            nonlocal tcol
            o = coln[0]
            coln[0] += k
            assert coln[0] <= 256
            colat[name] = cols[:, o:o + k]
            tcol = dma_small("cols", cols[:, o:o + k], src.rearrange("(k p) -> p k", p=P))

        tcon = S.dma("con", dcount, lambda e: e.dma_start(con[:, 0:N1], A["c_one"]))
        tx = None
        for i in range(NT):
            tx = SP.dma("xin", dcount, lambda e, i=i: e.dma_start(xtm[:, i, :], A["x"][0, i * P:(i + 1) * P, :]))
        for l in range(2):
            load_cols(("gq", l), A["mla_g_q"][l], 2)
            load_cols(("gkv", l), A["mla_g_kv"][l], 1)
            load_cols(("mixg", l), A["mix_g"][l], 8)
            load_cols(("mixn", l), A["mix_norm_2"][l], 8)
            for j in range(2):
                load_cols(("ffn", l, j), A["ffn_norm_2"][l, j], 8)
            load_cols(("mu", l), A["rwkv_mu_2"][l], 7)
            for w in range(4):
                load_cols(("conv", l, w), A["gdn_conv_2"][l, w], 6)

        pb_at = [0]

        def load_row(batch, src, n, *toks):
            o = pb_at[0]
            pb_at[0] += n
            dst = pbuf[:, o:o + n]
            t = dma_small(batch, dst, src.unsqueeze(0).broadcast_to([P, n]), *toks)
            return dst, t

        def split(h, lo, src, *toks, scale=None):
            t = copy(h, src, *toks, scale=scale, eng="S")
            if scale is None:
                return tt(lo, src, h.bitcast(F32), ALU.subtract, t)
            return stt(lo, src, scale, h.bitcast(F32), ALU.mult, ALU.subtract, t)

        def to_T(src, scale_col, *toks):
            last = []
            for k in range(8):
                i, b, fr = B.take()
                t = trs([(b[:, j * P:(j + 1) * P], src[:, j, k * P:(k + 1) * P]) for j in range(NT)], fr, *toks)
                sc = None if scale_col is None else scale_col[:, k:k + 1]
                t = split(xTh[:, k, :], xTl[:, k, :], b[:, :], t, scale=sc)
                B.release(i, t)
                last.append(t)
            return last

        def proj_F(M, c0, rd):
            wi, (wh, wl), tw = wmat(*M, 0, 8, c0, P)
            i, b, fr = B.take()
            lst = []
            for k in range(8):
                lst += [(b[:, :], wh[:, k, :], xTh[:, k, :], k == 0, False),
                        (b[:, :], wh[:, k, :], xTl[:, k, :], False, False),
                        (b[:, :], wl[:, k, :], xTh[:, k, :], False, k == 7)]
            t = mms(lst, fr, tw, rd)
            HL.release(wi, t)
            return i, b, t

        def proj_T(M, r0, K, c0, n, lh, ll, rd, finish):
            bks = [B.take() for _ in range(NT)]
            kk = max(1, WCH // n)
            for k0 in range(0, K, kk):
                nk = min(kk, K - k0)
                wi, (wh, wl), tw = wmat(*M, r0 + k0 * P, nk, c0, n)
                lst = []
                for q in range(nk):
                    k = k0 + q
                    for j in range(NT):
                        o = bks[j][1][:, 0:n]
                        xh, xl = lh[:, k, j * P:(j + 1) * P], ll[:, k, j * P:(j + 1) * P]
                        lst += [(o, xh, wh[:, q, :], k == 0, False), (o, xh, wl[:, q, :], False, False),
                                (o, xl, wh[:, q, :], False, k == K - 1)]
                t = mms(lst, tw, rd, [b[2] for b in bks] if k0 == 0 else None)
                HL.release(wi, t)
            last = []
            for j in range(NT):
                tf = finish(j, bks[j][1], t)
                B.release(bks[j][0], tf)
                last.append(tf)
            return last

        def proj_s(w, tw, n, tile, rd, K, src):
            i, b, fr = B.take()
            t = mms([(b[:, 0:n], src[:, k, tile * P:(tile + 1) * P], w[:, k, 0:n], k == 0, k == K - 1)
                     for k in range(K)], fr, tw, rd)
            return i, b, t

        def rms_norm_T(gcol, *toks):
            ss = sml()
            for i in range(NT):
                t = act(mx[:, i, :], xtm[:, i, :], ACT.Square, *toks, accum_out=ss[:, i:i + 1])
            rr = sml()
            t = rstd(rr[:, 0:NT], ss[:, 0:NT], 1.0 / D, 1e-6, t)
            for i in range(NT):
                t = ts(mx[:, i, :], xtm[:, i, :], rr[:, i:i + 1], None, ALU.mult, None, t)
            return to_T(mx, gcol, t, tcol)

        def layer_norm(gsrc, bsrc, *toks):
            gi, gw, tg = rget(D, gsrc.unsqueeze(0).broadcast_to([P, D]))
            bi, bw, tb = rget(D, bsrc.unsqueeze(0).broadcast_to([P, D]))
            st, mv = [], sml()
            for i in range(NT):
                s = sml()
                for j in range(2):
                    V(lambda e, s=s, i=i, j=j: e.bn_stats(s[:, 6 * j:6 * j + 6], xtm[:, i, j * 512:(j + 1) * 512]),
                      *toks)
                t = V(lambda e, s=s, i=i: e.bn_aggr(mv[:, 2 * i:2 * i + 2], s[:, 0:12]))
            rr = sml()
            t = rstd(rr[:, 0:NT], mv[:, 1:2 * NT:2], 1.0, 1e-5, t)
            for i in range(NT):
                t = ts(xtm[:, i, :], xtm[:, i, :], mv[:, 2 * i:2 * i + 1], rr[:, i:i + 1], ALU.subtract, ALU.mult, t)
                t = tt(xtm[:, i, :], xtm[:, i, :], gw, ALU.mult, tg)
                t = tt(xtm[:, i, :], xtm[:, i, :], bw, ALU.add, tb)
            PR.release(gi, t)
            PR.release(bi, t)
            return t

        def ffn(Wg, Wu, Wd, rd, finish):
            last = None
            for grp in range(2):
                th = None
                for f in range(11):
                    c0 = (11 * grp + f) * P
                    bi, bg, t1 = proj_F(Wg, c0, rd)
                    bj, bu, t2 = proj_F(Wu, c0, rd)
                    ri, sg, rf = R.take()
                    t = act(sg[:, :], bg[:, :], ACT.Sigmoid, t1, rf)
                    t = tt(sg[:, :], sg[:, :], bg[:, :], ALU.mult, t)
                    B.release(bi, t)
                    t = tt(sg[:, :], sg[:, :], bu[:, :], ALU.mult, t2)
                    B.release(bj, t)
                    th = split(hTh[:, f, :], hTl[:, f, :], sg[:, :], t)
                    R.release(ri, th)
                for half in range(2):
                    last = proj_T(Wd, 11 * grp * P, 11, half * 512, 512, hTh, hTl, [th, last],
                                  lambda j, b, t, half=half, grp=grp: finish(j, half, grp, b, t))
            return last

        def run(gens, depth):
            live = []
            gens = list(gens)
            while gens or live:
                if gens:
                    live.append(gens.pop(0))
                for g in list(live):
                    try:
                        next(g)
                    except StopIteration:
                        live.remove(g)

        def softmax_unit(tile, nk, qk, vs, dst, *toks, mask=None, sink=None):
            bi, b, fr = B.take()
            t = mms([(b[:, c0:c1], l, r, n == 0, n == len(qk) - 1) for n, (c0, c1, l, r) in enumerate(qk)], fr, *toks)
            yield
            m = sml()
            pi, pbf, pf = R.take()
            if mask is not None:
                t = tt(pbf[:, 0:nk], b[:, 0:nk], mask, ALU.add, t, pf)
                B.release(bi, t)
                t = red(m[:, 0:1], pbf[:, 0:nk], ALU.max, t, negate=True)
                src = pbf
            else:
                src = b
                if sink is not None:
                    t = red(m[:, 2:3], b[:, 0:nk], ALU.max, t)
                    t = ts(m[:, 0:1], m[:, 2:3], sink, -1.0, ALU.max, ALU.mult, t)
                else:
                    t = red(m[:, 0:1], b[:, 0:nk], ALU.max, t, negate=True)
            te = act(pbf[:, 0:nk], src[:, 0:nk], ACT.Exp, t, pf, bias=m[:, 0:1], accum_out=m[:, 1:2])
            if mask is None:
                B.release(bi, te)
            if sink is not None:
                t = act(m[:, 3:4], sink, ACT.Exp, te, bias=m[:, 0:1])
                t = tt(m[:, 1:2], m[:, 1:2], m[:, 3:4], ALU.add, t)
            else:
                t = te
            tr = rec(m[:, 4:5], m[:, 1:2], t)
            yield
            nb = nk // P
            ti, tb, tf = B.take()
            t = trs([(tb[:, j * P:(j + 1) * P], pbf[:, j * P:(j + 1) * P]) for j in range(nb)], tf, te)
            R.release(pi, t)
            qi, qb, qf = R.take()
            t = copy(qb[:, 0:nk], tb[:, 0:nk], t, qf)
            B.release(ti, t)
            yield
            oi, ob, of = B.take()
            t = mms([(ob[:, 0:64], qb[:, j * P:(j + 1) * P], vs[j], j == 0, j == nb - 1) for j in range(nb)], of, t)
            R.release(qi, t)
            t = ts(dst, ob[:, 0:64], m[:, 4:5], None, ALU.mult, None, t, tr)
            B.release(oi, t)

        def hb(h):
            return slice((h % 2) * 64, (h % 2) * 64 + 64)

        def debug(name, ap, *toks):
            if name in dbg:
                d = dbg[name]
                S.dma("dbg", dcount, lambda e: e.dma_start(d, ap), marks())
                for q in ENG:
                    q.after(("dbg", dcount["dbg"]))

        tx_in = [tx]
        t = to_T(xtm, None, tx, tcon)
        for l in range(2):
            barrier()
            ar_at[0] = 0
            pb_at[0] = 0
            win = ("w_in", l)
            bn = f"pb1{l}"
            fb, tp = load_row(bn, A["fox_b_f"][l], 4, marks())
            snk, tp = load_row(bn, A["swa_sinks"][l], 4)
            fq = take(2 * T, "p (k t) -> p k t", k=2)
            fk = take(2 * T, "p (k t) -> p k t", k=2)
            fv = take(4 * 260, "p (t n) -> p t n", t=4)

            def load_F(c0, n, dst, scale=None):
                for s in range(n // P):
                    i, b, t = proj_F(win, c0 + s * P, None)
                    B.release(i, copy(dst[:, s, :], b[:, :], t, scale=scale))

            def load_T(c0, n, dst):
                proj_T(win, 0, 8, c0, n, xTh, xTl, None,
                       lambda j, b, t: copy(dst[:, j, 0:n], b[:, 0:n], t))

            load_F(0, 256, fq, 0.125)
            load_F(256, 256, fk)
            load_T(512, 260, fv)
            g1 = sml()
            g2 = sml()
            g3 = sml()

            def v44(x):
                return x.rearrange("p (t h) -> p t h", t=4)

            t = tt(v44(g1), fv[:, :, 256:260], bc(fb.unsqueeze(1), [P, 4, 4]), ALU.add, marks(), tp)
            t = ts(g2, g1, -1.0, None, ALU.mult, None)
            t = tt(g2, g2, g1, ALU.max)
            t = act(g2, g2, ACT.Exp, t, scale=-1.0)
            t = act(g2, g2, ACT.Ln, t, bias=1.0)
            t = ts(g1, g1, 0.0, None, ALU.min, None, t)
            t = tt(g3, g1, g2, ALU.subtract)
            LQ = take(4 * 2 * 128, "p (t a c) -> p t a c", t=4, a=2)
            LK = take(4 * 2 * 128, "p (t a c) -> p t a c", t=4, a=2)
            AQ = take(2 * T, "p (a t) -> p a t", a=2)
            AK = take(2 * T, "p (a t) -> p a t", a=2)
            memset(LQ, 0.0)
            memset(LK, 0.0)
            for a in range(2):
                for q in range(2):
                    src = v44(g3)[:, :, 2 * a + q:2 * a + q + 1]
                    vcopy(LQ[:, :, a, 64 * q:64 * q + 1], src)
                    t = ts(LK[:, :, a, 64 * q + 1:64 * q + 2], src, -1.0, None, ALU.mult, None)
            for L_, O_, cc in ((LQ, AQ, 0), (LK, AK, 1)):
                for a in range(2):
                    i, b, fr = B.take()
                    t2 = mms([(b[:, tb * P:(tb + 1) * P], L_[:, jt, a, :], uu if jt == tb else ones,
                               jt == 0, jt == tb) for tb in range(4) for jt in range(tb + 1)], fr, t)
                    t3 = act(O_[:, a, :], b[:, :], ACT.Identity, t2, bias=con[:, C_AB + cc:C_AB + cc + 1])
                    B.release(i, t3)
            t = marks()

            def fox_unit(h, i):
                a, nk = h // 2, (i + 1) * P
                qk = [(0, nk, fq[hb(h), a, i * P:nk], fk[hb(h), a, 0:nk]),
                      (0, nk, AQ[hb(h), a, i * P:nk], AK[hb(h), a, 0:nk]),
                      (i * P, nk, ident, cmask)]
                return softmax_unit(i, nk, qk, [fv[:, j, h * 64:h * 64 + 64] for j in range(i + 1)],
                                    mx[:, i, h * 64:h * 64 + 64], t)
            run([fox_unit(h, i) for h in range(4) for i in range(4)], 4)

            barrier()
            ar_at[0] = 0
            cqg = take(2 * T, "p (k t) -> p k t", k=2)
            ckg = take(T, "p (k t) -> p k t", k=1)
            sq2 = take(3 * T, "p (k t) -> p k t", k=3)
            kr = take(4 * 32, "p (t n) -> p t n", t=4)
            qtm = take(4 * 384, "p (t n) -> p t n", t=4)
            ktm = take(4 * 384, "p (t n) -> p t n", t=4)
            vtm = take(4 * 256, "p (t n) -> p t n", t=4)
            qTh = take(4 * T, "p (h t) -> p h t", h=4)
            kTh = take(4 * T, "p (h t) -> p h t", h=4)
            rt = take(4 * 256, "p (a n) -> p a n", a=4)
            gq, gkv = colat[("gq", l)], colat[("gkv", l)]
            for s in range(3):
                i, b, t = proj_F(win, 772 + s * P, None)
                t2 = act(sq2[:, s, :], b[:, :], ACT.Square, t)
                if s < 2:
                    t3 = ts(cqg[:, s, :], b[:, :], gq[:, s:s + 1], None, ALU.mult, None, t2, tcol)
                else:
                    t3 = ts(ckg[:, 0, :], b[:, :], gkv[:, 0:1], None, ALU.mult, None, t2)
                B.release(i, t3)
            load_T(1156, 32, kr)
            i, b, fr = B.take()
            t = mms([(b[:, 8 * k + j:8 * k + j + 1], sq2[:, s, j * P:(j + 1) * P], ones[:, 0:1], s in (0, 2), s in (1, 2))
                     for j in range(NT) for k, s in ((0, 0), (0, 1), (1, 2))], fr, marks())
            rq, rk = sml(), sml()
            t = ts(rq[:, 0:4], b[:, 0:4], 1.0 / 256, 1e-6, ALU.mult, ALU.add, t)
            t = ts(rk[:, 0:4], b[:, 8:12], 1.0 / 128, 1e-6, ALU.mult, ALU.add)
            B.release(i, t)
            act(rq[:, 0:4], rq[:, 0:4], ACT.Sqrt, t)
            t = act(rk[:, 0:4], rk[:, 0:4], ACT.Sqrt)
            rec(rq[:, 0:4], rq[:, 0:4], t)
            rec(rk[:, 0:4], rk[:, 0:4])
            t = ts(rq[:, 0:4], rq[:, 0:4], 96.0 ** -0.5, None, ALU.mult, None)
            wi, wuq, twq = rget(768, A["mla_w_uq"][l].rearrange("(k p) n -> p k n", p=P), view=2)
            wj, wukv, twk = rget(512, A["mla_w_ukv"][l].rearrange("(k p) n -> p k n", p=P), view=1)
            for j in range(NT):
                i, b, t1 = proj_s(wuq, twq, 384, j, t, 2, cqg)
                t2 = ts(qtm[:, j, :], b[:, 0:384], rq[:, j:j + 1], None, ALU.mult, None, t1)
                B.release(i, t2)
                i, b, t1 = proj_s(wukv, twk, 512, j, t, 1, ckg)
                bv = b[:, :].rearrange("p (h a d) -> p h a d", h=4, a=2)
                kv_ = ktm[:, j, :].rearrange("p (h d) -> p h d", h=4)
                t2 = ts(kv_[:, :, 0:64], bv[:, :, 0, :], rk[:, j:j + 1], None, ALU.mult, None, t1)
                t2 = ts(vtm[:, j, :].rearrange("p (h d) -> p h d", h=4), bv[:, :, 1, :], rk[:, j:j + 1],
                        None, ALU.mult, None)
                B.release(i, t2)
            PR.release(wi, t1)
            PR.release(wj, t1)
            cosb = con[:, C_RP1:C_RP1 + 64].rearrange("p (t n) -> p t n", t=4)
            sinb = con[:, C_RP1 + 64:C_RP1 + 128].rearrange("p (t n) -> p t n", t=4)

            def rope(x1, x2, cs, sn, tmp, shape):
                a, b_, c_, d_ = tmp
                tt(a, x1, cs, ALU.mult, marks())
                tt(b_, x2, sn, ALU.mult)
                tt(c_, x1, sn, ALU.mult)
                tt(d_, x2, cs, ALU.mult)
                tt(x1, a, b_, ALU.subtract)
                return tt(x2, c_, d_, ALU.add)

            for j in range(NT):
                q4 = qtm[:, j, :].rearrange("p (h d) -> p h d", h=4)
                tm = [rt[:, a, 0:64].rearrange("p (h d) -> p h d", h=4) for a in range(4)]
                rope(q4[:, :, 64:80], q4[:, :, 80:96], bc(cosb[:, j, :].unsqueeze(1), [P, 4, 16]),
                     bc(sinb[:, j, :].unsqueeze(1), [P, 4, 16]), tm, None)
            tm = [rt[:, a, 0:64].rearrange("p (h d) -> p h d", h=4) for a in range(4)]
            rope(kr[:, :, 0:16], kr[:, :, 16:32], cosb, sinb, tm, None)
            for j in range(NT):
                t = vcopy(ktm[:, j, :].rearrange("p (h d) -> p h d", h=4)[:, :, 64:96],
                          bc(kr[:, j, :].unsqueeze(1), [P, 4, 32]))
            for h in range(4):
                for src, dst in ((qtm, qTh), (ktm, kTh)):
                    i, b, fr = B.take()
                    t1 = trs([(b[0:96, j * P:(j + 1) * P], src[:, j, h * 96:h * 96 + 96]) for j in range(NT)], fr, t)
                    t2 = copy(dst[0:96, h, :], b[0:96, :], t1)
                    B.release(i, t2)
            t = marks()

            def mla_unit(h, i):
                nk = (i + 1) * P
                qk = [(0, nk, qTh[0:96, h, i * P:nk], kTh[0:96, h, 0:nk]), (i * P, nk, ident, cmask)]
                return softmax_unit(i, nk, qk, [vtm[:, j, h * 64:h * 64 + 64] for j in range(i + 1)],
                                    mx[:, i, 256 + h * 64:256 + h * 64 + 64], t)
            run([mla_unit(h, i) for h in range(4) for i in range(4)], 4)

            barrier()
            ar_at[0] = 0
            sq = take(2 * T, "p (k t) -> p k t", k=2)
            sk = take(2 * T, "p (k t) -> p k t", k=2)
            sv = take(4 * 256, "p (t n) -> p t n", t=4)
            zbuf = [take(1280) for _ in range(3)]
            spbuf = [take(1280) for _ in range(3)]
            ZS, SS = Slots(zbuf), Slots(spbuf)
            load_F(1188, 256, sq, 0.125)
            load_F(1444, 256, sk)
            load_T(1700, 256, sv)
            t = marks()

            def blk(s, c):
                if s == c:
                    return s * P
                return {0: 512, 2: 896, 1: 1024}[s] + (c - s - 1) * P

            def stick_unit(h):
                a = h // 2
                zi, z, zf = ZS.take()
                si, sp, sf = SS.take()
                tz = []
                parts = [(0, [(s, s, s + 1) for s in range(4)]), (512, [(0, 1, 4), (2, 3, 4)]), (1024, [(1, 2, 4)])]
                for base, ents in parts:
                    bi, b, fr = B.take()
                    wdt = sum((c1 - c0) * P for _, c0, c1 in ents)
                    t1 = mms([(b[:, blk(s, c0) - base:blk(s, c0) - base + (c1 - c0) * P], sk[hb(h), a, s * P:(s + 1) * P],
                               sq[hb(h), a, c0 * P:c1 * P], True, True) for s, c0, c1 in ents], fr, t)
                    t2 = copy(z[:, base:base + wdt], b[:, 0:wdt], t1, zf)
                    B.release(bi, t2)
                    tz.append(t2)
                yield
                t1 = act(sp[:, :], z[:, :], ACT.Abs, tz, sf)
                t1 = act(sp[:, :], sp[:, :], ACT.Exp, scale=-1.0)
                t1 = act(sp[:, :], sp[:, :], ACT.Ln, bias=1.0)
                t1 = stt(sp[:, :], z[:, :], 0.0, sp[:, :], ALU.max, ALU.add, t1)
                sd = sp[:, 0:512].rearrange("p (s c) -> p s c", s=4)
                tsp = tt(sd, sd, bc(smask.unsqueeze(1), [P, 4, P]), ALU.mult)
                yield
                te = []
                for base, ents in parts:
                    bi, b, fr = B.take()
                    lst = []
                    for s, c0, c1 in ents:
                        for c in range(c0, c1):
                            o = b[:, blk(s, c) - base:blk(s, c) - base + P]
                            if s == c:
                                lst.append((o, ident, pmask, True, False))
                            for j in range(s, c + 1):
                                lst.append((o, ltm if j == s else ones, sp[:, blk(j, c):blk(j, c) + P],
                                            s != c and j == s, j == c))
                    wdt = sum((c1 - c0) * P for _, c0, c1 in ents)
                    t1 = mms(lst, fr, tsp)
                    t2 = tt(z[:, base:base + wdt], z[:, base:base + wdt], b[:, 0:wdt], ALU.subtract, t1)
                    B.release(bi, t2)
                SS.release(si, t1)
                te = act(z[:, :], z[:, :], ACT.Exp, t2)
                yield
                bi, b, fr = B.take()
                t1 = mms([(b[:, c * 64:c * 64 + 64], z[:, blk(s, c):blk(s, c) + P], sv[:, s, h * 64:h * 64 + 64],
                           s == 0, s == c) for c in range(4) for s in range(c + 1)], fr, te)
                ZS.release(zi, t1)
                t2 = copy(mx[:, :, 512 + h * 64:512 + h * 64 + 64], b[:, 0:256].rearrange("p (c d) -> p c d", c=4), t1)
                B.release(bi, t2)
            run([stick_unit(h) for h in range(4)], 4)

            barrier()
            ar_at[0] = 0
            wq = take(2 * T, "p (k t) -> p k t", k=2)
            wk = take(2 * T, "p (k t) -> p k t", k=2)
            wv = take(4 * 128, "p (t n) -> p t n", t=4)
            load_F(1956, 256, wq, 0.125)
            i, b, t = proj_F(win, 2212, None)
            for g in range(2):
                for q in range(2):
                    t2 = copy(wk[64 * q:64 * q + 64, g, :], b[64 * g:64 * g + 64, :], t, eng="S")
            B.release(i, t2)
            load_T(2340, 128, wv)
            t = marks()

            def swa_unit(h, i):
                a, g = h // 2, h // 2
                j0 = max(i - 1, 0)
                nk = (i + 1 - j0) * P
                so = C_SWA + 256 * h
                qk = [(0, nk, wq[hb(h), a, i * P:(i + 1) * P], wk[hb(h), g, j0 * P:(i + 1) * P]),
                      (0, nk, ident, con[:, so + 256 - nk:so + 256])]
                return softmax_unit(i, nk, qk, [wv[:, j, g * 64:g * 64 + 64] for j in range(j0, i + 1)],
                                    mx[:, i, 768 + h * 64:768 + h * 64 + 64], t, tp, sink=snk[:, h:h + 1])
            run([swa_unit(h, i) for h in range(4) for i in range(4)], 4)

            barrier()
            debug(f"mix{l}", mix[:, :])
            ss = sml()
            ri, rb, rf = R.take()
            for i in range(NT):
                for g in range(4):
                    t = act(rb[:, 0:256], mx[:, i, g * 256:(g + 1) * 256], ACT.Square, rf,
                            accum_out=ss[:, 4 * i + g:4 * i + g + 1])
            R.release(ri, t)
            rr = sml()
            t = rstd(rr, ss, 1.0 / 256, 1e-6, t)
            for i in range(NT):
                m4 = mx[:, i, :].rearrange("p (g d) -> p g d", g=4)
                t = tt(m4, m4, bc(rr[:, 4 * i:4 * i + 4].unsqueeze(2), [P, 4, 256]), ALU.mult, t)
            t = to_T(mx, colat[("mixg", l)], t, tcol)

            def add_y(j, half, b, t):
                xs = xtm[:, j, half * 512:(half + 1) * 512]
                return stt(xs, xs, ALPHA, b[:, :], ALU.mult, ALU.add, t)
            for half in range(2):
                t2 = proj_T(("w_o", l), 0, 8, half * 512, 512, xTh, xTl, t,
                            lambda j, b, t, half=half: add_y(j, half, b, t))
            t = layer_norm(A["ln1_g"][l], A["ln1_b"][l], t2)
            debug(f"x1{l}", x_tm[:, :])
            t = to_T(xtm, None, t)

            def fin1(i, half, grp, b, t):
                xs = xtm[:, i, half * 512:(half + 1) * 512]
                return stt(xs, xs, 1.0 if grp else ALPHA, b[:, :], ALU.mult, ALU.add, t)
            barrier()
            t = ffn(("w_gate", l), ("w_up", l), ("w_down", l), t, fin1)
            t = layer_norm(A["ln2_g"][l], A["ln2_b"][l], t)
            debug(f"x2{l}", x_tm[:, :])
            if l == 0:
                t = to_T(xtm, None, t)

        def fin2(i, half, grp, b, t):
            xs = xtm[:, i, half * 512:(half + 1) * 512]
            return stt(xs, b[:, :], 0.5, xs, ALU.mult, ALU.add, t)

        m = barrier()
        t = S.dma("con2", dcount, lambda e: e.dma_start(con[:, 0:N2], A["c_two"]), m)
        for q in ENG:
            q.after(t)
        rope_c = con[:, C_RP2:C_RP2 + 128].rearrange("p (t n) -> p t n", t=4)
        rope_s = con[:, C_RP2 + 128:C_RP2 + 256].rearrange("p (t n) -> p t n", t=4)
        m_bi = con[:, C_BI:C_BI + P]
        m_bs = con[:, C_BS:C_BS + P]
        m_br = con[:, C_BR:C_BR + P]
        m_bibs = con[:, C_BI:C_BI + 256]
        ind = con[:, C_IND:C_IND + 2]
        vf3 = vfirst[:, :].rearrange("p (t n) -> p t n", t=4)

        def h64(ap, n):
            return ap.rearrange("p (h d) -> p h d", h=n)

        for l in range(2):
            barrier()
            pb_at[0] = 0
            bn = f"pb2{l}"
            mk = marks()
            rows = {}
            for nm, src, n in ([(k, A[f"rwkv_{k}_2"][l], 256) for k in ("w0", "a0", "k_k", "k_a")] +
                               [("r_k", A["rwkv_r_k_2"][l].rearrange("h d -> (h d)"), 256),
                                ("gn_w", A["rwkv_gn_w_2"][l], 256), ("gn_b", A["rwkv_gn_b_2"][l], 256)] +
                               ([("v0", A["rwkv_v0_2"][0], 256)] if l else []) +
                               [("qn", A["att_q_norm_2"][l], 64), ("kn", A["att_k_norm_2"][l], 64),
                                ("on", A["gdn_o_norm_2"][l], 64), ("al", A["gdn_a_log_2"][l], 4),
                                ("dt", A["gdn_dt_bias_2"][l], 4)]):
                rows[nm], tp = load_row(bn, src, n, mk)
            t = rms_norm_T(colat[("ffn", l, 0)], marks())
            barrier()
            t = ffn(("ffn_w_gate_2", 2 * l + 0), ("ffn_w_up_2", 2 * l + 0), ("ffn_w_down_2", 2 * l + 0), t, fin2)
            debug(f"xa{l}", x_tm[:, :])
            t = rms_norm_T(colat[("mixn", l)], marks())
            win = ("w_in_2", l)

            barrier()
            ar_at[0] = 0
            pa = take(4 * 1352, "p (t n) -> p t n", t=4)
            qT = take(4 * T, "p (a t) -> p a t", a=4)
            qiT = take(4 * T, "p (a t) -> p a t", a=4)
            kd = take(2 * T, "p (a t) -> p a t", a=2)
            kid = take(T)
            msk = take(3 * 512, "p (a n) -> p a n", a=3)

            def load_F2(c0, n, dst, s0):
                for s in range(n // P):
                    i, b, t = proj_F(win, c0 + s * P, None)
                    B.release(i, copy(dst[:, s0 + s, :], b[:, :], t))

            def load_T2(c0, n, dst, o2):
                proj_T(win, 0, 8, c0, n, xTh, xTl, None,
                       lambda j, b, t: copy(dst[:, j, o2:o2 + n], b[:, 0:n], t))

            for c0, n in ((0, 512), (512, 256), (768, 512), (1280, 72)):
                load_T2(c0, n, pa, c0)
            rr2 = take(4 * 16, "p (t n) -> p t n", t=4)
            t = marks()
            for j in range(NT):
                ri, rb, rf = R.take()
                rj, rc_, rf2 = R.take()
                t = act(rb[:, :], pa[:, j, 0:512], ACT.Square, t, rf)
                t = act(rc_[:, 0:128], pa[:, j, 512:640], ACT.Square, rf2)
                t = red(rr2[:, j, 0:8], h64(rb[:, :], 8), ALU.add, t)
                t = red(rr2[:, j, 8:10], h64(rc_[:, 0:128], 2), ALU.add, t)
                R.release(ri, t)
                R.release(rj, t)
            t = rstd(rr2[:, :, 0:10], rr2[:, :, 0:10], 1.0 / 64, 1e-6, t)
            ts(rr2[:, :, 0:8], rr2[:, :, 0:8], 0.125, None, ALU.mult, None, t)
            for j in range(NT):
                x10 = h64(pa[:, j, 0:640], 10)
                tt(x10, x10, bc(rr2[:, j, 0:10].unsqueeze(2), [P, 10, 64]), ALU.mult)
                tt(x10[:, 0:8, :], x10[:, 0:8, :], bc(rows["qn"].unsqueeze(1), [P, 8, 64]), ALU.mult, tp)
                tt(x10[:, 8:10, :], x10[:, 8:10, :], bc(rows["kn"].unsqueeze(1), [P, 2, 64]), ALU.mult)
                for c0, nh in ((0, 10), (768, 9)):
                    xx = h64(pa[:, j, c0:c0 + nh * 64], nh)
                    tk = [R.take() for _ in range(4)]
                    V.after([x[2] for x in tk])
                    tm = [x[1][:, 0:nh * 32].rearrange("p (h d) -> p h d", h=nh) for x in tk]
                    t = rope(xx[:, :, 0:32], xx[:, :, 32:64], bc(rope_c[:, j, :].unsqueeze(1), [P, nh, 32]),
                             bc(rope_s[:, j, :].unsqueeze(1), [P, nh, 32]), tm, None)
                    for x in tk:
                        R.release(x[0], t)
                t = ts(pa[:, j, 1344:1352], pa[:, j, 1344:1352], 8 ** -0.5 * 64 ** -0.5, None, ALU.mult, None)
            for a in range(4):
                for dst, c0 in ((qT, 0), (qiT, 768)):
                    i, b, fr = B.take()
                    t1 = trs([(b[:, j * P:(j + 1) * P], pa[:, j, c0 + a * P:c0 + (a + 1) * P]) for j in range(NT)], fr, t)
                    t2 = copy(dst[:, a, :], b[:, :], t1)
                    B.release(i, t2)
            i, b, fr = B.take()
            t1 = trs([(b[:, j * P:(j + 1) * P], pa[:, j, 512:640]) for j in range(NT)], fr, t)
            for g in range(2):
                for q in range(2):
                    t2 = copy(kd[64 * q:64 * q + 64, g, :], b[64 * g:64 * g + 64, :], t1, eng="S")
            B.release(i, t2)
            i, b, fr = B.take()
            t1 = trs([(b[0:64, j * P:(j + 1) * P], pa[:, j, 1280:1344]) for j in range(NT)], fr, t)
            for q in range(2):
                t2 = copy(kid[64 * q:64 * q + 64, :], b[0:64, :], t1, eng="S")
            B.release(i, t2)
            t = marks()
            for i in range(1, NT):
                nk = (i + 1) * P
                acc = msk[:, i - 1, 0:nk]
                for h in range(8):
                    bi, b, fr = B.take()
                    t1 = mms([(b[:, 0:nk], qiT[hb(h), h // 2, i * P:nk], kid[hb(h), 0:nk], True, True)], fr, t)
                    ri, rb, rf = R.take()
                    t1 = act(rb[:, 0:nk], b[:, 0:nk], ACT.Relu, t1, rf)
                    B.release(bi, t1)
                    wi_ = pa[:, i, 1344 + h:1345 + h]
                    if h == 0:
                        t1 = ts(acc, rb[:, 0:nk], wi_, None, ALU.mult, None, t1)
                    else:
                        t1 = stt(acc, rb[:, 0:nk], wi_, acc, ALU.mult, ALU.add, t1)
                    R.release(ri, t1)
                tt(msk[:, i - 1, i * P:nk], msk[:, i - 1, i * P:nk], cmask, ALU.add)
                m8 = sml()

                def top8(acc, m8):
                    V(lambda e: e.max(m8[:, 0:8], acc))
                    V(lambda e: e.match_replace(acc, m8[:, 0:8], acc, SENT))
                for _ in range(16):
                    top8(acc, m8)
                ts(acc, acc, SENT, 1.0, ALU.is_equal, ALU.subtract)
                t1 = ts(acc, acc, 1e30, None, ALU.mult, None)
            t = marks()

            def dsa_unit(h, i):
                nk = (i + 1) * P
                qk = [(0, nk, qT[hb(h), h // 2, i * P:nk], kd[hb(h), h // 4, 0:nk])]
                mask = None
                if i == 0:
                    qk.append((0, P, ident, cmask))
                else:
                    mask = msk[:, i - 1, 0:nk]
                g = h // 4
                return softmax_unit(i, nk, qk, [pa[:, j, 640 + g * 64:704 + g * 64] for j in range(i + 1)],
                                    mx[:, i, h * 64:h * 64 + 64], t, mask=mask)
            run([dsa_unit(h, i) for i in range(4) for h in range(8)], 4)

            barrier()
            ar_at[0] = 0
            hbT = take(7 * T, "p (a t) -> p a t", a=7)
            gT = take(6 * T, "p (a t) -> p a t", a=6)
            gz = take(4 * 264, "p (t n) -> p t n", t=4)
            lora = take(256)
            vdn = take(64, "p (k n) -> p k n", k=2)
            vup = take(256)
            gate = take(64, "p (a t h) -> p a t h", a=4, t=4)
            vz = take(512)
            UNs = [take(512) for _ in range(2)]
            Ms = [take(256) for _ in range(4)]
            extra = [take(512) for _ in range((AR - ar_at[0]) // 512)]
            mk = marks()
            ln_ = f"lora{l}"
            dma_small(ln_, lora[0:32, :], A["rwkv_w_up_2"][l], mk)
            dma_small(ln_, lora[32:64, :], A["rwkv_a_up_2"][l])
            tl = dma_small(ln_, lora[64:128, :], A["rwkv_g_up_2"][l])
            if l:
                dma_small(ln_, vdn, A["rwkv_v_down_2"][0].rearrange("(k p) n -> p k n", p=P))
                tl = dma_small(ln_, vup[0:32, :], A["rwkv_v_up_2"][0])
            for c0, n, s0 in ((1352, 256, 0), (1608, 256, 2), (1864, 256, 4), (2120, 128, 6)):
                load_F2(c0, n, hbT, s0)
            for c0, s0 in ((2248, 0), (2504, 2), (2760, 4)):
                load_F2(c0, 256, gT, s0)
            load_T2(3016, 264, gz, 0)
            barrier()
            mu = colat[("mu", l)]
            for s in range(7):
                ri, rb, rf = R.take()
                t = tt(rb[:, 1:512], hbT[:, s, 0:511], hbT[:, s, 1:512], ALU.subtract, rf, tcol)
                t = ts(rb[:, 0:1], hbT[:, s, 0:1], -1.0, None, ALU.mult, None)
                t = stt(hbT[:, s, :], rb[:, :], mu[:, s:s + 1], hbT[:, s, :], ALU.mult, ALU.add)
                R.release(ri, t)
            t = act(hbT[0:32, 6, :], hbT[0:32, 6, :], ACT.Tanh, t)
            t = act(hbT[64:128, 6, :], hbT[64:128, 6, :], ACT.Sigmoid, t)
            cv = [colat[("conv", l, w)] for w in range(4)]
            for s in range(6):
                ri, rb, rf = R.take()
                rj, rc_, rf2 = R.take()
                t = ts(rb[:, :], gT[:, s, :], cv[3][:, s:s + 1], None, ALU.mult, None, rf, rf2)
                for w in range(1, 4):
                    t = stt(rb[:, w:512], gT[:, s, 0:512 - w], cv[3 - w][:, s:s + 1], rb[:, w:512], ALU.mult, ALU.add)
                t = act(rc_[:, :], rb[:, :], ACT.Sigmoid, t)
                t = tt(gT[:, s, :], rb[:, :], rc_[:, :], ALU.mult, t)
                R.release(ri, t)
                R.release(rj, t)
            ga, gb_, gg, gt = (gate[:, a] for a in range(4))
            t = act(gb_, gz[:, :, 256:260], ACT.Sigmoid, t)
            t = tt(ga, gz[:, :, 260:264], bc(rows["dt"].unsqueeze(1), [P, 4, 4]), ALU.add, tp)
            ts(gt, ga, -1.0, None, ALU.mult, None)
            t = tt(gt, gt, ga, ALU.max)
            t = act(gt, gt, ACT.Exp, t, scale=-1.0)
            t = act(gt, gt, ACT.Ln, t, bias=1.0)
            t = stt(gt, ga, 0.0, gt, ALU.max, ALU.add, t)
            al = sml()
            t = act(al[:, 0:4], rows["al"], ACT.Exp, t)
            t = tt(gg, gt, bc(al[:, 0:4].unsqueeze(1), [P, 4, 4]), ALU.mult, t)
            t = ts(gg, gg, -1.0, None, ALU.mult, None)
            if l:
                i, b, fr = B.take()
                t1 = mms([(b[0:32, :], vdn[:, k, :], hbT[:, 4 + k, :], k == 0, k == 1) for k in range(2)],
                         fr, tl, marks())
                t2 = copy(vz[0:32, :], b[0:32, :], t1)
                B.release(i, t2)
            barrier()
            for u_ in UNs:
                memset(u_, 0.0)
            memset(Ms[0], 0.0)

            stock = [(x, []) for x in [spare[:, i * 512:(i + 1) * 512] for i in range(16)] + extra]
            for _ in range(8):
                stock.append((R.bufs[_][:, :], []))

            def get():
                buf, fr = stock.pop(0)
                for q in ENG:
                    q.after(fr)
                return buf

            def put(*bufs):
                m = marks()
                for b_ in bufs:
                    stock.append((b_, m))

            mcur = [0]

            def rec_tile(j):
                js = slice(j * P, (j + 1) * P)
                RK, VV, QK = get(), get(), get()
                for dst, srcs in ((RK, [hbT[:, a, js] for a in range(4)]),
                                  (VV, [hbT[:, 4, js], hbT[:, 5, js], gT[:, 4, js], gT[:, 5, js]]),
                                  (QK, [gT[:, a, js] for a in range(4)])):
                    i, b, fr = B.take()
                    t1 = trs([(b[:, n * P:(n + 1) * P], s) for n, s in enumerate(srcs)], fr)
                    t2 = copy(dst, b[:, :], t1)
                    B.release(i, t2)
                LW, UA = get(), get()
                i1, b1, f1 = B.take()
                i2, b2, f2 = B.take()
                i3, b3, f3 = B.take()
                t1 = mms([(b1[:, 0:256], hbT[0:32, 6, js], lora[0:32, :], True, True)] +
                         ([(b1[:, 256:512], vz[0:32, js], vup[0:32, :], True, True)] if l else []), f1, tl)
                t2 = mms([(b2[:, 0:256], hbT[32:64, 6, js], lora[32:64, :], True, True)], f2)
                t3 = mms([(b3[:, 0:256], hbT[64:128, 6, js], lora[64:128, :], True, True)], f3)
                tt(LW[:, 0:256], b1[:, 0:256], rows["w0"], ALU.add, t1)
                if l:
                    tt(UA[:, 256:512], b1[:, 256:512], rows["v0"], ALU.add)
                t = tt(UA[:, 0:256], b2[:, 0:256], rows["a0"], ALU.add, t2)
                B.release(i1, t)
                B.release(i2, t)
                GG = get()
                t = copy(GG[:, 0:256], b3[:, 0:256], t3, t)
                B.release(i3, t)
                t = act(LW[:, 0:256], LW[:, 0:256], ACT.Sigmoid, marks())
                w_ = 512 if l else 256
                t = act(UA[:, 0:w_], UA[:, 0:w_], ACT.Sigmoid)
                t = ts(LW[:, 0:256], LW[:, 0:256], -float(np.exp(-0.5)), None, ALU.mult, None, t)
                t = vcopy(h64(LW[:, 256:512], 4), bc(gg[:, j, :].unsqueeze(2), [P, 4, 64]))
                r_, k_, v_ = RK[:, 0:256], RK[:, 256:512], VV[:, 0:256]
                a_ = UA[:, 0:256]
                KB, BK = get(), get()
                kk = KB[:, 0:256]
                tmp = get()
                tt(kk, k_, rows["k_k"], ALU.mult, tp)
                tt(tmp[:, 0:256], kk, kk, ALU.mult)
                nn = sml()
                t = red(nn[:, 0:4], h64(tmp[:, 0:256], 4), ALU.add)
                t = act(tmp, QK, ACT.Square, t)
                t = red(nn[:, 4:12], h64(tmp, 8), ALU.add, t)
                ts(nn[:, 0:4], nn[:, 0:4], 1e-12, None, ALU.add, None)
                t = ts(nn[:, 4:12], nn[:, 4:12], 1e-6, None, ALU.add, None)
                t = rec(nn[:, 0:12], nn[:, 0:12])
                t = act(nn[:, 0:12], nn[:, 0:12], ACT.Sqrt, t)
                t = ts(nn[:, 4:8], nn[:, 4:8], 0.125, None, ALU.mult, None, t)
                tt(h64(kk, 4), h64(kk, 4), bc(nn[:, 0:4].unsqueeze(2), [P, 4, 64]), ALU.mult)
                tt(h64(QK, 8), h64(QK, 8), bc(nn[:, 4:12].unsqueeze(2), [P, 8, 64]), ALU.mult)
                tt(BK[:, 0:256], kk, a_, ALU.mult)
                vcopy(BK[:, 256:512], QK[:, 256:512])
                bcb = bc(gb_[:, j, :].unsqueeze(2), [P, 4, 64])
                tt(h64(KB[:, 256:512], 4), h64(QK[:, 256:512], 4), bcb, ALU.mult)
                stt(tmp[:, 0:256], a_, 1.0, rows["k_a"], ALU.subtract, ALU.mult)
                stt(k_, tmp[:, 0:256], 1.0, k_, ALU.add, ALU.mult)
                if l:
                    tt(tmp[:, 0:256], vf3[:, j, :], v_, ALU.subtract)
                    tt(tmp[:, 0:256], tmp[:, 0:256], UA[:, 256:512], ALU.mult)
                    tt(v_, v_, tmp[:, 0:256], ALU.add)
                else:
                    vcopy(vf3[:, j, :], v_)
                bon = sml()
                tt(tmp[:, 0:256], r_, k_, ALU.mult)
                tt(tmp[:, 0:256], tmp[:, 0:256], rows["r_k"], ALU.mult)
                t = red(bon[:, 0:4], h64(tmp[:, 0:256], 4), ALU.add)
                put(tmp, UA)
                yield
                i1, b1, f1 = B.take()
                i2, b2, f2 = B.take()
                i3, b3, f3 = B.take()
                t1 = mms([(b1[:, :], m_bi, LW, True, True)], f1, marks())
                t2 = mms([(b2[:, :], m_br, LW, True, True)], f2)
                t3 = mms([(b3[:, 0:256], m_bs, LW[:, 0:256], True, True)] +
                         [(b3[:, 256 + 2 * p:258 + 2 * p], LW[:, p * P:(p + 1) * P], ind, True, True)
                          for p in range(4)], f3)
                E1, E3, E4, EX = get(), get(), get(), get()
                DC, gcs = sml(), sml()
                act(E1, b1[:, :], ACT.Exp, t1)
                act(E3[:, 0:256], b1[:, 0:256], ACT.Exp, scale=-1.0)
                t = act(E4, b2[:, :], ACT.Exp, t2)
                B.release(i2, t)
                act(EX[:, 0:256], b3[:, 0:256], ACT.Exp, t3)
                t = act(DC[:, 0:8], b3[:, 256:264], ACT.Exp)
                B.release(i3, t)
                t = vcopy(gcs[:, 0:4], b1[:, 256:512:64], t)
                B.release(i1, t)
                vcopy(EX[:, 256:512], E1[:, 256:512])
                Qh, K2, K3, BT = get(), get(), get(), get()
                tt(Qh[:, 0:256], r_, E1[:, 0:256], ALU.mult)
                tt(Qh[:, 256:512], QK[:, 0:256], E1[:, 256:512], ALU.mult)
                tt(K2, BK, E4, ALU.mult)
                tt(K3[:, 0:256], k_, E4[:, 0:256], ALU.mult)
                tt(BT[:, 0:256], BK[:, 0:256], E3[:, 0:256], ALU.mult)
                tt(BT[:, 256:512], k_, E3[:, 0:256], ALU.mult)
                F4 = get()
                f4v = F4.rearrange("p (a c n) -> p a c n", a=2, c=2)
                F3 = get()
                i, b, fr = B.take()
                t = trs([(b[:, (2 * a + 0) * P:(2 * a + 1) * P], QK[:, a * P:(a + 1) * P]) for a in range(2)] +
                        [(b[:, (2 * a + 1) * P:(2 * a + 2) * P], KB[:, 256 + a * P:384 + a * P]) for a in range(2)],
                        fr, marks())
                t2 = copy(F4, b[:, :], t)
                B.release(i, t2)
                t = tt(KB, KB, EX, ALU.mult, t)
                put(E1, E3, E4, EX, BK)
                i, b, fr = B.take()
                t = trs([(b[:, a * P:(a + 1) * P], QK[:, 256 + a * P:384 + a * P]) for a in range(2)] +
                        [(b[:, (2 + a) * P:(3 + a) * P], Qh[:, 256 + a * P:384 + a * P]) for a in range(2)],
                        fr, t)
                t2 = copy(F3, b[:, :], t)
                B.release(i, t2)
                F1, F2 = get(), get()
                f1v = F1.rearrange("p (a c n) -> p a c n", a=2, c=2)
                i, b, fr = B.take()
                t = trs([(b[:, (2 * a) * P:(2 * a + 1) * P], Qh[:, a * P:(a + 1) * P]) for a in range(2)] +
                        [(b[:, (2 * a + 1) * P:(2 * a + 2) * P], KB[:, a * P:(a + 1) * P]) for a in range(2)],
                        fr, marks())
                t2 = copy(F1, b[:, :], t)
                B.release(i, t2)
                i, b, fr = B.take()
                t = trs([(b[:, a * P:(a + 1) * P], BT[:, a * P:(a + 1) * P]) for a in range(4)], fr)
                t2 = copy(F2, b[:, :], t)
                B.release(i, t2)
                put(QK, BT, Qh)
                yield
                i, b, fr = B.take()
                t = mms([(b[:, h * P:(h + 1) * P], bc(gg[:, j, h:h + 1], [P, P]), m_bi, True, True)
                         for h in range(4)], fr, marks())
                DT, DN = get(), get()
                for h in range(4):
                    hs = slice(h * P, (h + 1) * P)
                    t1 = ts(DT[:, hs], b[:, hs], gcs[:, h:h + 1], 0.0, ALU.subtract, ALU.min, t)
                    t2 = ts(DN[:, hs], b[:, hs], gcs[:, h:h + 1], 0.0, ALU.subtract, ALU.max)
                B.release(i, t2)
                act(DT, DT, ACT.Exp, t2)
                t = act(DN, DN, ACT.Exp, scale=-1.0)
                RW = [get() for _ in range(4)]
                tn = marks()
                for h in range(4):
                    i, b, fr = B.take()
                    fa = F1.rearrange("p (a n) -> p a n", a=2)[hb(h), h // 2, :]
                    p_ = h // 2
                    t1 = mms([(b[:, 0:256], F2[hb(h), p_ * P:(p_ + 1) * P], fa, True, True),
                              (b[:, 256:512], F2[hb(h), 256 + p_ * P:384 + p_ * P], fa, True, True)], fr, tn)
                    t2 = tt(RW[h].rearrange("p (a n) -> p a n", a=2), b[:, :].rearrange("p (a n) -> p a n", a=2),
                            bc(m_bibs.unsqueeze(1), [P, 2, 256]), ALU.mult, t1)
                    B.release(i, t2)
                NR, NG = get(), get()
                for par in range(2):
                    i, b, fr = B.take()
                    t1 = mms([(b[:, q * P:(q + 1) * P], f1v[64 * par:64 * par + 64, q, 1, :],
                               F2[64 * par:64 * par + 64, q * P:(q + 1) * P], True, True) for q in range(2)] +
                             [(b[:, (2 + q) * P:(3 + q) * P], f4v[64 * par:64 * par + 64, q, 1, :],
                               F3[64 * par:64 * par + 64, q * P:(q + 1) * P], True, True) for q in range(2)], fr)
                    nv = NR.rearrange("p (q r n) -> p q r n", q=2, r=2)[:, :, par, :]
                    gv = NG.rearrange("p (q r n) -> p q r n", q=2, r=2)[:, :, par, :]
                    mb = bc(m_br.unsqueeze(1), [P, 2, P])
                    tt(nv, b[:, 0:256].rearrange("p (q n) -> p q n", q=2), mb, ALU.mult, t1)
                    t2 = tt(gv, b[:, 256:512].rearrange("p (q n) -> p q n", q=2), mb, ALU.mult)
                    B.release(i, t2)
                tt(NG, NG, DN, ALU.mult, t)
                PN = [get(), get()]
                for par in range(2):
                    i, b, fr = B.take()
                    t1 = mms([(b[:, q * 256:(q + 1) * 256], F3[64 * par:64 * par + 64, q * P:(q + 1) * P],
                               F4.rearrange("p (a n) -> p a n", a=2)[64 * par:64 * par + 64, q, :], True, True)
                              for q in range(2)], fr)
                    pv = PN[par].rearrange("p (q c n) -> p q c n", q=2, c=2)
                    t2 = tt(PN[par].rearrange("p (q n) -> p q n", q=2), b[:, :].rearrange("p (q n) -> p q n", q=2),
                            bc(m_bibs.unsqueeze(1), [P, 2, 256]), ALU.mult, t1)
                    B.release(i, t2)
                    dv = DT.rearrange("p (q r n) -> p q r n", q=2, r=2)[:, :, par, :]
                    for c in range(2):
                        tt(pv[:, :, c, :], pv[:, :, c, :], dv, ALU.mult)
                put(DT, DN, F4, F2)
                yield

                def lv(k, tr):
                    o = C_LV + (k + 6 * tr) * P
                    return bc(con[:, o:o + P].unsqueeze(1), [P, 4, P])

                def v4(ap):
                    return ap.rearrange("p (h n) -> p h n", h=4)
                DR, DRt, DG, DGt = get(), get(), get(), get()
                idb = bc(ident.unsqueeze(1), [P, 4, P])
                for h in range(4):
                    hs = slice(h * P, (h + 1) * P)
                    tt(DR[:, hs], RW[h][:, 128:256], con[:, C_LV:C_LV + P], ALU.mult)
                    tt(DG[:, hs], PN[h % 2][:, (h // 2) * 256 + 128:(h // 2) * 256 + 256],
                       con[:, C_LV:C_LV + P], ALU.mult)
                tt(v4(DRt), v4(NR), lv(0, 1), ALU.mult)
                tt(v4(DGt), v4(NG), lv(0, 1), ALU.mult)
                for x in (DR, DG, DRt, DGt):
                    t = tt(v4(x), idb, v4(x), ALU.subtract)
                tD = {0: t, 1: t}
                for k in range(1, 6):
                    ym = {}
                    for g, (N_, D_, Dt_) in enumerate(((NR, DR, DRt), (NG, DG, DGt))):
                        i, b, fr = B.take()
                        t1 = mms([(b[:, h * P:(h + 1) * P], N_[:, h * P:(h + 1) * P], D_[:, h * P:(h + 1) * P],
                                   True, True) for h in range(4)], fr, tD[g])
                        y_ = get()
                        t2 = tt(v4(y_), v4(b[:, :]), lv(k, 0), ALU.mult, t1)
                        B.release(i, t2)
                        ym[g] = (y_, t2)
                    for g, (N_, D_, Dt_) in enumerate(((NR, DR, DRt), (NG, DG, DGt))):
                        y_, t2 = ym[g]
                        i, b, fr = B.take()
                        t1 = mms([(b[:, h * P:(h + 1) * P], Dt_[:, h * P:(h + 1) * P], y_[:, h * P:(h + 1) * P],
                                   True, True) for h in range(4)], fr, t2)
                        if k < 5:
                            i_, b_, fr_ = B.take()
                            t1_ = mms([(b_[:, h * P:(h + 1) * P], y_[:, h * P:(h + 1) * P],
                                        Dt_[:, h * P:(h + 1) * P], True, True) for h in range(4)], fr_)
                            t1 = t1_
                        t3 = tt(D_, D_, b[:, :], ALU.subtract, t1)
                        B.release(i, t3)
                        if k < 5:
                            t3 = tt(Dt_, Dt_, b_[:, :], ALU.subtract)
                            B.release(i_, t3)
                        tD[g] = t3
                        put(y_)
                    yield
                put(DRt, DGt, NR, NG)
                X, WT = get(), get()
                i, b, fr = B.take()
                t1 = mms([(b[:, h * 64:(h + 1) * 64], RW[h][:, 384:512], VV[:, h * 64:(h + 1) * 64], True, True)
                          for h in range(4)], fr, marks())
                t2 = copy(X[:, 0:256], b[:, 0:256], t1)
                B.release(i, t2)
                t2 = stt(h64(X[:, 256:512], 4), h64(VV[:, 256:512], 4), -1.0, bcb, ALU.mult, ALU.mult)
                i, b, fr = B.take()
                t1 = mms([(b[hb(h), (h // 2) * P:(h // 2 + 1) * P], KB[:, h * 64:(h + 1) * 64],
                           (DR if h < 4 else DG)[:, (h % 4) * P:(h % 4 + 1) * P], True, True) for h in range(8)], fr)
                t2 = copy(WT, b[:, :], t1, eng="S")
                B.release(i, t2)
                put(KB)
                UN = UNs[j % 2]
                tm_ = marks()
                m0s = []
                for e_ in range(2):
                    rs = slice(64 * e_, 64 * e_ + 64)
                    M = Ms[mcur[0] % 4]
                    Mn = Ms[(mcur[0] + 1) % 4]
                    mcur[0] += 1
                    m0s.append(M)
                    bks = []
                    for par in range(2):
                        i, b, fr = B.take()
                        lst = []
                        for q in range(4):
                            h = 2 * q + par
                            TT_ = (DR if h < 4 else DG)[:, (h % 4) * P + 64 * e_:(h % 4) * P + 64 * e_ + 64]
                            o = b[rs, q * 64:(q + 1) * 64]
                            lst.append((o, TT_, X[:, h * 64:(h + 1) * 64], True, False))
                            lst.append((o, WT[hb(h), q * P + 64 * e_:q * P + 64 * e_ + 64],
                                        M[hb(h), q * 64:(q + 1) * 64], False, True))
                        t1 = mms(lst, fr, tm_)
                        t2 = copy(UN[rs, par * 256:(par + 1) * 256], b[rs, 0:256], t1, scale=-1.0,
                                  eng="SV"[par])
                        B.release(i, t2)
                        bks.append(t2)
                    tt(h64(Mn, 4), h64(M, 4), bc(DC[:, e_:8:2].unsqueeze(2), [P, 4, 64]), ALU.mult)
                    i, b, fr = B.take()
                    lst = []
                    for h in range(8):
                        o = b[hb(h), (h // 2) * 64:(h // 2) * 64 + 64]
                        un = UN[rs, (h % 2) * 256 + (h // 2) * 64:(h % 2) * 256 + (h // 2) * 64 + 64]
                        lst.append((o, K2[rs, h * 64:(h + 1) * 64], un, True, h >= 4))
                        if h < 4:
                            lst.append((o, K3[rs, h * 64:(h + 1) * 64], VV[rs, h * 64:(h + 1) * 64], False, True))
                    t1 = mms(lst, fr, bks)
                    tm_ = tt(Mn, Mn, b[:, 0:256], ALU.add, t1)
                    B.release(i, tm_)
                yield
                Y = get()
                for par in range(2):
                    i, b, fr = B.take()
                    lst = []
                    for q in range(4):
                        h = 2 * q + par
                        o = b[:, q * 64:(q + 1) * 64]
                        un = UN[:, par * 256 + q * 64:par * 256 + q * 64 + 64]
                        if h < 4:
                            lst.append((o, RW[h][:, 0:128], un, True, False))
                            lst.append((o, RW[h][:, 256:384], VV[:, h * 64:(h + 1) * 64], False, False))
                        else:
                            lst.append((o, PN[par][:, (q - 2) * 256:(q - 2) * 256 + 128], un, True, False))
                        for e_ in range(2):
                            if h < 4:
                                qs = f1v[hb(h), q, 0, 64 * e_:64 * e_ + 64]
                            else:
                                qs = F3[hb(h), 256 + (q - 2) * P + 64 * e_:256 + (q - 2) * P + 64 * e_ + 64]
                            lst.append((b[64 * e_:64 * e_ + 64, q * 64:(q + 1) * 64], qs,
                                        m0s[e_][hb(h), q * 64:(q + 1) * 64], False, e_ == 1))
                    t1 = mms(lst, fr)
                    yv = Y.rearrange("p (q r n) -> p q r n", q=4, r=2)[:, :, par, :]
                    t2 = copy(yv, b[:, 0:256].rearrange("p (q n) -> p q n", q=4), t1, eng="V")
                    B.release(i, t2)
                put(*RW, *PN, DR, DG, X, WT, K2, K3, F1, F3)
                tmp, tmp2 = get(), get()
                yr, yg = Y[:, 0:256], Y[:, 256:512]
                s1 = sml()
                s2 = sml()
                t = red(s1[:, 0:4], h64(yr, 4), ALU.add, t2)
                ts(s1[:, 0:4], s1[:, 0:4], 1.0 / 64, None, ALU.mult, None)
                tt(h64(yr, 4), h64(yr, 4), bc(s1[:, 0:4].unsqueeze(2), [P, 4, 64]), ALU.subtract)
                t = tt(tmp, Y, Y, ALU.mult)
                red(s2[:, 0:8], h64(tmp, 8), ALU.add)
                ts(s2[:, 0:4], s2[:, 0:4], 1.0 / 64, 64e-5, ALU.mult, ALU.add)
                t = ts(s2[:, 4:8], s2[:, 4:8], 1.0 / 64, 1e-6, ALU.mult, ALU.add)
                t = act(s2[:, 0:8], s2[:, 0:8], ACT.Sqrt, t)
                t = rec(s2[:, 0:8], s2[:, 0:8], t)
                t = act(tmp[:, 0:256], gz[:, j, 0:256], ACT.Sigmoid, t)
                tt(h64(Y, 8), h64(Y, 8), bc(s2[:, 0:8].unsqueeze(2), [P, 8, 64]), ALU.mult, t)
                tt(yr, yr, rows["gn_w"], ALU.mult)
                tt(yr, yr, rows["gn_b"], ALU.add)
                tt(h64(tmp2[:, 0:256], 4), h64(v_, 4), bc(bon[:, 0:4].unsqueeze(2), [P, 4, 64]), ALU.mult)
                tt(yr, yr, tmp2[:, 0:256], ALU.add)
                tt(mx[:, j, 512:768], yr, GG[:, 0:256], ALU.mult)
                tt(h64(yg, 4), h64(yg, 4), bc(rows["on"].unsqueeze(1), [P, 4, 64]), ALU.mult)
                tt(tmp[:, 0:256], tmp[:, 0:256], gz[:, j, 0:256], ALU.mult)
                tt(mx[:, j, 768:1024], yg, tmp[:, 0:256], ALU.mult)
                put(Y, tmp, tmp2, RK, VV, LW, GG)

            for j in range(4):
                for _ in rec_tile(j):
                    pass
            assert len(stock) == 24 + len(extra)

            barrier()
            debug(f"my{l}", mix[:, :])
            t = to_T(mx, None)
            for half in range(2):
                t2 = proj_T(("w_out_2", l), 0, 8, half * 512, 512, xTh, xTl, t,
                            lambda j, b, t, half=half: tt(xtm[:, j, half * 512:(half + 1) * 512],
                                                          xtm[:, j, half * 512:(half + 1) * 512], b[:, :],
                                                          ALU.add, t))
            debug(f"xb{l}", x_tm[:, :])
            barrier()
            t = rms_norm_T(colat[("ffn", l, 1)], marks())
            barrier()
            t = ffn(("ffn_w_gate_2", 2 * l + 1), ("ffn_w_up_2", 2 * l + 1), ("ffn_w_down_2", 2 * l + 1), t, fin2)

        for i in range(NT):
            t = SP.dma("out", dcount, lambda e, i=i: e.dma_start(out[0, i * P:(i + 1) * P, :], xtm[:, i, :]), marks())
        SP.ops.append((None, [t], None))
        if "dbg" in dcount:
            SP.ops.append((None, [("dbg", dcount["dbg"])], None))

        for q in ENG + (SP,):
            for fn, w, inc in q.ops:
                for s, v in w:
                    sem(s)
                if inc:
                    sem(inc[0])
        block = ctx.enter_context(nc.Block())

        def play(q):
            def body(e):
                seen = {}
                for fn, w, inc in q.ops:
                    need = {}
                    for s, v in w:
                        if v > seen.get(s, 0):
                            need[s] = max(need.get(s, 0), v)
                    for s, v in need.items():
                        e.wait_ge(sems[s], v)
                        seen[s] = v
                    if fn is not None:
                        ins = fn(e)
                        if inc:
                            ins.then_inc(sems[inc[0]], inc[1])
            return body

        block.tensor(play(PE))
        block.vector(play(V))
        block.scalar(play(S))
        block.gpsimd(play(G))
        block.sync(play(SP))


_INS = ['x', 'w_in', 'fox_b_f', 'mla_g_q', 'mla_g_kv', 'mla_w_uq', 'mla_w_ukv', 'swa_sinks', 'mix_g', 'w_o',
        'ln1_g', 'ln1_b', 'w_gate', 'w_up', 'w_down', 'ln2_g', 'ln2_b', 'ffn_norm_2', 'ffn_w_gate_2',
        'ffn_w_up_2', 'ffn_w_down_2', 'mix_norm_2', 'w_in_2', 'w_out_2', 'att_q_norm_2', 'att_k_norm_2',
        'rwkv_mu_2', 'rwkv_w0_2', 'rwkv_w_up_2', 'rwkv_a0_2', 'rwkv_a_up_2', 'rwkv_g_up_2', 'rwkv_k_k_2',
        'rwkv_k_a_2', 'rwkv_r_k_2', 'rwkv_gn_w_2', 'rwkv_gn_b_2', 'rwkv_v0_2', 'rwkv_v_down_2',
        'rwkv_v_up_2', 'gdn_conv_2', 'gdn_a_log_2', 'gdn_dt_bias_2', 'gdn_o_norm_2']
_DBG = []


def kernel(**inputs):
    import numpy as _np
    import concourse.bacc as _bacc
    from concourse import mybir as _mybir
    from concourse.bass_utils import run_bass_kernel_spmd as _run

    nc = _bacc.Bacc("TRN2", target_bir_lowering=False, num_devices=1)
    c1, c2 = make_consts()
    arrays, aps = {}, {}
    for name in _INS + ["c_one", "c_two"]:
        a = c1 if name == "c_one" else c2 if name == "c_two" else _np.ascontiguousarray(inputs[name])
        arrays[f"in_{name}_dram"] = a
        aps[name] = nc.dram_tensor(f"in_{name}_dram", a.shape, _mybir.dt.from_np(a.dtype), kind="ExternalInput").ap()
    out = nc.dram_tensor("out_0_dram", (1, T, D), F32, kind="ExternalOutput").ap()
    dbg = {n: nc.dram_tensor(f"dbg_{n}", (P, w), F32, kind="ExternalOutput").ap() for n, w in _DBG}
    build_program(nc, aps, out, dbg)
    r = _run(nc, [arrays], core_ids=[0])
    got = r.results[0]["out_0_dram"]
    if _DBG:
        return (got,) + tuple(r.results[0][f"dbg_{n}"] for n, _ in _DBG)
    return got
```

```python
from contextlib import ExitStack

import numpy as np

import concourse.bass as bass
from concourse import mybir

F32 = mybir.dt.float32
FR = mybir.dt.float32r
ALU = mybir.AluOpType
ACT = mybir.ActivationFunctionType
AX_X = mybir.AxisListType.X

P = 128
T = 512
NT = 4
D = 1024
DFF = 2816
NF = DFF // P
ALPHA = 4.0 ** 0.25
NEG = -1e30
SENT = -3e38
WCH = 1024
NRAW = 3
NHL = 3
AHEAD = NHL - 1

C_ID, C_U, C_ONE, C_CM = 0, 128, 256, 384
C_LT, C_PM, C_SM = 512, 640, 768
C_EXTRA = 896
C_AB = C_EXTRA
C_SWA = C_AB + 2
C_RP1 = C_SWA + 1024
N1 = C_RP1 + 128
C_RP2 = C_EXTRA
C_BI = C_RP2 + 256
C_BS = C_BI + 128
C_BR = C_BS + 128
C_IND = C_BR + 128
C_LV = C_IND + 2
N2 = C_LV + 12 * 128


def make_consts():
    i = np.arange(P)
    r, c = i[:, None], i[None, :]
    f = np.float32
    common = [(r == c).astype(f), (r <= c).astype(f), np.ones((P, P), f),
              np.where(c > r, f(NEG), f(0)), (r >= c).astype(f),
              np.where(r >= c, f(1e30), f(0)), (r < c).astype(f)]
    ab = np.zeros((P, 2), f)
    ab[[0, 64], 1] = 1
    ab[[1, 65], 0] = 1
    swa = []
    for h in range(4):
        dist = r + P - np.arange(2 * P)[None, :]
        slope = f(2.0 ** (-2.0 * (h + 1)))
        swa.append(np.where((dist >= 0) & (dist < P), -slope * dist.astype(f), f(NEG)).astype(f))

    def rope_tab(half):
        pos = np.arange(T, dtype=f)
        inv = (f(10000.0) ** (-np.arange(half, dtype=f) / f(half))).astype(f)
        ang = (pos[:, None] * inv[None, :]).astype(f)
        cs = np.stack([np.cos(ang), np.sin(ang)], 0).astype(f)
        return cs.reshape(2, NT, P, half).transpose(2, 0, 1, 3).reshape(P, -1)

    c1 = np.concatenate(common + [ab] + swa + [rope_tab(16)], 1)
    same = (r // 64) == (c // 64)
    lv = []
    for k in range(6):
        w = 1 << k
        m = ((r // (2 * w)) == (c // (2 * w))) & ((r // w) % 2 == 0) & ((c // w) % 2 == 1)
        lv.append(m.astype(f))
    for k in range(6):
        lv.append(lv[k].T.copy())
    ind = np.stack([(i < 64), (i >= 64)], 1).astype(f)
    c2 = np.concatenate(common + [rope_tab(32), (same & (r <= c)).astype(f), (same & (r < c)).astype(f),
                                  (same & (r > c)).astype(f), ind] + lv, 1)
    assert c1.shape[1] == N1 and c2.shape[1] == N2
    return np.ascontiguousarray(c1.astype(f)), np.ascontiguousarray(c2.astype(f))


def flat(x):
    if x is None:
        return []
    if isinstance(x, tuple) and len(x) == 2 and isinstance(x[1], int) and isinstance(x[0], str):
        return [x]
    out = []
    for y in x:
        out += flat(y)
    return out


class Queue:

    def __init__(self, name, chain):
        self.name, self.chain = name, chain
        self.ops, self.n, self.pend, self.base, self.own = [], 0, [], None, True

    def after(self, *toks):
        self.pend += flat(toks)

    def __call__(self, fn, *toks, inc=True):
        w = flat(toks) + self.pend
        self.pend = []
        own = self.n if self.base is None else self.base
        if self.chain and own and self.own:
            w.append((self.name, own))
        self.own = True
        if inc:
            self.n += 1
        self.ops.append((fn, w, (self.name, 1) if inc else None))
        return (self.name, self.n)

    def dma(self, sem, count, fn, *toks):
        self.ops.append((fn, flat(toks) + self.pend, (sem, 16)))
        self.pend = []
        count[sem] = count.get(sem, 0) + 16
        return (sem, count[sem])

    def mark(self):
        return (self.name, self.n)

    def loose(self):
        self.base = self.n

    def tight(self):
        self.base = None


class Slots:

    def __init__(self, bufs):
        self.bufs, self.free, self.held, self.at = bufs, [[] for _ in bufs], [False] * len(bufs), 0

    def take(self):
        assert not all(self.held), "slots held"
        while self.held[self.at % len(self.bufs)]:
            self.at += 1
        i = self.at % len(self.bufs)
        self.at += 1
        self.held[i] = True
        return i, self.bufs[i], self.free[i]

    def release(self, i, *toks):
        self.held[i] = False
        self.free[i] = flat(toks)


def weight_order(A):
    out = []

    def one(name, l, r0, nk, c0, n):
        M = A[name]
        M = M[l // 2, l % 2] if len(M.shape) == 4 else M[l]
        out.append(((name, l, r0, nk, c0, n), M))

    def f(name, l, c0, n):
        for s in range(n // P):
            one(name, l, 0, 8, c0 + s * P, P)

    def t(name, l, r0, K, c0, n):
        kk = max(1, WCH // n)
        for k0 in range(0, K, kk):
            one(name, l, r0 + k0 * P, min(kk, K - k0), c0, n)

    def ffn(g, u, d, l):
        for grp in range(2):
            for i in range(11):
                f(g, l, (11 * grp + i) * P, P)
                f(u, l, (11 * grp + i) * P, P)
            for half in range(2):
                t(d, l, 11 * grp * P, 11, half * 512, 512)

    for l in range(2):
        w = "w_in"
        f(w, l, 0, 512)
        t(w, l, 0, 8, 512, 260)
        f(w, l, 1188, 512)
        t(w, l, 0, 8, 1700, 256)
        f(w, l, 772, 384)
        t(w, l, 0, 8, 1156, 32)
        f(w, l, 1956, 384)
        t(w, l, 0, 8, 2340, 128)
        for half in range(2):
            t("w_o", l, 0, 8, half * 512, 512)
        ffn("w_gate", "w_up", "w_down", l)
    for l in range(2):
        ffn("ffn_w_gate_2", "ffn_w_up_2", "ffn_w_down_2", 2 * l)
        w = "w_in_2"
        for c0, n in ((0, 512), (512, 256), (768, 512), (1280, 72)):
            t(w, l, 0, 8, c0, n)
        t(w, l, 0, 8, 3016, 264)
        f(w, l, 1352, 896)
        f(w, l, 2248, 768)
        for half in range(2):
            t("w_out_2", l, 0, 8, half * 512, 512)
        ffn("ffn_w_gate_2", "ffn_w_up_2", "ffn_w_down_2", 2 * l + 1)
    return out


def build_program(nc, A, out, dbg):
    ctx = ExitStack()
    with ctx:
        sems = {}

        def sem(name):
            if name not in sems:
                sems[name] = ctx.enter_context(nc.semaphore(name))
            return sems[name]

        def sb(name, n, dt=F32):
            return ctx.enter_context(nc.sbuf_tensor(name, [P, n], dt))

        def sb2(*pair):
            with nc.sbuf_tensor(pair[0][0], [P, pair[0][1]], pair[0][2]) as a:
                pass
            b = ctx.enter_context(nc.sbuf_tensor(pair[1][0], [P, pair[1][1]], pair[1][2]))
            assert pair[1][1] >= pair[0][1]
            return a, b

        dcount = {}
        PE, V, S, G, SP = (Queue(n, c) for n, c in
                           (("pe", False), ("dve", True), ("act", True), ("pool", True), ("sp", False)))
        ENG = (PE, V, S, G)
        x_tm = sb("x_tm", 4096)
        mix = sb("mix", 4096)
        con = sb("con", max(N1, N2))
        cols = sb("cols", 256)
        small = sb("small", 64 * 16)
        wraw = [sb(f"wraw{i}", WCH) for i in range(NRAW)]
        whl = [(sb(f"wh{i}", WCH, FR), sb(f"wl{i}", WCH, FR)) for i in range(NHL)]
        vfirst = sb("vfirst", 1024)
        pbuf = sb("pbuf", 2304)
        scr = [sb(f"scr{i}", 512) for i in range(8)]
        prm = [sb(f"prm{i}", D) for i in range(2)]
        x_T, spare = sb2(("x_T", 8192, FR), ("spare", 8192, F32))
        AR = 13700
        h_T, arena = sb2(("h_T", 11 * 2 * T, FR), ("arena", AR, F32))
        psum = [ctx.enter_context(nc.psum_tensor(f"ps{i}", [P, 512], F32)) for i in range(8)]
        RAW = Slots(wraw)
        HL = Slots(whl)
        PR = Slots(prm)
        B = Slots(psum)
        R = Slots(scr)
        sm_at = [0]

        xtm = x_tm[:, :].rearrange("p (t d) -> p t d", t=NT)
        xTs = x_T[:, :].rearrange("p (c k t) -> p c k t", c=2, k=8)
        xTh, xTl = xTs[:, 0], xTs[:, 1]
        hTs = h_T[:, :].rearrange("p (c f t) -> p c f t", c=2, f=11)
        hTh, hTl = hTs[:, 0], hTs[:, 1]
        mx = mix[:, :].rearrange("p (t d) -> p t d", t=NT)
        ident = con[:, C_ID:C_ID + P]
        uu = con[:, C_U:C_U + P]
        ones = con[:, C_ONE:C_ONE + P]
        cmask = con[:, C_CM:C_CM + P]
        ltm = con[:, C_LT:C_LT + P]
        pmask = con[:, C_PM:C_PM + P]
        smask = con[:, C_SM:C_SM + P]

        def sml():
            sm_at[0] += 1
            o = (sm_at[0] % 64) * 16
            return small[:, o:o + 16]

        def marks():
            return [q.mark() for q in ENG if q.n]

        def loosen(on=True):
            for q in (V, S):
                q.loose() if on else q.tight()

        def barrier():
            m = marks()
            for q in ENG:
                q.after(m)
            return m

        ar_at = [0]

        def take(n, view=None, at=None, **kw):
            if at is not None:
                ar_at[0] = at
            o = ar_at[0]
            ar_at[0] += n
            assert ar_at[0] <= AR, ar_at[0]
            v = arena[:, o:o + n]
            return v.rearrange(view, **kw) if view else v

        def rget(n, src, view=None):
            i, buf, free = PR.take()
            dst = buf[:, 0:n]
            if view:
                dst = dst.rearrange("p (k n) -> p k n", k=view)
            return i, dst, SP.dma(f"p{i}", dcount, lambda e: e.dma_start(dst, src), free)

        weights = weight_order(A)
        staged = []

        def stage(M, r0, nk, c0, n):
            src = M[r0:r0 + nk * P, c0:c0 + n].rearrange("(k p) n -> p k n", p=P)
            ri, raw, rfree = RAW.take()
            raw = raw[:, 0:nk * n].rearrange("p (k n) -> p k n", k=nk)
            tr = SP.dma(f"w{ri}", dcount, lambda e: e.dma_start(raw, src), rfree)
            i, (wh, wl), free = HL.take()
            wh = wh[:, 0:nk * n].rearrange("p (k n) -> p k n", k=nk)
            wl = wl[:, 0:nk * n].rearrange("p (k n) -> p k n", k=nk)
            t = S(lambda e: e.activation(wh, raw, ACT.Copy), tr, free)
            t = G(lambda e: e.tensor_tensor(wl, raw, wh.bitcast(F32), ALU.subtract), t)
            RAW.release(ri, t)
            staged.append((i, (wh, wl), t))

        wat = [0]

        def wmat(name, l, r0, nk, c0, n):
            assert weights[wat[0]][0] == (name, l, r0, nk, c0, n), (weights[wat[0]][0], (name, l, r0, nk, c0, n))
            wat[0] += 1
            while len(staged) < min(wat[0] + AHEAD, len(weights)):
                nm, M = weights[len(staged)]
                stage(M, *nm[2:])
            return staged[wat[0] - 1]

        def mms(lst, *toks):
            t = None
            for n, (o, l, r, st, sp) in enumerate(lst):
                t = PE(lambda e, o=o, l=l, r=r, st=st, sp=sp: e.matmul(o, l, r, start=st, stop=sp,
                                                                      skip_group_check=True),
                       *(toks if n == 0 else ()), inc=(n == len(lst) - 1))
            return t

        def trs(lst, *toks):
            t = None
            for n, (o, x) in enumerate(lst):
                k = x.shape[0]
                b = x.base_partition() if callable(x.base_partition) else x.base_partition
                t = PE(lambda e, o=o, x=x, k=k: e.transpose(o, x, ident[0:k, 0:k]),
                       *(toks if n == 0 else ()), inc=(n == len(lst) - 1))
            return t

        alt = [0]

        def copy(dst, src, *toks, scale=None, eng=None):
            if eng is None:
                alt[0] += 1
                eng = "S" if alt[0] % 2 else "V"
            if eng == "S":
                if scale is None:
                    return S(lambda e: e.activation(dst, src, ACT.Copy), *toks)
                return S(lambda e: e.activation(dst, src, ACT.Copy, scale=scale), *toks)
            if scale is None:
                return V(lambda e: e.tensor_copy(dst, src), *toks)
            return V(lambda e: e.tensor_scalar(dst, src, scale, None, ALU.mult), *toks)

        def tt(dst, a, b, op, *toks):
            return V(lambda e: e.tensor_tensor(dst, a, b, op), *toks)

        def ttf(dst, a, b, op, *toks):
            V.own = False
            return tt(dst, a, b, op, *toks)

        def ts(dst, a, s1, s2, o1, o2, *toks):
            if s2 is None:
                return V(lambda e: e.tensor_scalar(dst, a, s1, None, o1), *toks)
            return V(lambda e: e.tensor_scalar(dst, a, s1, s2, o1, o2), *toks)

        def stt(dst, a, s, b, o1, o2, *toks):
            return V(lambda e: e.scalar_tensor_tensor(out=dst, in0=a, scalar=s, in1=b, op0=o1, op1=o2), *toks)

        def act(dst, src, f, *toks, **kw):
            return S(lambda e: e.activation(dst, src, f, **kw), *toks)

        def red(dst, src, op, *toks, **kw):
            return V(lambda e: e.tensor_reduce(dst, src, AX_X, op, **kw), *toks)

        def rec(dst, src, *toks):
            return V(lambda e: e.reciprocal(dst, src), *toks)

        def vcopy(dst, src, *toks):
            return V(lambda e: e.tensor_copy(dst, src), *toks)

        def memset(dst, v, *toks):
            return V(lambda e: e.memset(dst, v), *toks)

        def rstd(dst, ssq, scale, eps, *toks):
            t = ts(dst, ssq, scale, eps, ALU.mult, ALU.add, *toks)
            t = act(dst, dst, ACT.Sqrt, t)
            return rec(dst, dst, t)

        def bc(ap, shape):
            return ap.broadcast_to(shape)

        def dma_small(batch, dst, src, *toks):
            return S.dma(batch, dcount, lambda e: e.dma_start(dst, src, allow_slow_non_contiguous=True), *toks)

        colat = {}
        coln = [0]
        tcol = None

        def load_cols(name, src, k):
            nonlocal tcol
            o = coln[0]
            coln[0] += k
            assert coln[0] <= 248
            colat[name] = cols[:, o:o + k]
            tcol = dma_small("cols", cols[:, o:o + k], src.rearrange("(k p) -> p k", p=P))

        tcon = S.dma("con", dcount, lambda e: e.dma_start(con[:, 0:N1], A["c_one"]))
        tx = None
        for i in range(NT):
            tx = SP.dma("xin", dcount, lambda e, i=i: e.dma_start(xtm[:, i, :], A["x"][0, i * P:(i + 1) * P, :]))
        for l in range(2):
            load_cols(("gq", l), A["mla_g_q"][l], 2)
            load_cols(("gkv", l), A["mla_g_kv"][l], 1)
            load_cols(("mixg", l), A["mix_g"][l], 8)
            load_cols(("mixn", l), A["mix_norm_2"][l], 8)
            for j in range(2):
                load_cols(("ffn", l, j), A["ffn_norm_2"][l, j], 8)
            load_cols(("mu", l), A["rwkv_mu_2"][l], 7)
            for w in range(4):
                load_cols(("conv", l, w), A["gdn_conv_2"][l, w], 6)

        pb_at = [0]

        def load_row(batch, src, n, *toks):
            o = pb_at[0]
            pb_at[0] += n
            dst = pbuf[:, o:o + n]
            t = dma_small(batch, dst, src.unsqueeze(0).broadcast_to([P, n]), *toks)
            return dst, t

        def split(h, lo, src, *toks, scale=None):
            t = copy(h, src, *toks, scale=scale, eng="S")
            if scale is None:
                return tt(lo, src, h.bitcast(F32), ALU.subtract, t)
            return stt(lo, src, scale, h.bitcast(F32), ALU.mult, ALU.subtract, t)

        def to_T(src, scale_col, *toks):
            last = []
            for j in range(NT):
                for c in range(2):
                    i, b, fr = B.take()
                    t = trs([(b[:, q * P:(q + 1) * P], src[:, j, (4 * c + q) * P:(4 * c + q + 1) * P])
                             for q in range(4)], fr, toks[j])
                    v4_ = b[:, :].rearrange("p (q n) -> p q n", q=4)
                    oh = xTh[:, 4 * c:4 * c + 4, j * P:(j + 1) * P]
                    ol = xTl[:, 4 * c:4 * c + 4, j * P:(j + 1) * P]
                    if scale_col is None:
                        t = split(oh, ol, v4_, t)
                        B.release(i, t)
                    else:
                        ri, rb, rf = R.take()
                        r4 = rb[:, :].rearrange("p (q n) -> p q n", q=4)
                        t = tt(r4, v4_, bc(scale_col[:, 4 * c:4 * c + 4].unsqueeze(2), [P, 4, P]), ALU.mult,
                               t, rf, tcol)
                        B.release(i, t)
                        t = split(oh, ol, r4, t)
                        R.release(ri, t)
                    last.append(t)
            return last

        def proj_F(M, c0, rd):
            wi, (wh, wl), tw = wmat(*M, 0, 8, c0, P)
            i, b, fr = B.take()
            lst = []
            for k in range(8):
                lst += [(b[:, :], wh[:, k, :], xTh[:, k, :], k == 0, False),
                        (b[:, :], wh[:, k, :], xTl[:, k, :], False, False),
                        (b[:, :], wl[:, k, :], xTh[:, k, :], False, k == 7)]
            t = mms(lst, fr, tw, rd)
            HL.release(wi, t)
            return i, b, t

        def proj_T(M, r0, K, c0, n, lh, ll, rd, finish):
            bks = [B.take() for _ in range(NT)]
            kk = max(1, WCH // n)
            for k0 in range(0, K, kk):
                nk = min(kk, K - k0)
                wi, (wh, wl), tw = wmat(*M, r0 + k0 * P, nk, c0, n)
                lst = []
                for q in range(nk):
                    k = k0 + q
                    for j in range(NT):
                        o = bks[j][1][:, 0:n]
                        xh, xl = lh[:, k, j * P:(j + 1) * P], ll[:, k, j * P:(j + 1) * P]
                        lst += [(o, xh, wh[:, q, :], k == 0, False), (o, xh, wl[:, q, :], False, False),
                                (o, xl, wh[:, q, :], False, k == K - 1)]
                t = mms(lst, tw, rd, [b[2] for b in bks] if k0 == 0 else None)
                HL.release(wi, t)
            last = []
            for j in range(NT):
                tf = finish(j, bks[j][1], t)
                B.release(bks[j][0], tf)
                last.append(tf)
            return last

        def proj_s(w, tw, n, tile, rd, K, src):
            i, b, fr = B.take()
            t = mms([(b[:, 0:n], src[:, k, tile * P:(tile + 1) * P], w[:, k, 0:n], k == 0, k == K - 1)
                     for k in range(K)], fr, tw, rd)
            return i, b, t

        def rms_norm_T(gcol, *toks):
            loosen()
            ss, rr = sml(), sml()
            done = []
            for i in range(NT):
                t = act(mx[:, i, :], xtm[:, i, :], ACT.Square, *toks, accum_out=ss[:, i:i + 1])
                t = rstd(rr[:, i:i + 1], ss[:, i:i + 1], 1.0 / D, 1e-6, t)
                done.append(ts(mx[:, i, :], xtm[:, i, :], rr[:, i:i + 1], None, ALU.mult, None, t))
            t = to_T(mx, gcol, *done)
            loosen(False)
            return t

        def layer_norm(gsrc, bsrc, *toks):
            gi, gw, tg = rget(D, gsrc.unsqueeze(0).broadcast_to([P, D]))
            bi, bw, tb = rget(D, bsrc.unsqueeze(0).broadcast_to([P, D]))
            loosen()
            done = []
            for i in range(NT):
                s, mv, rr = sml(), sml(), sml()
                for j in range(2):
                    t = V(lambda e, s=s, i=i, j=j: e.bn_stats(s[:, 6 * j:6 * j + 6],
                                                              xtm[:, i, j * 512:(j + 1) * 512]), *toks)
                t = V(lambda e, s=s, mv=mv: e.bn_aggr(mv[:, 0:2], s[:, 0:12]), t)
                t = rstd(rr[:, 0:1], mv[:, 1:2], 1.0, 1e-5, t)
                t = ts(xtm[:, i, :], xtm[:, i, :], mv[:, 0:1], rr[:, 0:1], ALU.subtract, ALU.mult, t)
                t = tt(xtm[:, i, :], xtm[:, i, :], gw, ALU.mult, tg, t)
                t = G(lambda e, i=i, bw=bw: e.tensor_tensor(xtm[:, i, :], xtm[:, i, :], bw, ALU.add), tb, t)
                done.append(t)
            PR.release(gi, done)
            PR.release(bi, done)
            loosen(False)
            return done

        def ffn(Wg, Wu, Wd, rd, finish):
            last = None
            loosen()
            for grp in range(2):
                th = None
                for f in range(11):
                    c0 = (11 * grp + f) * P
                    bi, bg, t1 = proj_F(Wg, c0, rd)
                    bj, bu, t2 = proj_F(Wu, c0, rd)
                    ri, sg, rf = R.take()
                    t = act(sg[:, :], bg[:, :], ACT.Sigmoid, t1, rf)
                    t = tt(sg[:, :], sg[:, :], bg[:, :], ALU.mult, t)
                    B.release(bi, t)
                    t = tt(sg[:, :], sg[:, :], bu[:, :], ALU.mult, t, t2)
                    B.release(bj, t)
                    th = split(hTh[:, f, :], hTl[:, f, :], sg[:, :], t)
                    R.release(ri, th)
                for half in range(2):
                    last = proj_T(Wd, 11 * grp * P, 11, half * 512, 512, hTh, hTl, [th, last],
                                  lambda j, b, t, half=half, grp=grp: finish(j, half, grp, b, t))
            loosen(False)
            return last

        def run(gens, depth):
            live = []
            gens = list(gens)
            loosen()
            while gens or live:
                if gens:
                    live.append(gens.pop(0))
                for g in list(live):
                    try:
                        next(g)
                    except StopIteration:
                        live.remove(g)
            loosen(False)

        def softmax_unit(tile, nk, qk, vs, dst, *toks, mask=None, sink=None, eng=None):
            bi, b, fr = B.take()
            t = mms([(b[:, c0:c1], l, r, n == 0, n == len(qk) - 1) for n, (c0, c1, l, r) in enumerate(qk)], fr, *toks)
            yield
            m = sml()
            pi, pbf, pf = R.take()
            if mask is not None:
                t = tt(pbf[:, 0:nk], b[:, 0:nk], mask, ALU.add, t, pf)
                B.release(bi, t)
                t = red(m[:, 0:1], pbf[:, 0:nk], ALU.max, t, negate=True)
                src = pbf
            else:
                src = b
                if sink is not None:
                    t = red(m[:, 2:3], b[:, 0:nk], ALU.max, t)
                    t = ts(m[:, 0:1], m[:, 2:3], sink, -1.0, ALU.max, ALU.mult, t)
                else:
                    t = red(m[:, 0:1], b[:, 0:nk], ALU.max, t, negate=True)
            te = act(pbf[:, 0:nk], src[:, 0:nk], ACT.Exp, t, pf, bias=m[:, 0:1], accum_out=m[:, 1:2])
            if mask is None:
                B.release(bi, te)
            if sink is not None:
                t = act(m[:, 3:4], sink, ACT.Exp, te, bias=m[:, 0:1])
            else:
                t = te
            yield
            if sink is not None:
                t = tt(m[:, 1:2], m[:, 1:2], m[:, 3:4], ALU.add, t)
            tr = rec(m[:, 4:5], m[:, 1:2], t)
            nb = nk // P
            ti, tb, tf = B.take()
            t = trs([(tb[:, j * P:(j + 1) * P], pbf[:, j * P:(j + 1) * P]) for j in range(nb)], tf, te)
            R.release(pi, t)
            qi, qb, qf = R.take()
            t = copy(qb[:, 0:nk], tb[:, 0:nk], t, qf, eng=eng)
            B.release(ti, t)
            yield
            oi, ob, of = B.take()
            t = mms([(ob[:, 0:64], qb[:, j * P:(j + 1) * P], vs[j], j == 0, j == nb - 1) for j in range(nb)], of, t)
            R.release(qi, t)
            t = ts(dst, ob[:, 0:64], m[:, 4:5], None, ALU.mult, None, t, tr)
            B.release(oi, t)

        def hb(h):
            return slice((h % 2) * 64, (h % 2) * 64 + 64)

        def debug(name, ap, *toks):
            if name in dbg:
                d = dbg[name]
                S.dma("dbg", dcount, lambda e: e.dma_start(d, ap), marks())
                for q in ENG:
                    q.after(("dbg", dcount["dbg"]))

        tx_in = [tx]
        t = to_T(xtm, None, *[[tx, tcon]] * 4)
        for l in range(2):
            barrier()
            ar_at[0] = 0
            pb_at[0] = 0
            win = ("w_in", l)
            bn = f"pb1{l}"
            fb, tp = load_row(bn, A["fox_b_f"][l], 4, marks())
            snk, tp = load_row(bn, A["swa_sinks"][l], 4)
            fq = take(2 * T, "p (k t) -> p k t", k=2)
            fk = take(2 * T, "p (k t) -> p k t", k=2)
            fv = take(4 * 260, "p (t n) -> p t n", t=4)

            def load_F(c0, n, dst, scale=None):
                for s in range(n // P):
                    i, b, t = proj_F(win, c0 + s * P, None)
                    B.release(i, copy(dst[:, s, :], b[:, :], t, scale=scale))

            def load_T(c0, n, dst):
                proj_T(win, 0, 8, c0, n, xTh, xTl, None,
                       lambda j, b, t: copy(dst[:, j, 0:n], b[:, 0:n], t))

            load_F(0, 256, fq, 0.125)
            load_F(256, 256, fk)
            load_T(512, 260, fv)
            sq = take(2 * T, "p (k t) -> p k t", k=2)
            sk = take(2 * T, "p (k t) -> p k t", k=2)
            sv = take(4 * 256, "p (t n) -> p t n", t=4)
            g1 = sml()
            g2 = sml()
            g3 = sml()
            tf_ = marks()
            load_F(1188, 256, sq, 0.125)
            load_F(1444, 256, sk)

            def v44(x):
                return x.rearrange("p (t h) -> p t h", t=4)

            t = tt(v44(g1), fv[:, :, 256:260], bc(fb.unsqueeze(1), [P, 4, 4]), ALU.add, tf_, tp)
            t = ts(g2, g1, -1.0, None, ALU.mult, None)
            t = tt(g2, g2, g1, ALU.max)
            t = act(g2, g2, ACT.Exp, t, scale=-1.0)
            t = act(g2, g2, ACT.Ln, t, bias=1.0)
            t = ts(g1, g1, 0.0, None, ALU.min, None, t)
            t = tt(g3, g1, g2, ALU.subtract)
            AQ = take(2 * T, "p (a t) -> p a t", a=2)
            AK = take(2 * T, "p (a t) -> p a t", a=2)
            zat = ar_at[0]
            LQ = take(4 * 2 * 128, "p (t a c) -> p t a c", t=4, a=2)
            LK = take(4 * 2 * 128, "p (t a c) -> p t a c", t=4, a=2)
            zbuf = [take(1280, at=zat + 2560 * n) for n in range(2)]
            spbuf = [take(1280, at=zat + 2560 * n + 1280) for n in range(2)]
            ZS, SS = Slots(zbuf), Slots(spbuf)
            memset(LQ, 0.0)
            memset(LK, 0.0)
            for a in range(2):
                for q in range(2):
                    src = v44(g3)[:, :, 2 * a + q:2 * a + q + 1]
                    vcopy(LQ[:, :, a, 64 * q:64 * q + 1], src)
                    t = ts(LK[:, :, a, 64 * q + 1:64 * q + 2], src, -1.0, None, ALU.mult, None)
            for L_, O_, cc in ((LQ, AQ, 0), (LK, AK, 1)):
                for a in range(2):
                    i, b, fr = B.take()
                    t2 = mms([(b[:, tb * P:(tb + 1) * P], L_[:, jt, a, :], uu if jt == tb else ones,
                               jt == 0, jt == tb) for tb in range(4) for jt in range(tb + 1)], fr, t)
                    t3 = act(O_[:, a, :], b[:, :], ACT.Identity, t2, bias=con[:, C_AB + cc:C_AB + cc + 1])
                    B.release(i, t3)
            load_T(1700, 256, sv)
            t = marks()

            def fox_unit(h, i):
                a, nk = h // 2, (i + 1) * P
                qk = [(0, nk, fq[hb(h), a, i * P:nk], fk[hb(h), a, 0:nk]),
                      (0, nk, AQ[hb(h), a, i * P:nk], AK[hb(h), a, 0:nk]),
                      (i * P, nk, ident, cmask)]
                return softmax_unit(i, nk, qk, [fv[:, j, h * 64:h * 64 + 64] for j in range(i + 1)],
                                    mx[:, i, h * 64:h * 64 + 64], t)

            def blk(s, c):
                if s == c:
                    return s * P
                return {0: 512, 2: 896, 1: 1024}[s] + (c - s - 1) * P

            def stick_unit(h):
                a = h // 2
                zi, z, zf = ZS.take()
                si, sp, sf = SS.take()
                tz = []
                parts = [(0, [(s, s, s + 1) for s in range(4)]), (512, [(0, 1, 4), (2, 3, 4)]), (1024, [(1, 2, 4)])]
                for base, ents in parts:
                    bi, b, fr = B.take()
                    wdt = sum((c1 - c0) * P for _, c0, c1 in ents)
                    t1 = mms([(b[:, blk(s, c0) - base:blk(s, c0) - base + (c1 - c0) * P], sk[hb(h), a, s * P:(s + 1) * P],
                               sq[hb(h), a, c0 * P:c1 * P], True, True) for s, c0, c1 in ents], fr, t)
                    t2 = copy(z[:, base:base + wdt], b[:, 0:wdt], t1, zf)
                    B.release(bi, t2)
                    tz.append(t2)
                yield
                t1 = act(sp[:, :], z[:, :], ACT.Abs, tz, sf)
                t1 = act(sp[:, :], sp[:, :], ACT.Exp, t1, scale=-1.0)
                t1 = act(sp[:, :], sp[:, :], ACT.Ln, t1, bias=1.0)
                t1 = stt(sp[:, :], z[:, :], 0.0, sp[:, :], ALU.max, ALU.add, t1)
                sd = sp[:, 0:512].rearrange("p (s c) -> p s c", s=4)
                tsp = tt(sd, sd, bc(smask.unsqueeze(1), [P, 4, P]), ALU.mult, t1)
                yield
                te = []
                for base, ents in parts:
                    bi, b, fr = B.take()
                    lst = []
                    for s, c0, c1 in ents:
                        for c in range(c0, c1):
                            o = b[:, blk(s, c) - base:blk(s, c) - base + P]
                            if s == c:
                                lst.append((o, ident, pmask, True, False))
                            for j in range(s, c + 1):
                                lst.append((o, ltm if j == s else ones, sp[:, blk(j, c):blk(j, c) + P],
                                            s != c and j == s, j == c))
                    wdt = sum((c1 - c0) * P for _, c0, c1 in ents)
                    t1 = mms(lst, fr, tsp)
                    t2 = tt(z[:, base:base + wdt], z[:, base:base + wdt], b[:, 0:wdt], ALU.subtract, t1)
                    B.release(bi, t2)
                    te.append(t2)
                SS.release(si, t1)
                te = act(z[:, :], z[:, :], ACT.Exp, te)
                yield
                bi, b, fr = B.take()
                t1 = mms([(b[:, c * 64:c * 64 + 64], z[:, blk(s, c):blk(s, c) + P], sv[:, s, h * 64:h * 64 + 64],
                           s == 0, s == c) for c in range(4) for s in range(c + 1)], fr, te)
                ZS.release(zi, t1)
                t2 = copy(mx[:, :, 512 + h * 64:512 + h * 64 + 64], b[:, 0:256].rearrange("p (c d) -> p c d", c=4), t1)
                B.release(bi, t2)
            run([u for h in range(4)
                 for u in [fox_unit(h, 0), stick_unit(h)] + [fox_unit(h, i) for i in (1, 2, 3)]], 4)

            barrier()
            ar_at[0] = 0
            cqg = take(2 * T, "p (k t) -> p k t", k=2)
            ckg = take(T, "p (k t) -> p k t", k=1)
            sq_at = ar_at[0]
            wk = take(2 * T, "p (k t) -> p k t", k=2)
            wv = take(4 * 128, "p (t n) -> p t n", t=4)
            sq2 = take(3 * T, "p (k t) -> p k t", at=sq_at, k=3)
            kr = take(4 * 32, "p (t n) -> p t n", t=4)
            qtm = take(4 * 384, "p (t n) -> p t n", t=4)
            ktm = take(4 * 384, "p (t n) -> p t n", t=4)
            vtm = take(4 * 256, "p (t n) -> p t n", t=4)
            qTh = take(4 * T, "p (h t) -> p h t", h=4)
            kTh = take(4 * T, "p (h t) -> p h t", h=4)
            rt = take(4 * 64, "p (a n) -> p a n", a=4)
            wq = take(2 * T, "p (k t) -> p k t", k=2)
            gq, gkv = colat[("gq", l)], colat[("gkv", l)]
            for s in range(3):
                i, b, t = proj_F(win, 772 + s * P, None)
                t2 = act(sq2[:, s, :], b[:, :], ACT.Square, t)
                if s < 2:
                    t3 = ts(cqg[:, s, :], b[:, :], gq[:, s:s + 1], None, ALU.mult, None, t2, tcol)
                else:
                    t3 = ts(ckg[:, 0, :], b[:, :], gkv[:, 0:1], None, ALU.mult, None, t2)
                B.release(i, t3)
            load_T(1156, 32, kr)
            i, b, fr = B.take()
            t = mms([(b[:, 8 * k + j:8 * k + j + 1], sq2[:, s, j * P:(j + 1) * P], ones[:, 0:1], s in (0, 2), s in (1, 2))
                     for j in range(NT) for k, s in ((0, 0), (0, 1), (1, 2))], fr, marks())
            rq, rk = sml(), sml()
            t = ts(rq[:, 0:4], b[:, 0:4], 1.0 / 256, 1e-6, ALU.mult, ALU.add, t)
            t = ts(rk[:, 0:4], b[:, 8:12], 1.0 / 128, 1e-6, ALU.mult, ALU.add)
            B.release(i, t)
            act(rq[:, 0:4], rq[:, 0:4], ACT.Sqrt, t)
            t = act(rk[:, 0:4], rk[:, 0:4], ACT.Sqrt)
            rec(rq[:, 0:4], rq[:, 0:4], t)
            rec(rk[:, 0:4], rk[:, 0:4])
            t = ts(rq[:, 0:4], rq[:, 0:4], 96.0 ** -0.5, None, ALU.mult, None)
            wi, wuq, twq = rget(768, A["mla_w_uq"][l].rearrange("(k p) n -> p k n", p=P), view=2)
            wj, wukv, twk = rget(512, A["mla_w_ukv"][l].rearrange("(k p) n -> p k n", p=P), view=1)
            for j in range(NT):
                i, b, t1 = proj_s(wuq, twq, 384, j, t, 2, cqg)
                t2 = ts(qtm[:, j, :], b[:, 0:384], rq[:, j:j + 1], None, ALU.mult, None, t1)
                B.release(i, t2)
                i, b, t1 = proj_s(wukv, twk, 512, j, t, 1, ckg)
                bv = b[:, :].rearrange("p (h a d) -> p h a d", h=4, a=2)
                kv_ = ktm[:, j, :].rearrange("p (h d) -> p h d", h=4)
                t2 = ts(kv_[:, :, 0:64], bv[:, :, 0, :], rk[:, j:j + 1], None, ALU.mult, None, t1)
                t2 = ts(vtm[:, j, :].rearrange("p (h d) -> p h d", h=4), bv[:, :, 1, :], rk[:, j:j + 1],
                        None, ALU.mult, None)
                B.release(i, t2)
            PR.release(wi, t1)
            PR.release(wj, t1)
            cosb = con[:, C_RP1:C_RP1 + 64].rearrange("p (t n) -> p t n", t=4)
            sinb = con[:, C_RP1 + 64:C_RP1 + 128].rearrange("p (t n) -> p t n", t=4)

            def rope(x1, x2, cs, sn, tmp, shape):
                a, b_, c_, d_ = tmp
                tt(a, x1, cs, ALU.mult, marks())
                tt(b_, x2, sn, ALU.mult)
                tt(c_, x1, sn, ALU.mult)
                tt(d_, x2, cs, ALU.mult)
                tt(x1, a, b_, ALU.subtract)
                return tt(x2, c_, d_, ALU.add)

            for j in range(NT):
                q4 = qtm[:, j, :].rearrange("p (h d) -> p h d", h=4)
                tm = [rt[:, a, 0:64].rearrange("p (h d) -> p h d", h=4) for a in range(4)]
                rope(q4[:, :, 64:80], q4[:, :, 80:96], bc(cosb[:, j, :].unsqueeze(1), [P, 4, 16]),
                     bc(sinb[:, j, :].unsqueeze(1), [P, 4, 16]), tm, None)
            tm = [rt[:, a, 0:64].rearrange("p (h d) -> p h d", h=4) for a in range(4)]
            rope(kr[:, :, 0:16], kr[:, :, 16:32], cosb, sinb, tm, None)
            for j in range(NT):
                t = vcopy(ktm[:, j, :].rearrange("p (h d) -> p h d", h=4)[:, :, 64:96],
                          bc(kr[:, j, :].unsqueeze(1), [P, 4, 32]))
            tr_ = t
            load_F(1956, 256, wq, 0.125)
            i, b, t = proj_F(win, 2212, None)
            for g in range(2):
                for q in range(2):
                    t2 = copy(wk[64 * q:64 * q + 64, g, :], b[64 * g:64 * g + 64, :], t, eng="S")
            B.release(i, t2)
            load_T(2340, 128, wv)
            t = tr_
            for h in range(4):
                for src, dst in ((qtm, qTh), (ktm, kTh)):
                    i, b, fr = B.take()
                    t1 = trs([(b[0:96, j * P:(j + 1) * P], src[:, j, h * 96:h * 96 + 96]) for j in range(NT)], fr, t)
                    t2 = copy(dst[0:96, h, :], b[0:96, :], t1)
                    B.release(i, t2)
            t = marks()

            def mla_unit(h, i):
                nk = (i + 1) * P
                qk = [(0, nk, qTh[0:96, h, i * P:nk], kTh[0:96, h, 0:nk]), (i * P, nk, ident, cmask)]
                return softmax_unit(i, nk, qk, [vtm[:, j, h * 64:h * 64 + 64] for j in range(i + 1)],
                                    mx[:, i, 256 + h * 64:256 + h * 64 + 64], t)

            def swa_unit(h, i):
                a, g = h // 2, h // 2
                j0 = max(i - 1, 0)
                nk = (i + 1 - j0) * P
                so = C_SWA + 256 * h
                qk = [(0, nk, wq[hb(h), a, i * P:(i + 1) * P], wk[hb(h), g, j0 * P:(i + 1) * P]),
                      (0, nk, ident, con[:, so + 256 - nk:so + 256])]
                return softmax_unit(i, nk, qk, [wv[:, j, g * 64:g * 64 + 64] for j in range(j0, i + 1)],
                                    mx[:, i, 768 + h * 64:768 + h * 64 + 64], t, tp, sink=snk[:, h:h + 1])
            run([u for h in range(4) for i in range(4) for u in (mla_unit(h, i), swa_unit(h, i))], 4)


            barrier()
            debug(f"mix{l}", mix[:, :])
            ss = sml()
            ri, rb, rf = R.take()
            for i in range(NT):
                for g in range(4):
                    t = act(rb[:, 0:256], mx[:, i, g * 256:(g + 1) * 256], ACT.Square, rf,
                            accum_out=ss[:, 4 * i + g:4 * i + g + 1])
            R.release(ri, t)
            rr, done = sml(), []
            t = rstd(rr, ss, 1.0 / 256, 1e-6, t)
            for i in range(NT):
                m4 = mx[:, i, :].rearrange("p (g d) -> p g d", g=4)
                done.append(tt(m4, m4, bc(rr[:, 4 * i:4 * i + 4].unsqueeze(2), [P, 4, 256]), ALU.mult, t))
            t = to_T(mx, colat[("mixg", l)], *done)

            def add_y(j, half, b, t):
                xs = xtm[:, j, half * 512:(half + 1) * 512]
                return stt(xs, xs, ALPHA, b[:, :], ALU.mult, ALU.add, t)
            for half in range(2):
                t2 = proj_T(("w_o", l), 0, 8, half * 512, 512, xTh, xTl, t,
                            lambda j, b, t, half=half: add_y(j, half, b, t))
            t = layer_norm(A["ln1_g"][l], A["ln1_b"][l], t2)
            debug(f"x1{l}", x_tm[:, :])
            t = to_T(xtm, None, *t)

            def fin1(i, half, grp, b, t):
                xs = xtm[:, i, half * 512:(half + 1) * 512]
                return stt(xs, xs, 1.0 if grp else ALPHA, b[:, :], ALU.mult, ALU.add, t)
            barrier()
            t = ffn(("w_gate", l), ("w_up", l), ("w_down", l), t, fin1)
            t = layer_norm(A["ln2_g"][l], A["ln2_b"][l], t)
            debug(f"x2{l}", x_tm[:, :])
            if l == 0:
                t = to_T(xtm, None, *t)

        def fin2(i, half, grp, b, t):
            xs = xtm[:, i, half * 512:(half + 1) * 512]
            return stt(xs, b[:, :], 0.5, xs, ALU.mult, ALU.add, t)

        m = barrier()
        t = S.dma("con2", dcount, lambda e: e.dma_start(con[:, 0:N2], A["c_two"]), m)
        for q in ENG:
            q.after(t)
        rope_c = con[:, C_RP2:C_RP2 + 128].rearrange("p (t n) -> p t n", t=4)
        rope_s = con[:, C_RP2 + 128:C_RP2 + 256].rearrange("p (t n) -> p t n", t=4)
        m_bi = con[:, C_BI:C_BI + P]
        m_bs = con[:, C_BS:C_BS + P]
        m_br = con[:, C_BR:C_BR + P]
        m_bibs = con[:, C_BI:C_BI + 256]
        ind = con[:, C_IND:C_IND + 2]
        small8 = cols[:, 248:256]
        vf3 = vfirst[:, :].rearrange("p (t n) -> p t n", t=4)

        def h64(ap, n):
            return ap.rearrange("p (h d) -> p h d", h=n)

        for l in range(2):
            barrier()
            pb_at[0] = 0
            bn = f"pb2{l}"
            mk = marks()
            rows = {}
            for nm, src, n in ([(k, A[f"rwkv_{k}_2"][l], 256) for k in ("w0", "a0", "k_k", "k_a")] +
                               [("r_k", A["rwkv_r_k_2"][l].rearrange("h d -> (h d)"), 256),
                                ("gn_w", A["rwkv_gn_w_2"][l], 256), ("gn_b", A["rwkv_gn_b_2"][l], 256)] +
                               ([("v0", A["rwkv_v0_2"][0], 256)] if l else []) +
                               [("qn", A["att_q_norm_2"][l], 64), ("kn", A["att_k_norm_2"][l], 64),
                                ("on", A["gdn_o_norm_2"][l], 64), ("al", A["gdn_a_log_2"][l], 4),
                                ("dt", A["gdn_dt_bias_2"][l], 4)]):
                rows[nm], tp = load_row(bn, src, n, mk)
            t = rms_norm_T(colat[("ffn", l, 0)], marks())
            barrier()
            t = ffn(("ffn_w_gate_2", 2 * l + 0), ("ffn_w_up_2", 2 * l + 0), ("ffn_w_down_2", 2 * l + 0), t, fin2)
            debug(f"xa{l}", x_tm[:, :])
            t = rms_norm_T(colat[("mixn", l)], marks())
            win = ("w_in_2", l)

            barrier()
            ar_at[0] = 0
            pa = take(4 * 1352, "p (t n) -> p t n", t=4)
            hbT = take(7 * T, "p (a t) -> p a t", at=0, a=7)
            gT = take(6 * T, "p (a t) -> p a t", a=6)
            rec_at = ar_at[0]
            qT = mx[:, :, 512:1024]
            qiT = take(4 * T, "p (a t) -> p a t", a=4)
            vv = take(4 * 128, "p (t n) -> p t n", t=4)
            wiv = take(4 * 8, "p (t n) -> p t n", t=4)
            kd = take(2 * T, "p (a t) -> p a t", a=2)
            kid = take(T)
            msk = take(3 * 512, "p (a n) -> p a n", a=3)

            def load_T2(c0, n, dst, o2):
                proj_T(win, 0, 8, c0, n, xTh, xTl, None,
                       lambda j, b, t: copy(dst[:, j, o2:o2 + n], b[:, 0:n], t))

            def rotate(j, c0, nh):
                xx = h64(pa[:, j, c0:c0 + nh * 64], nh)
                tk = [R.take() for _ in range(4)]
                V.after([x[2] for x in tk])
                tm = [x[1][:, 0:nh * 32].rearrange("p (h d) -> p h d", h=nh) for x in tk]
                t = rope(xx[:, :, 0:32], xx[:, :, 32:64], bc(rope_c[:, j, :].unsqueeze(1), [P, nh, 32]),
                         bc(rope_s[:, j, :].unsqueeze(1), [P, nh, 32]), tm, None)
                for x in tk:
                    R.release(x[0], t)
                return t

            load_T2(0, 512, pa, 0)
            load_T2(512, 256, pa, 512)
            rr2 = take(4 * 16, "p (t n) -> p t n", t=4)
            rec_end = ar_at[0]
            gz = take(4 * 264, "p (t n) -> p t n", t=4)
            t = marks()
            for j in range(NT):
                ri, rb, rf = R.take()
                rj, rc_, rf2 = R.take()
                t = act(rb[:, :], pa[:, j, 0:512], ACT.Square, t, rf)
                t = act(rc_[:, 0:128], pa[:, j, 512:640], ACT.Square, rf2)
                t = red(rr2[:, j, 0:8], h64(rb[:, :], 8), ALU.add, t)
                t = red(rr2[:, j, 8:10], h64(rc_[:, 0:128], 2), ALU.add, t)
                R.release(ri, t)
                R.release(rj, t)
            t = rstd(rr2[:, :, 0:10], rr2[:, :, 0:10], 1.0 / 64, 1e-6, t)
            ts(rr2[:, :, 0:8], rr2[:, :, 0:8], 0.125, None, ALU.mult, None, t)
            for j in range(NT):
                x10 = h64(pa[:, j, 0:640], 10)
                tt(x10, x10, bc(rr2[:, j, 0:10].unsqueeze(2), [P, 10, 64]), ALU.mult)
                tt(x10[:, 0:8, :], x10[:, 0:8, :], bc(rows["qn"].unsqueeze(1), [P, 8, 64]), ALU.mult, tp)
                tt(x10[:, 8:10, :], x10[:, 8:10, :], bc(rows["kn"].unsqueeze(1), [P, 2, 64]), ALU.mult)
                rotate(j, 0, 10)
                t = vcopy(vv[:, j, :], pa[:, j, 640:768])
            load_T2(768, 512, pa, 768)
            load_T2(1280, 72, pa, 1280)
            tq = marks()
            load_T2(3016, 264, gz, 0)
            for j in range(NT):
                V.after(tq)
                rotate(j, 768, 9)
                t = ts(wiv[:, j, :], pa[:, j, 1344:1352], 8 ** -0.5 * 64 ** -0.5, None, ALU.mult, None)
            for a in range(4):
                for dst, c0 in ((qT, 0), (qiT, 768)):
                    i, b, fr = B.take()
                    t1 = trs([(b[:, j * P:(j + 1) * P], pa[:, j, c0 + a * P:c0 + (a + 1) * P]) for j in range(NT)], fr, t)
                    t2 = copy(dst[:, a, :], b[:, :], t1)
                    B.release(i, t2)
            i, b, fr = B.take()
            t1 = trs([(b[:, j * P:(j + 1) * P], pa[:, j, 512:640]) for j in range(NT)], fr, t)
            for g in range(2):
                for q in range(2):
                    t2 = copy(kd[64 * q:64 * q + 64, g, :], b[64 * g:64 * g + 64, :], t1, eng="S")
            B.release(i, t2)
            i, b, fr = B.take()
            t1 = trs([(b[0:64, j * P:(j + 1) * P], pa[:, j, 1280:1344]) for j in range(NT)], fr, t)
            for q in range(2):
                t2 = copy(kid[64 * q:64 * q + 64, :], b[0:64, :], t1, eng="S")
            B.release(i, t2)
            t = marks()

            def project():
                for s in range(7):
                    i, b, t1 = proj_F(win, 1352 + s * P, None)
                    x = hbT[:, s, :]
                    t1 = copy(x, b[:, :], t1, t)
                    B.release(i, t1)
                    yield
                    ri, rb, rf = R.take()
                    t2 = tt(rb[:, 1:512], x[:, 0:511], x[:, 1:512], ALU.subtract, rf, t1)
                    t3 = ts(rb[:, 0:1], x[:, 0:1], -1.0, None, ALU.mult, None, rf, t1)
                    R.release(ri, stt(x, rb[:, :], mu[:, s:s + 1], x, ALU.mult, ALU.add, t2, t3))
                for s in range(6):
                    i, b, t1 = proj_F(win, 2248 + s * P, None)
                    x = gT[:, s, :]
                    t1 = copy(x, b[:, :], t1, t)
                    B.release(i, t1)
                    yield
                    ri, rb, rf = R.take()
                    t2 = memset(rb[:, 0:1], 0.0, rf)
                    t3 = ts(rb[:, 1:512], x[:, 0:511], cv[2][:, s:s + 1], None, ALU.mult, None, rf, t1)
                    for w in (2, 3):
                        t3 = stt(rb[:, w:512], x[:, 0:512 - w], cv[3 - w][:, s:s + 1], rb[:, w:512],
                                 ALU.mult, ALU.add, t3)
                    R.release(ri, stt(x, x, cv[3][:, s:s + 1], rb[:, :], ALU.mult, ALU.add, t2, t3))

            masks = {0: None}

            def pick():
                for i in (3, 2, 1):
                    nk = (i + 1) * P
                    acc = msk[:, i - 1, 0:nk]
                    ta = None
                    for h in range(8):
                        bi, b, fr = B.take()
                        t1 = mms([(b[:, 0:nk], qiT[hb(h), h // 2, i * P:nk], kid[hb(h), 0:nk], True, True)], fr, t)
                        ri, rb, rf = R.take()
                        t1 = act(rb[:, 0:nk], b[:, 0:nk], ACT.Relu, t1, rf)
                        B.release(bi, t1)
                        if h == 0:
                            ta = ts(acc, rb[:, 0:nk], wiv[:, i, h:h + 1], None, ALU.mult, None, t1)
                        else:
                            ta = stt(acc, rb[:, 0:nk], wiv[:, i, h:h + 1], acc, ALU.mult, ALU.add, t1, ta)
                        R.release(ri, ta)
                        yield
                    ta = tt(msk[:, i - 1, i * P:nk], msk[:, i - 1, i * P:nk], cmask, ALU.add, ta)
                    m8 = small8
                    for _ in range(16):
                        ta = V(lambda e, a=acc: e.max(m8, a), ta)
                        ta = V(lambda e, a=acc: e.match_replace(a, m8, a, SENT), ta)
                        yield
                    ta = ts(acc, acc, SENT, 1.0, ALU.is_equal, ALU.subtract, ta)
                    masks[i] = ts(acc, acc, 1e30, None, ALU.mult, None, ta)
                    yield

            def dsa_unit(h, i):
                nk = (i + 1) * P
                qk = [(0, nk, qT[hb(h), h // 2, i * P:nk], kd[hb(h), h // 4, 0:nk])]
                mask = None
                if i == 0:
                    qk.append((0, P, ident, cmask))
                else:
                    mask = msk[:, i - 1, 0:nk]
                g = h // 4
                return softmax_unit(i, nk, qk, [vv[:, j, g * 64:g * 64 + 64] for j in range(i + 1)],
                                    mx[:, i, h * 64:h * 64 + 64], t, masks[i], mask=mask, eng="S")

            mu = colat[("mu", l)]
            cv = [colat[("conv", l, w)] for w in range(4)]
            loosen()
            V.after(tcol)
            todo = [(h, i) for i in (0, 3, 2, 1) for h in range(8)]
            live, rnd, picking, projecting = [], 0, pick(), project()
            while todo or live or picking or projecting:
                for g in list(live):
                    if next(g, "end") == "end":
                        live.remove(g)
                if todo and len(live) < 4 and todo[0][1] in masks:
                    live.append(dsa_unit(*todo.pop(0)))
                    next(live[-1])
                if picking and next(picking, "end") == "end":
                    picking = None
                if projecting and rnd % 6 == 0 and next(projecting, "end") == "end":
                    projecting = None
                rnd += 1
            loosen(False)

            barrier()
            lora = take(256, at=rec_at)
            vdn = take(64, "p (k n) -> p k n", k=2)
            vup = take(256)
            gate = take(64, "p (a t h) -> p a t h", a=4, t=4)
            vz = take(512)
            UNs = [take(512) for _ in range(2)]
            Ms = [take(256) for _ in range(4)]
            extra = [take(512) for _ in range((rec_end - ar_at[0]) // 512)]
            mk = marks()
            ln_ = f"lora{l}"
            dma_small(ln_, lora[0:32, :], A["rwkv_w_up_2"][l], mk)
            dma_small(ln_, lora[32:64, :], A["rwkv_a_up_2"][l])
            tl = dma_small(ln_, lora[64:128, :], A["rwkv_g_up_2"][l])
            if l:
                dma_small(ln_, vdn, A["rwkv_v_down_2"][0].rearrange("(k p) n -> p k n", p=P))
                tl = dma_small(ln_, vup[0:32, :], A["rwkv_v_up_2"][0])
            barrier()
            t = act(hbT[0:32, 6, :], hbT[0:32, 6, :], ACT.Tanh)
            t = act(hbT[64:128, 6, :], hbT[64:128, 6, :], ACT.Sigmoid)
            for s in range(6):
                ri, rb, rf = R.take()
                t = act(rb[:, :], gT[:, s, :], ACT.Sigmoid, rf)
                R.release(ri, tt(gT[:, s, :], gT[:, s, :], rb[:, :], ALU.mult, t))
            rz, sgz, fz = zip(*[R.take() for _ in range(2)])
            for q in range(2):
                zq = gz[:, 2 * q:2 * q + 2, 0:256]
                sq_ = sgz[q][:, :].rearrange("p (t n) -> p t n", t=2)
                t = act(sq_, zq, ACT.Sigmoid, t, fz[q])
                t = tt(zq, zq, sq_, ALU.mult, t)
                R.release(rz[q], t)
            ga, gb_, gg, gt = (gate[:, a] for a in range(4))
            t = act(gb_, gz[:, :, 256:260], ACT.Sigmoid, t)
            t = tt(ga, gz[:, :, 260:264], bc(rows["dt"].unsqueeze(1), [P, 4, 4]), ALU.add, tp)
            ts(gt, ga, -1.0, None, ALU.mult, None)
            t = tt(gt, gt, ga, ALU.max)
            t = act(gt, gt, ACT.Exp, t, scale=-1.0)
            t = act(gt, gt, ACT.Ln, t, bias=1.0)
            t = stt(gt, ga, 0.0, gt, ALU.max, ALU.add, t)
            al = sml()
            t = act(al[:, 0:4], rows["al"], ACT.Exp, t)
            t = tt(gg, gt, bc(al[:, 0:4].unsqueeze(1), [P, 4, 4]), ALU.mult, t)
            t = ts(gg, gg, -1.0, None, ALU.mult, None)
            if l:
                i, b, fr = B.take()
                t1 = mms([(b[0:32, :], vdn[:, k, :], hbT[:, 4 + k, :], k == 0, k == 1) for k in range(2)],
                         fr, tl, marks())
                t2 = copy(vz[0:32, :], b[0:32, :], t1)
                B.release(i, t2)
            barrier()
            for u_ in UNs:
                memset(u_, 0.0)
            memset(Ms[0], 0.0)

            stock = [(x, []) for x in [spare[:, i * 512:(i + 1) * 512] for i in range(16)] + extra]
            for _ in range(8):
                stock.append((R.bufs[_][:, :], []))
            for n, w_ in enumerate(prm):
                stock += [(w_[:, 0:512], []), (w_[:, 512:1024], [])]
            for n, w_ in enumerate(wraw):
                stock += [(w_[:, 0:512], RAW.free[n]), (w_[:, 512:1024], RAW.free[n])]

            def get():
                buf, fr = stock.pop(0)
                V.after(fr)
                S.after(fr)
                G.after(fr)
                return buf

            def put(*bufs):
                m = marks()
                for b_ in bufs:
                    stock.append((b_, m))

            def vs():
                return [V.mark(), S.mark()]

            def gp(dst, a, b, op, *toks):
                return G(lambda e: e.tensor_tensor(dst, a, b, op), *toks)

            mcur = [0]
            mdone = [None]

            def rec_tile(j):
                js = slice(j * P, (j + 1) * P)
                RK, VV, QK = get(), get(), get()
                for dst, srcs in ((RK, [hbT[:, a, js] for a in range(4)]),
                                  (VV, [hbT[:, 4, js], hbT[:, 5, js], gT[:, 4, js], gT[:, 5, js]]),
                                  (QK, [gT[:, a, js] for a in range(4)])):
                    i, b, fr = B.take()
                    t1 = trs([(b[:, n * P:(n + 1) * P], s) for n, s in enumerate(srcs)], fr)
                    t2 = copy(dst, b[:, :], t1)
                    B.release(i, t2)
                LW, UA = get(), get()
                i1, b1, f1 = B.take()
                i2, b2, f2 = B.take()
                i3, b3, f3 = B.take()
                t1 = mms([(b1[:, 0:256], hbT[0:32, 6, js], lora[0:32, :], True, True)] +
                         ([(b1[:, 256:512], vz[0:32, js], vup[0:32, :], True, True)] if l else []), f1, tl)
                t2 = mms([(b2[:, 0:256], hbT[32:64, 6, js], lora[32:64, :], True, True)], f2)
                t3 = mms([(b3[:, 0:256], hbT[64:128, 6, js], lora[64:128, :], True, True)], f3)
                tt(LW[:, 0:256], b1[:, 0:256], rows["w0"], ALU.add, t1)
                if l:
                    tt(UA[:, 256:512], b1[:, 256:512], rows["v0"], ALU.add)
                t = tt(UA[:, 0:256], b2[:, 0:256], rows["a0"], ALU.add, t2)
                B.release(i1, t)
                B.release(i2, t)
                K3 = get()
                GG = K3[:, 256:512]
                t = copy(GG, b3[:, 0:256], t3, t)
                B.release(i3, t)
                yield
                t = act(LW[:, 0:256], LW[:, 0:256], ACT.Sigmoid, vs())
                w_ = 512 if l else 256
                t = act(UA[:, 0:w_], UA[:, 0:w_], ACT.Sigmoid)
                t = ts(LW[:, 0:256], LW[:, 0:256], -float(np.exp(-0.5)), None, ALU.mult, None, t)
                t = vcopy(h64(LW[:, 256:512], 4), bc(gg[:, j, :].unsqueeze(2), [P, 4, 64]))
                r_, k_, v_ = RK[:, 0:256], RK[:, 256:512], VV[:, 0:256]
                a_ = UA[:, 0:256]
                yield
                KB, BK = get(), get()
                kk = KB[:, 0:256]
                tmp = get()
                tt(kk, k_, rows["k_k"], ALU.mult, tp)
                tt(tmp[:, 0:256], kk, kk, ALU.mult)
                nn = sml()
                t = red(nn[:, 0:4], h64(tmp[:, 0:256], 4), ALU.add)
                t = act(tmp, QK, ACT.Square, t)
                t = red(nn[:, 4:12], h64(tmp, 8), ALU.add, t)
                ts(nn[:, 0:4], nn[:, 0:4], 1e-12, None, ALU.add, None)
                t = ts(nn[:, 4:12], nn[:, 4:12], 1e-6, None, ALU.add, None)
                t = rec(nn[:, 0:12], nn[:, 0:12])
                t = act(nn[:, 0:12], nn[:, 0:12], ACT.Sqrt, t)
                t = ts(nn[:, 4:8], nn[:, 4:8], 0.125, None, ALU.mult, None, t)
                tt(h64(kk, 4), h64(kk, 4), bc(nn[:, 0:4].unsqueeze(2), [P, 4, 64]), ALU.mult)
                tt(h64(QK, 8), h64(QK, 8), bc(nn[:, 4:12].unsqueeze(2), [P, 8, 64]), ALU.mult)
                yield
                tt(BK[:, 0:256], kk, a_, ALU.mult)
                copy(BK[:, 256:512], QK[:, 256:512], V.mark(), eng="S")
                bcb = bc(gb_[:, j, :].unsqueeze(2), [P, 4, 64])
                tt(h64(KB[:, 256:512], 4), h64(QK[:, 256:512], 4), bcb, ALU.mult)
                yield
                stt(tmp[:, 0:256], a_, 1.0, rows["k_a"], ALU.subtract, ALU.mult)
                stt(k_, tmp[:, 0:256], 1.0, k_, ALU.add, ALU.mult)
                if l:
                    tt(tmp[:, 0:256], vf3[:, j, :], v_, ALU.subtract)
                    tt(tmp[:, 0:256], tmp[:, 0:256], UA[:, 256:512], ALU.mult)
                    tt(v_, v_, tmp[:, 0:256], ALU.add)
                else:
                    vcopy(vf3[:, j, :], v_)
                bon = sml()
                gp(tmp[:, 0:256], r_, k_, ALU.mult, vs())
                tg = gp(tmp[:, 0:256], tmp[:, 0:256], rows["r_k"], ALU.mult, tp)
                put(UA)
                i1, b1, f1 = B.take()
                i2, b2, f2 = B.take()
                i3, b3, f3 = B.take()
                t1 = mms([(b1[:, :], m_bi, LW, True, True)], f1, vs())
                t2 = mms([(b2[:, :], m_br, LW, True, True)], f2)
                t3 = mms([(b3[:, 0:256], m_bs, LW[:, 0:256], True, True)] +
                         [(b3[:, 256 + 2 * p:258 + 2 * p], LW[:, p * P:(p + 1) * P], ind, True, True)
                          for p in range(4)], f3)
                E1, E3X, E4 = get(), get(), get()
                E3, EX = E3X[:, 0:256], E3X[:, 256:512]
                DC, gcs = sml(), sml()
                act(E1, b1[:, :], ACT.Exp, t1)
                act(E3, b1[:, 0:256], ACT.Exp, scale=-1.0)
                t = act(E4, b2[:, :], ACT.Exp, t2)
                B.release(i2, t)
                act(EX, b3[:, 0:256], ACT.Exp, t3)
                t = act(DC[:, 0:8], b3[:, 256:264], ACT.Exp)
                B.release(i3, t)
                t = vcopy(gcs[:, 0:4], b1[:, 256:512:64], t)
                B.release(i1, t)
                put(LW)
                yield
                Qh, K2, BT = get(), get(), get()
                yield
                t0 = V.mark()
                ttf(Qh[:, 0:256], r_, E1[:, 0:256], ALU.mult, t0)
                ttf(Qh[:, 256:512], QK[:, 0:256], E1[:, 256:512], ALU.mult, t0)
                red(bon[:, 0:4], h64(tmp[:, 0:256], 4), ALU.add, tg)
                put(tmp)
                gp(BT[:, 0:256], BK[:, 0:256], E3, ALU.mult, vs())
                tbt = gp(BT[:, 256:512], k_, E3, ALU.mult)
                gp(K2, BK, E4, ALU.mult)
                tk = gp(K3[:, 0:256], k_, E4[:, 0:256], ALU.mult)
                F4 = get()
                f4v = F4.rearrange("p (a c n) -> p a c n", a=2, c=2)
                F3 = get()
                i, b, fr = B.take()
                t = trs([(b[:, (2 * a + 0) * P:(2 * a + 1) * P], QK[:, a * P:(a + 1) * P]) for a in range(2)] +
                        [(b[:, (2 * a + 1) * P:(2 * a + 2) * P], KB[:, 256 + a * P:384 + a * P]) for a in range(2)],
                        fr, vs())
                t2 = copy(F4, b[:, :], t)
                B.release(i, t2)
                tt(KB[:, 0:256], KB[:, 0:256], EX, ALU.mult)
                t = tt(KB[:, 256:512], KB[:, 256:512], E1[:, 256:512], ALU.mult, t)
                put(E1, E3X, E4, BK, RK)
                yield
                i, b, fr = B.take()
                t = trs([(b[:, a * P:(a + 1) * P], QK[:, 256 + a * P:384 + a * P]) for a in range(2)] +
                        [(b[:, (2 + a) * P:(3 + a) * P], Qh[:, 256 + a * P:384 + a * P]) for a in range(2)],
                        fr, t)
                t2 = copy(F3, b[:, :], t)
                B.release(i, t2)
                yield
                F1, F2 = get(), get()
                f1v = F1.rearrange("p (a c n) -> p a c n", a=2, c=2)
                i, b, fr = B.take()
                t = trs([(b[:, (2 * a) * P:(2 * a + 1) * P], Qh[:, a * P:(a + 1) * P]) for a in range(2)] +
                        [(b[:, (2 * a + 1) * P:(2 * a + 2) * P], KB[:, a * P:(a + 1) * P]) for a in range(2)],
                        fr, vs())
                t2 = copy(F1, b[:, :], t)
                B.release(i, t2)
                i, b, fr = B.take()
                t = trs([(b[:, a * P:(a + 1) * P], BT[:, a * P:(a + 1) * P]) for a in range(4)], fr, tbt)
                t2 = copy(F2, b[:, :], t)
                B.release(i, t2)
                put(QK, BT, Qh)
                tn = vs()
                yield
                i, b, fr = B.take()
                t = mms([(b[:, h * P:(h + 1) * P], bc(gg[:, j, h:h + 1], [P, P]), m_bi, True, True)
                         for h in range(4)], fr)
                DT, DN = get(), get()
                for h in range(4):
                    hs = slice(h * P, (h + 1) * P)
                    t1 = ts(DT[:, hs], b[:, hs], gcs[:, h:h + 1], 0.0, ALU.subtract, ALU.min, t)
                    t2 = ts(DN[:, hs], b[:, hs], gcs[:, h:h + 1], 0.0, ALU.subtract, ALU.max)
                B.release(i, t2)
                act(DT, DT, ACT.Exp, t2)
                t = act(DN, DN, ACT.Exp, scale=-1.0)
                yield
                RW = [get() for _ in range(4)]
                for h in range(4):
                    if h == 2:
                        yield
                    i, b, fr = B.take()
                    fa = F1.rearrange("p (a n) -> p a n", a=2)[hb(h), h // 2, :]
                    p_ = h // 2
                    t1 = mms([(b[:, 0:256], F2[hb(h), p_ * P:(p_ + 1) * P], fa, True, True),
                              (b[:, 256:512], F2[hb(h), 256 + p_ * P:384 + p_ * P], fa, True, True)], fr, tn)
                    t2 = ttf(RW[h].rearrange("p (a n) -> p a n", a=2), b[:, :].rearrange("p (a n) -> p a n", a=2),
                             bc(m_bibs.unsqueeze(1), [P, 2, 256]), ALU.mult, t1)
                    B.release(i, t2)
                yield
                NR, NG = get(), get()
                for par in range(2):
                    i, b, fr = B.take()
                    t1 = mms([(b[:, q * P:(q + 1) * P], f1v[64 * par:64 * par + 64, q, 1, :],
                               F2[64 * par:64 * par + 64, q * P:(q + 1) * P], True, True) for q in range(2)] +
                             [(b[:, (2 + q) * P:(3 + q) * P], f4v[64 * par:64 * par + 64, q, 1, :],
                               F3[64 * par:64 * par + 64, q * P:(q + 1) * P], True, True) for q in range(2)], fr)
                    nv = NR.rearrange("p (q r n) -> p q r n", q=2, r=2)[:, :, par, :]
                    gv = NG.rearrange("p (q r n) -> p q r n", q=2, r=2)[:, :, par, :]
                    mb = bc(m_br.unsqueeze(1), [P, 2, P])
                    tt(nv, b[:, 0:256].rearrange("p (q n) -> p q n", q=2), mb, ALU.mult, t1)
                    t2 = tt(gv, b[:, 256:512].rearrange("p (q n) -> p q n", q=2), mb, ALU.mult)
                    B.release(i, t2)
                tt(NG, NG, DN, ALU.mult, t)
                yield
                PN = [get(), get()]
                for par in range(2):
                    i, b, fr = B.take()
                    t1 = mms([(b[:, q * 256:(q + 1) * 256], F3[64 * par:64 * par + 64, q * P:(q + 1) * P],
                               F4.rearrange("p (a n) -> p a n", a=2)[64 * par:64 * par + 64, q, :], True, True)
                              for q in range(2)], fr)
                    pv = PN[par].rearrange("p (q c n) -> p q c n", q=2, c=2)
                    t2 = tt(PN[par].rearrange("p (q n) -> p q n", q=2), b[:, :].rearrange("p (q n) -> p q n", q=2),
                            bc(m_bibs.unsqueeze(1), [P, 2, 256]), ALU.mult, t1)
                    B.release(i, t2)
                    dv = DT.rearrange("p (q r n) -> p q r n", q=2, r=2)[:, :, par, :]
                    for c in range(2):
                        tt(pv[:, :, c, :], pv[:, :, c, :], dv, ALU.mult)
                put(DT, DN, F4, F2)
                yield

                def lv(k, tr):
                    o = C_LV + (k + 6 * tr) * P
                    return bc(con[:, o:o + P].unsqueeze(1), [P, 4, P])

                def v4(ap):
                    return ap.rearrange("p (h n) -> p h n", h=4)
                DR, DRt, DG, DGt = get(), get(), get(), get()
                idb = bc(ident.unsqueeze(1), [P, 4, P])
                t0 = V.mark()
                for h in range(4):
                    hs = slice(h * P, (h + 1) * P)
                    ttf(DR[:, hs], RW[h][:, 128:256], con[:, C_LV:C_LV + P], ALU.mult, t0)
                    ttf(DG[:, hs], PN[h % 2][:, (h // 2) * 256 + 128:(h // 2) * 256 + 256],
                        con[:, C_LV:C_LV + P], ALU.mult, t0)
                ttf(v4(DRt), v4(NR), lv(0, 1), ALU.mult, t0)
                t0 = ttf(v4(DGt), v4(NG), lv(0, 1), ALU.mult, t0)
                for x in (DR, DG, DRt, DGt):
                    t = ttf(v4(x), idb, v4(x), ALU.subtract, t0)
                tD, tDt = {0: t, 1: t}, {0: t, 1: t}
                both = ((NR, DR, DRt), (NG, DG, DGt))
                yield True
                for k in range(1, 6):
                    ym = {}
                    for g, (N_, D_, Dt_) in enumerate(both):
                        i, b, fr = B.take()
                        t1 = mms([(b[:, h * P:(h + 1) * P], N_[:, h * P:(h + 1) * P], D_[:, h * P:(h + 1) * P],
                                   True, True) for h in range(4)], fr, tD[g])
                        y_ = get()
                        t2 = ttf(v4(y_), v4(b[:, :]), lv(k, 0), ALU.mult, t1)
                        B.release(i, t2)
                        ym[g] = (y_, t2)
                    yield
                    for g, (N_, D_, Dt_) in enumerate(both):
                        y_, t2 = ym[g]
                        i, b, fr = B.take()
                        t1 = mms([(b[:, h * P:(h + 1) * P], Dt_[:, h * P:(h + 1) * P], y_[:, h * P:(h + 1) * P],
                                   True, True) for h in range(4)], fr, t2, tDt[g])
                        tD[g] = ttf(D_, D_, b[:, :], ALU.subtract, t1, tD[g])
                        B.release(i, tD[g])
                        if k < 5:
                            i, b, fr = B.take()
                            t1 = mms([(b[:, h * P:(h + 1) * P], y_[:, h * P:(h + 1) * P],
                                       Dt_[:, h * P:(h + 1) * P], True, True) for h in range(4)], fr)
                            tDt[g] = ttf(Dt_, Dt_, b[:, :], ALU.subtract, t1, tDt[g])
                            B.release(i, tDt[g])
                        put(y_)
                        yield
                put(DRt, DGt, NR, NG)
                X, WT = get(), get()
                i, b, fr = B.take()
                t1 = mms([(b[:, h * 64:(h + 1) * 64], RW[h][:, 384:512], VV[:, h * 64:(h + 1) * 64], True, True)
                          for h in range(4)], fr, tD[0], tD[1], tn)
                t2 = copy(X[:, 0:256], b[:, 0:256], t1)
                B.release(i, t2)
                t2 = stt(h64(X[:, 256:512], 4), h64(VV[:, 256:512], 4), -1.0, bcb, ALU.mult, ALU.mult)
                i, b, fr = B.take()
                t1 = mms([(b[hb(h), (h // 2) * P:(h // 2 + 1) * P], KB[:, h * 64:(h + 1) * 64],
                           (DR if h < 4 else DG)[:, (h % 4) * P:(h % 4 + 1) * P], True, True) for h in range(8)], fr)
                t2 = copy(WT, b[:, :], t1, eng="S")
                B.release(i, t2)
                put(KB)
                UN = UNs[j % 2]
                m0s = []
                ub = []
                for par in range(2):
                    i, b, fr = B.take()
                    mms([(b[:, q * 64:(q + 1) * 64],
                          (DR if q < 2 else DG)[:, ((2 * q + par) % 4) * P:((2 * q + par) % 4 + 1) * P],
                          X[:, (2 * q + par) * 64:(2 * q + par + 1) * 64], q == 0, False) for q in range(4)],
                        fr, vs())
                    ub.append((i, b))
                tm_ = mdone[0]
                for e_ in range(2):
                    rs = slice(64 * e_, 64 * e_ + 64)
                    M = Ms[mcur[0] % 4]
                    Mn = Ms[(mcur[0] + 1) % 4]
                    mcur[0] += 1
                    m0s.append(M)
                    im, bm, fr = B.take()
                    mms([(bm[hb(h), (h // 2) * 64:(h // 2) * 64 + 64], K3[rs, h * 64:(h + 1) * 64],
                          VV[rs, h * 64:(h + 1) * 64], h < 2, False) for h in range(4)], fr, tk)
                    bks = []
                    for par in range(2):
                        i, b = ub[par]
                        t1 = mms([(b[rs, q * 64:(q + 1) * 64], WT[hb(par), q * P + 64 * e_:q * P + 64 * e_ + 64],
                                   M[hb(par), q * 64:(q + 1) * 64], False, True) for q in range(4)], tm_)
                        t2 = copy(UN[rs, par * 256:(par + 1) * 256], b[rs, 0:256], t1, scale=-1.0,
                                  eng="SV"[par])
                        bks.append(t2)
                    tt(h64(Mn, 4), h64(M, 4), bc(DC[:, e_:8:2].unsqueeze(2), [P, 4, 64]), ALU.mult)
                    t1 = mms([(bm[hb(h), (h // 2) * 64:(h // 2) * 64 + 64], K2[rs, h * 64:(h + 1) * 64],
                               UN[rs, (h % 2) * 256 + (h // 2) * 64:(h % 2) * 256 + (h // 2) * 64 + 64], False, True)
                              for h in range(8)], bks)
                    tm_ = tt(Mn, Mn, bm[:, 0:256], ALU.add, t1)
                    B.release(im, tm_)
                    mdone[0] = tm_
                    if e_:
                        for (i, b), t2 in zip(ub, bks):
                            B.release(i, t2)
                    yield
                Y = get()
                for par in range(2):
                    i, b, fr = B.take()
                    lst = []
                    for q in range(4):
                        h = 2 * q + par
                        o = b[:, q * 64:(q + 1) * 64]
                        un = UN[:, par * 256 + q * 64:par * 256 + q * 64 + 64]
                        if h < 4:
                            lst.append((o, RW[h][:, 0:128], un, True, False))
                            lst.append((o, RW[h][:, 256:384], VV[:, h * 64:(h + 1) * 64], False, False))
                        else:
                            lst.append((o, PN[par][:, (q - 2) * 256:(q - 2) * 256 + 128], un, True, False))
                        for e_ in range(2):
                            if h < 4:
                                qs = f1v[hb(h), q, 0, 64 * e_:64 * e_ + 64]
                            else:
                                qs = F3[hb(h), 256 + (q - 2) * P + 64 * e_:256 + (q - 2) * P + 64 * e_ + 64]
                            lst.append((b[64 * e_:64 * e_ + 64, q * 64:(q + 1) * 64], qs,
                                        m0s[e_][hb(h), q * 64:(q + 1) * 64], False, e_ == 1))
                    t1 = mms(lst, fr)
                    yv = Y.rearrange("p (q r n) -> p q r n", q=4, r=2)[:, :, par, :]
                    t2 = copy(yv, b[:, 0:256].rearrange("p (q n) -> p q n", q=4), t1, eng="V")
                    B.release(i, t2)
                put(*RW, *PN, DR, DG, X, WT, K2, F1, F3)
                yield False
                tmp, tmp2 = get(), get()
                yr, yg = Y[:, 0:256], Y[:, 256:512]
                s1 = sml()
                s2 = sml()
                t = red(s1[:, 0:4], h64(yr, 4), ALU.add, t2)
                ts(s1[:, 0:4], s1[:, 0:4], 1.0 / 64, None, ALU.mult, None)
                tt(h64(yr, 4), h64(yr, 4), bc(s1[:, 0:4].unsqueeze(2), [P, 4, 64]), ALU.subtract)
                t = tt(tmp, Y, Y, ALU.mult)
                red(s2[:, 0:8], h64(tmp, 8), ALU.add)
                ts(s2[:, 0:4], s2[:, 0:4], 1.0 / 64, 64e-5, ALU.mult, ALU.add)
                t = ts(s2[:, 4:8], s2[:, 4:8], 1.0 / 64, 1e-6, ALU.mult, ALU.add)
                yield
                t = act(s2[:, 0:8], s2[:, 0:8], ACT.Sqrt, t)
                t = rec(s2[:, 0:8], s2[:, 0:8], t)
                tt(h64(Y, 8), h64(Y, 8), bc(s2[:, 0:8].unsqueeze(2), [P, 8, 64]), ALU.mult, t)
                yield
                tt(yr, yr, rows["gn_w"], ALU.mult)
                tt(yr, yr, rows["gn_b"], ALU.add)
                tt(h64(tmp2[:, 0:256], 4), h64(v_, 4), bc(bon[:, 0:4].unsqueeze(2), [P, 4, 64]), ALU.mult)
                tt(yr, yr, tmp2[:, 0:256], ALU.add)
                tt(mx[:, j, 512:768], yr, GG, ALU.mult)
                tt(h64(yg, 4), h64(yg, 4), bc(rows["on"].unsqueeze(1), [P, 4, 64]), ALU.mult)
                tt(mx[:, j, 768:1024], yg, gz[:, j, 0:256], ALU.mult)
                put(Y, tmp, tmp2, VV, K3)

            def until(g, mark):
                return next(g, "end") is mark

            tiles = [rec_tile(j) for j in range(4)]
            while not until(tiles[0], True):
                pass
            for j in range(4):
                solved, made, step = False, j == 3, 0
                while not (solved and made):
                    if j:
                        next(tiles[j - 1], None)
                    if not solved:
                        solved = until(tiles[j], False)
                    step += 1
                    if not made and (solved or step > 2):
                        made = until(tiles[j + 1], True)
            for _ in tiles[3]:
                pass
            assert len(stock) == 34 + len(extra)
            for n in range(NRAW):
                RAW.free[n] = marks()
            for n in range(2):
                PR.free[n] = marks()

            barrier()
            debug(f"my{l}", mix[:, :])
            t = to_T(mx, None, None, None, None, None)
            for half in range(2):
                t2 = proj_T(("w_out_2", l), 0, 8, half * 512, 512, xTh, xTl, t,
                            lambda j, b, t, half=half: tt(xtm[:, j, half * 512:(half + 1) * 512],
                                                          xtm[:, j, half * 512:(half + 1) * 512], b[:, :],
                                                          ALU.add, t))
            debug(f"xb{l}", x_tm[:, :])
            barrier()
            t = rms_norm_T(colat[("ffn", l, 1)], marks())
            barrier()
            t = ffn(("ffn_w_gate_2", 2 * l + 1), ("ffn_w_up_2", 2 * l + 1), ("ffn_w_down_2", 2 * l + 1), t, fin2)

        for i in range(NT):
            t = SP.dma("out", dcount, lambda e, i=i: e.dma_start(out[0, i * P:(i + 1) * P, :], xtm[:, i, :]), marks())
        SP.ops.append((None, [t], None))
        if "dbg" in dcount:
            SP.ops.append((None, [("dbg", dcount["dbg"])], None))

        for q in ENG + (SP,):
            for fn, w, inc in q.ops:
                for s, v in w:
                    sem(s)
                if inc:
                    sem(inc[0])
        block = ctx.enter_context(nc.Block())

        def play(q):
            def body(e):
                seen = {}
                for fn, w, inc in q.ops:
                    need = {}
                    for s, v in w:
                        if v > seen.get(s, 0):
                            need[s] = max(need.get(s, 0), v)
                    for s, v in need.items():
                        e.wait_ge(sems[s], v)
                        seen[s] = v
                    if fn is not None:
                        ins = fn(e)
                        if inc:
                            ins.then_inc(sems[inc[0]], inc[1])
            return body

        block.tensor(play(PE))
        block.vector(play(V))
        block.scalar(play(S))
        block.gpsimd(play(G))
        block.sync(play(SP))


_INS = ['x', 'w_in', 'fox_b_f', 'mla_g_q', 'mla_g_kv', 'mla_w_uq', 'mla_w_ukv', 'swa_sinks', 'mix_g', 'w_o',
        'ln1_g', 'ln1_b', 'w_gate', 'w_up', 'w_down', 'ln2_g', 'ln2_b', 'ffn_norm_2', 'ffn_w_gate_2',
        'ffn_w_up_2', 'ffn_w_down_2', 'mix_norm_2', 'w_in_2', 'w_out_2', 'att_q_norm_2', 'att_k_norm_2',
        'rwkv_mu_2', 'rwkv_w0_2', 'rwkv_w_up_2', 'rwkv_a0_2', 'rwkv_a_up_2', 'rwkv_g_up_2', 'rwkv_k_k_2',
        'rwkv_k_a_2', 'rwkv_r_k_2', 'rwkv_gn_w_2', 'rwkv_gn_b_2', 'rwkv_v0_2', 'rwkv_v_down_2',
        'rwkv_v_up_2', 'gdn_conv_2', 'gdn_a_log_2', 'gdn_dt_bias_2', 'gdn_o_norm_2']
_DBG = []


def kernel(**inputs):
    import numpy as _np
    import concourse.bacc as _bacc
    from concourse import mybir as _mybir
    from concourse.bass_utils import run_bass_kernel_spmd as _run

    nc = _bacc.Bacc("TRN2", target_bir_lowering=False, num_devices=1)
    c1, c2 = make_consts()
    arrays, aps = {}, {}
    for name in _INS + ["c_one", "c_two"]:
        a = c1 if name == "c_one" else c2 if name == "c_two" else _np.ascontiguousarray(inputs[name])
        arrays[f"in_{name}_dram"] = a
        aps[name] = nc.dram_tensor(f"in_{name}_dram", a.shape, _mybir.dt.from_np(a.dtype), kind="ExternalInput").ap()
    out = nc.dram_tensor("out_0_dram", (1, T, D), F32, kind="ExternalOutput").ap()
    dbg = {n: nc.dram_tensor(f"dbg_{n}", (P, w), F32, kind="ExternalOutput").ap() for n, w in _DBG}
    build_program(nc, aps, out, dbg)
    r = _run(nc, [arrays], core_ids=[0])
    got = r.results[0]["out_0_dram"]
    if _DBG:
        return (got,) + tuple(r.results[0][f"dbg_{n}"] for n, _ in _DBG)
    return got
```
